# Optimizing a Trainium2 kernel written in Bass

```python
import math
import jax, jax.numpy as jnp
from jax import lax
import numpy as np

D_MODEL = 1024
BATCH = 1
SEQ = 128
DEPTH = 2
DEC_BATCH = 1
DEC_SEQ = 256
PAST_LEN = 128

GRID_W = 64
RW_HEADS = 4
RW_N = 64
RW_W = RW_HEADS * RW_N
RW_LORA_W = 64
RW_LORA_A = 64
RW_LORA_G = 128
RW_DIR = RW_LORA_W + RW_LORA_A + RW_LORA_G
RW_IN = 3 * RW_W + 2 * RW_DIR
RW_GN_EPS = 64e-5
GLA_HEADS = 4
GLA_DK = 32
GLA_DV = 64
GLA_QK = GLA_HEADS * GLA_DK
GLA_W = GLA_HEADS * GLA_DV
GLA_LORA = 16
GLA_DIR = GLA_LORA + GLA_W
GLA_IN = 2 * GLA_QK + GLA_W + 2 * GLA_DIR
GLA_TAU = 16.0
GLA_CHUNK = 64
DIFF_HEADS = 4
DIFF_D = 64
DIFF_W = DIFF_HEADS * 2 * DIFF_D
DIFF_IN = 3 * DIFF_W
Q_BLOCK = 128
ROPE_BASE = 10000.0
MIX_W = RW_W + GLA_W + DIFF_W
IN_W = RW_IN + GLA_IN + DIFF_IN
D_FF = 2816
N_MOD = 9
LN_EPS = 1e-5
NORM_EPS = 1e-6
ALPHA = (2 * DEPTH) ** 0.25
BETA = (8 * DEPTH) ** -0.25
F32 = jnp.float32

kernel_name = 'hybrid_rwkv7_gla_diffattn_dit_step'

def layer_norm(x, g, b):
    xf = x.astype(F32)
    mu = jnp.mean(xf, -1, keepdims=True)
    var = jnp.mean(jnp.square(xf - mu), -1, keepdims=True)
    return ((xf - mu) * lax.rsqrt(var + LN_EPS) * g + b).astype(x.dtype)

def head_layer_norm(y, eps):
    mu = jnp.mean(y, -1, keepdims=True)
    var = jnp.mean(jnp.square(y - mu), -1, keepdims=True)
    return (y - mu) * lax.rsqrt(var + eps)

def head_rms_norm(y, eps):
    yf = y.astype(F32)
    return yf * lax.rsqrt(jnp.mean(jnp.square(yf), -1, keepdims=True) + eps)

def swiglu(h, wg, wu, wd):
    return (jax.nn.silu(h @ wg) * (h @ wu)) @ wd

def centred_shift(p, mu):
    prev = jnp.pad(p[:, :-1], ((0, 0), (1, 0), (0, 0)))
    nxt = jnp.pad(p[:, 1:], ((0, 0), (0, 1), (0, 0)))
    return p + mu[0] * (prev - p) + mu[1] * (nxt - p)

def axial_rope(x):
    t = x.shape[1]
    rows = t // GRID_W
    row_pos = jnp.repeat(jnp.arange(rows, dtype=F32), GRID_W)
    col_pos = jnp.tile(jnp.arange(GRID_W, dtype=F32), rows)
    half = x.shape[-1] // 2
    nf = half // 2
    inv = ROPE_BASE ** (-jnp.arange(nf, dtype=F32) / nf)
    xf = x.astype(F32)

    def rot(part, pos):
        ang = pos[:, None] * inv
        cos = jnp.cos(ang)[None, :, None, None, :]
        sin = jnp.sin(ang)[None, :, None, None, :]
        x1, x2 = part[..., :nf], part[..., nf:]
        return jnp.concatenate([x1 * cos - x2 * sin, x1 * sin + x2 * cos], -1)

    out = jnp.concatenate([rot(xf[..., :half], row_pos), rot(xf[..., half:], col_pos)], -1)
    return out.astype(x.dtype)

def rwkv7_scan(r, w, k, v, kk, a, s0):
    def step(s, inp):
        r_t, w_t, k_t, v_t, kk_t, a_t = inp
        sa = jnp.einsum('bhvk,bhk->bhv', s, kk_t)
        s = (s * w_t[:, :, None, :] - sa[..., None] * (kk_t * a_t)[:, :, None, :]
             + v_t[..., None] * k_t[:, :, None, :])
        y = jnp.einsum('bhvk,bhk->bhv', s, r_t)
        return s, y

    xs = tuple(jnp.moveaxis(t, 1, 0) for t in (r, w, k, v, kk, a))
    s_fin, ys = lax.scan(step, s0, xs)
    return jnp.moveaxis(ys, 0, 1), s_fin

def gla_chunked(q, k, v, log_a, s0):
    bsz, t, h, _ = q.shape
    n = t // GLA_CHUNK

    def to_chunks(x):
        return jnp.transpose(x.reshape(bsz, n, GLA_CHUNK, h, x.shape[-1]), (1, 0, 3, 2, 4))

    mask = jnp.tril(jnp.ones((GLA_CHUNK, GLA_CHUNK), bool))[None, None, :, :, None]

    def step(s, inp):
        qc, kc, vc, lc = inp
        b = jnp.cumsum(lc, axis=2)
        b_last = b[:, :, -1:, :]
        o_inter = jnp.einsum('bhtd,bhde->bhte', qc * jnp.exp(b), s)
        diff = b[:, :, :, None, :] - b[:, :, None, :, :]
        dec = jnp.where(mask, jnp.exp(jnp.minimum(diff, 0.0)), 0.0)
        attn = jnp.einsum('bhtd,bhsd,bhtsd->bhts', qc, kc, dec)
        o = o_inter + jnp.einsum('bhts,bhse->bhte', attn, vc)
        s = (jnp.exp(b_last[:, :, 0, :])[..., None] * s
             + jnp.einsum('bhsd,bhse->bhde', kc * jnp.exp(b_last - b), vc))
        return s, o

    s_fin, o = lax.scan(step, s0, tuple(to_chunks(x) for x in (q, k, v, log_a)))
    o = jnp.transpose(o, (1, 0, 3, 2, 4)).reshape(bsz, t, h, v.shape[-1])
    return o, s_fin

def diff_attention(q, k, v, lam):
    bsz, tq, h, _, d = q.shape
    nb = tq // Q_BLOCK
    qb = jnp.moveaxis(q.reshape(bsz, nb, Q_BLOCK, h, 2, d), 1, 0)

    def one_block(qblk):
        s = jnp.einsum('bqhcd,bkhcd->bhcqk', qblk, k).astype(F32)
        p = jax.nn.softmax(s, axis=-1)
        att = p[:, :, 0] - lam * p[:, :, 1]
        return jnp.einsum('bhqk,bkhe->bqhe', att.astype(v.dtype), v)

    o = lax.map(one_block, qb)
    return jnp.moveaxis(o, 0, 1).reshape(bsz, tq, h, 2 * d)

def rwkv7_branch(p, s0, lp):
    p = centred_shift(p.astype(F32), lp['rw_mu'])
    bsz, t, _ = p.shape
    r, k, v, dir_f, dir_b = jnp.split(p, [RW_W, 2 * RW_W, 3 * RW_W, 3 * RW_W + RW_DIR], -1)

    def heads(x):
        return x.reshape(bsz, t, RW_HEADS, RW_N)

    kk = heads(k * lp['rw_k_k'])
    kk = kk / jnp.maximum(jnp.sqrt(jnp.sum(jnp.square(kk), -1, keepdims=True)), 1e-12)
    rh, vh = heads(r), heads(v)
    out = jnp.zeros((bsz, t, RW_W), F32)
    states = []
    for d, pd in enumerate((dir_f, dir_b)):
        wd, ad, gd = jnp.split(pd, [RW_LORA_W, RW_LORA_W + RW_LORA_A], -1)
        w_raw = lp['rw_w0'][d] + jnp.tanh(wd) @ lp['rw_w_up'][d]
        decay = jnp.exp(-jnp.exp(-jax.nn.softplus(-w_raw) - 0.5))
        a = jax.nn.sigmoid(lp['rw_a0'][d] + ad @ lp['rw_a_up'][d])
        g = jax.nn.sigmoid(gd) @ lp['rw_g_up'][d]
        kd = heads(k * (1.0 + (a - 1.0) * lp['rw_k_a']))
        seq = (rh, heads(decay), kd, vh, kk, heads(a))
        if d == 1:
            seq = tuple(jnp.flip(x, 1) for x in seq)
        y, s_fin = rwkv7_scan(*seq, s0[:, d].astype(F32))
        if d == 1:
            y = jnp.flip(y, 1)
        y = head_layer_norm(y, RW_GN_EPS).reshape(bsz, t, RW_W) * lp['rw_gn_g'][d] + lp['rw_gn_b'][d]
        bonus = (jnp.sum(rh * kd * lp['rw_r_k'][d], -1, keepdims=True) * vh).reshape(bsz, t, RW_W)
        out = out + (y + bonus) * g
        states.append(s_fin)
    return out, jnp.stack(states, 1)

def gla_branch(p, s0, lp):
    p = p.astype(F32)
    bsz, t, _ = p.shape
    q, k, v, dir_f, dir_b = jnp.split(
        p, [GLA_QK, 2 * GLA_QK, 2 * GLA_QK + GLA_W, 2 * GLA_QK + GLA_W + GLA_DIR], -1)
    q = q.reshape(bsz, t, GLA_HEADS, GLA_DK) * GLA_DK ** -0.5
    k = k.reshape(bsz, t, GLA_HEADS, GLA_DK)
    v = v.reshape(bsz, t, GLA_HEADS, GLA_DV)
    out = jnp.zeros((bsz, t, GLA_W), F32)
    states = []
    for d, pd in enumerate((dir_f, dir_b)):
        ad, gd = jnp.split(pd, [GLA_LORA], -1)
        log_a = jax.nn.log_sigmoid(ad @ lp['gla_a_up'][d] + lp['gla_a_b'][d]) / GLA_TAU
        seq = (q, k, v, log_a.reshape(bsz, t, GLA_HEADS, GLA_DK))
        if d == 1:
            seq = tuple(jnp.flip(x, 1) for x in seq)
        o, s_fin = gla_chunked(*seq, s0[:, d].astype(F32))
        if d == 1:
            o = jnp.flip(o, 1)
        o = head_rms_norm(o, NORM_EPS) * lp['gla_gn_g']
        out = out + o.reshape(bsz, t, GLA_W) * jax.nn.silu(gd)
        states.append(s_fin)
    return out, jnp.stack(states, 1)

def diff_branch(p, ctx_kv, lp, lam_init):
    bsz, t, _ = p.shape
    q, k, v = jnp.split(p, 3, -1)
    q = q.reshape(bsz, t, DIFF_HEADS, 2, DIFF_D)
    k = k.reshape(bsz, t, DIFF_HEADS, 2, DIFF_D)
    v = v.reshape(bsz, t, DIFF_HEADS, 2 * DIFF_D)
    lam_p = lp['diff_lam'].astype(F32)
    lam = jnp.exp(jnp.sum(lam_p[0] * lam_p[1])) - jnp.exp(jnp.sum(lam_p[2] * lam_p[3])) + lam_init
    if ctx_kv is None:
        keys, vals = k, v
        new_k, new_v = k.reshape(bsz, t, DIFF_HEADS, 2 * DIFF_D), v
    else:
        k_ctx, v_ctx = ctx_kv
        q = axial_rope(q)
        keys = jnp.concatenate(
            [axial_rope(k), k_ctx.reshape(bsz, -1, DIFF_HEADS, 2, DIFF_D).astype(k.dtype)], 1)
        vals = jnp.concatenate([v, v_ctx.astype(v.dtype)], 1)
        new_k, new_v = None, None
    o = diff_attention(q * DIFF_D ** -0.5, keys, vals, lam)
    o = head_rms_norm(o, NORM_EPS) * lp['diff_gn_g'] * (1.0 - lam_init)
    return o.reshape(bsz, t, DIFF_W), new_k, new_v

def token_mixer(h, lp, lam_init, cache):
    bsz = h.shape[0]
    p = h @ lp['w_in']
    p_rw, p_gla, p_diff = jnp.split(p, [RW_IN, RW_IN + GLA_IN], -1)
    if cache is None:
        s_rw0 = jnp.zeros((bsz, 2, RW_HEADS, RW_N, RW_N), F32)
        s_gla0 = jnp.zeros((bsz, 2, GLA_HEADS, GLA_DK, GLA_DV), F32)
        ctx_kv = None
    else:
        s_rw0, s_gla0, k_ctx, v_ctx = cache
        ctx_kv = (k_ctx, v_ctx)
    o_rw, s_rw = rwkv7_branch(p_rw, s_rw0, lp)
    o_gla, s_gla = gla_branch(p_gla, s_gla0, lp)
    o_diff, new_k, new_v = diff_branch(p_diff, ctx_kv, lp, lam_init)
    mixed = jnp.concatenate([o_rw, o_gla, o_diff.astype(F32)], -1).astype(h.dtype)
    out = mixed @ lp['w_out']
    if cache is None:
        return out, (s_rw.astype(h.dtype), s_gla.astype(h.dtype), new_k, new_v)
    return out, None

def trunk_layer(x, cond, lp, lam_init, cache):
    sh1, sc1, g1, sh2, sc2, g2, sh3, sc3, g3 = jnp.split(cond.astype(x.dtype), N_MOD, -1)
    h = x * (1.0 + sc1) + sh1
    f = swiglu(h, lp['ffn_w_gate'][0], lp['ffn_w_up'][0], lp['ffn_w_down'][0])
    x = layer_norm(ALPHA * x + 0.5 * g1 * f, lp['ln_g'][0], lp['ln_b'][0])
    h = x * (1.0 + sc2) + sh2
    m, new_cache = token_mixer(h, lp, lam_init, cache)
    x = layer_norm(ALPHA * x + g2 * m, lp['ln_g'][1], lp['ln_b'][1])
    h = x * (1.0 + sc3) + sh3
    f = swiglu(h, lp['ffn_w_gate'][1], lp['ffn_w_up'][1], lp['ffn_w_down'][1])
    x = layer_norm(ALPHA * x + 0.5 * g3 * f, lp['ln_g'][2], lp['ln_b'][2])
    return x, new_cache

def setup_inputs(seed: int = 0) -> dict:
    key = jax.random.key(seed)
    ks = iter(jax.random.split(key, 40))

    def nrm(shape, scale):
        return scale * jax.random.normal(next(ks), shape, F32)

    def unif(shape, lo, hi):
        return jax.random.uniform(next(ks), shape, F32, lo, hi)

    L = DEPTH
    return {
        'x_prompt': nrm((BATCH, SEQ, D_MODEL), 1.0),
        'x_sample': nrm((DEC_BATCH, DEC_SEQ, D_MODEL), 1.0),
        'state_rwkv': nrm((DEC_BATCH, L, 2, RW_HEADS, RW_N, RW_N), 1.0),
        'state_gla': nrm((DEC_BATCH, L, 2, GLA_HEADS, GLA_DK, GLA_DV), 1.0),
        'cache_diff_k': nrm((DEC_BATCH, L, PAST_LEN, DIFF_HEADS, 2 * DIFF_D), 1.0),
        'cache_diff_v': nrm((DEC_BATCH, L, PAST_LEN, DIFF_HEADS, 2 * DIFF_D), 1.0),
        'c': nrm((DEC_BATCH, D_MODEL), 1.0),
        'c_ctx': nrm((D_MODEL,), 1.0),
        'w_ada': nrm((L, D_MODEL, N_MOD * D_MODEL), 0.5 * D_MODEL ** -0.5),
        'b_ada': nrm((L, N_MOD * D_MODEL), 0.01),
        'ln_g': 1.0 + nrm((L, 3, D_MODEL), 0.02),
        'ln_b': nrm((L, 3, D_MODEL), 0.02),
        'ffn_w_gate': nrm((L, 2, D_MODEL, D_FF), D_MODEL ** -0.5),
        'ffn_w_up': nrm((L, 2, D_MODEL, D_FF), D_MODEL ** -0.5),
        'ffn_w_down': nrm((L, 2, D_FF, D_MODEL), BETA * D_FF ** -0.5),
        'w_in': nrm((L, D_MODEL, IN_W), D_MODEL ** -0.5),
        'w_out': nrm((L, MIX_W, D_MODEL), BETA * MIX_W ** -0.5),
        'rw_mu': unif((L, 2, RW_IN), 0.0, 0.5),
        'rw_k_k': 0.85 + nrm((L, RW_W), 0.1),
        'rw_k_a': 1.0 + nrm((L, RW_W), 0.1),
        'rw_w0': unif((L, 2, RW_W), -6.0, -1.0),
        'rw_w_up': nrm((L, 2, RW_LORA_W, RW_W), 0.5 * RW_LORA_W ** -0.5),
        'rw_a0': nrm((L, 2, RW_W), 0.1),
        'rw_a_up': nrm((L, 2, RW_LORA_A, RW_W), 0.5 * RW_LORA_A ** -0.5),
        'rw_g_up': nrm((L, 2, RW_LORA_G, RW_W), RW_LORA_G ** -0.5),
        'rw_r_k': nrm((L, 2, RW_HEADS, RW_N), 0.1),
        'rw_gn_g': 1.0 + nrm((L, 2, RW_W), 0.02),
        'rw_gn_b': nrm((L, 2, RW_W), 0.02),
        'gla_a_up': nrm((L, 2, GLA_LORA, GLA_QK), GLA_LORA ** -0.5),
        'gla_a_b': 2.0 + nrm((L, 2, GLA_QK), 0.5),
        'gla_gn_g': 1.0 + nrm((L, GLA_DV), 0.02),
        'diff_lam': nrm((L, 4, DIFF_D), 0.1),
        'diff_gn_g': 1.0 + nrm((L, 2 * DIFF_D), 0.02),
    }

def reference(x_prompt, x_sample, state_rwkv, state_gla, cache_diff_k, cache_diff_v, c, c_ctx,
              w_ada, b_ada, ln_g, ln_b, ffn_w_gate, ffn_w_up, ffn_w_down, w_in, w_out,
              rw_mu, rw_k_k, rw_k_a, rw_w0, rw_w_up, rw_a0, rw_a_up, rw_g_up, rw_r_k,
              rw_gn_g, rw_gn_b, gla_a_up, gla_a_b, gla_gn_g, diff_lam, diff_gn_g):
    y_p = x_prompt
    y_s = x_sample
    new_rw, new_gla, new_k, new_v = [], [], [], []
    for l in range(DEPTH):
        lp = {
            'w_in': w_in[l], 'w_out': w_out[l], 'ln_g': ln_g[l], 'ln_b': ln_b[l],
            'ffn_w_gate': ffn_w_gate[l], 'ffn_w_up': ffn_w_up[l], 'ffn_w_down': ffn_w_down[l],
            'rw_mu': rw_mu[l], 'rw_k_k': rw_k_k[l], 'rw_k_a': rw_k_a[l], 'rw_w0': rw_w0[l],
            'rw_w_up': rw_w_up[l], 'rw_a0': rw_a0[l], 'rw_a_up': rw_a_up[l], 'rw_g_up': rw_g_up[l],
            'rw_r_k': rw_r_k[l], 'rw_gn_g': rw_gn_g[l], 'rw_gn_b': rw_gn_b[l],
            'gla_a_up': gla_a_up[l], 'gla_a_b': gla_a_b[l], 'gla_gn_g': gla_gn_g[l],
            'diff_lam': diff_lam[l], 'diff_gn_g': diff_gn_g[l],
        }
        lam_init = 0.8 - 0.6 * math.exp(-0.3 * l)
        cond_ctx = (jax.nn.silu(c_ctx)[None, :] @ w_ada[l] + b_ada[l])[:, None, :]
        y_p, (s_rw, s_gla, k_c, v_c) = trunk_layer(y_p, cond_ctx, lp, lam_init, None)
        new_rw.append(s_rw)
        new_gla.append(s_gla)
        new_k.append(k_c)
        new_v.append(v_c)
        cond_lat = (jax.nn.silu(c) @ w_ada[l] + b_ada[l])[:, None, :]
        cache_l = (state_rwkv[:, l], state_gla[:, l], cache_diff_k[:, l], cache_diff_v[:, l])
        y_s, _ = trunk_layer(y_s, cond_lat, lp, lam_init, cache_l)
    return (y_p, y_s, jnp.stack(new_rw, 1), jnp.stack(new_gla, 1), jnp.stack(new_k, 1), jnp.stack(new_v, 1))


_drawn_inputs = setup_inputs


def setup_inputs(seed=0):
    import zlib

    import numpy as np

    out = dict(_drawn_inputs(seed))
    spreads = {}
    factors = {'state_rwkv': 3.511,
     'state_gla': 7.136,
     'rw_r_k': 5.497,
     'rw_gn_g': 57.098,
     'rw_gn_b': 40.286,
     'gla_gn_g': 42.564,
     'diff_lam': 3.584,
     'diff_gn_g': 29.306}
    for name, (base, spread) in spreads.items():
        noise = np.random.default_rng([zlib.crc32(name.encode()), seed]).standard_normal(out[name].shape)
        drawn = base * np.exp(spread * noise) if base else spread * noise
        out[name] = __import__('jax').numpy.asarray(drawn.astype(out[name].dtype))
    for name, factor in factors.items():
        out[name] = (out[name] * factor).astype(out[name].dtype)
    return out
```

```python
import math
from contextlib import ExitStack

import numpy as np

import concourse.bass as bass
from concourse import mybir

F32 = mybir.dt.float32
I32 = mybir.dt.int32
FR = mybir.dt.float32r
ALU = mybir.AluOpType
ACT = mybir.ActivationFunctionType
AX = mybir.AxisListType.X

P = 128
DM = 1024
KT = DM // P
DEPTH = 2
GROUPS = 3
TOK = GROUPS * P
LAT = TOK - P
GRID_W = 64
PAST = 128
NMIX = 3
D_FF = 2816
FT = D_FF // P
RW_W = 256
RW_N = 64
RW_IN = 1280
GLA_QK = 128
GLA_W = 256
GLA_DK = 32
GLA_LORA = 16
GLA_TAU = 16.0
GLA_IN = 1056
DIFF_D = 64
DIFF_W = 512
HEADS = 4
ALPHA = (2 * DEPTH) ** 0.25
LN_EPS = 1e-5
NORM_EPS = 1e-6
RW_GN_EPS = 64e-5
DECAY = -math.exp(-0.5)
CHUNK = 64
WPAD = TOK + 3
WIN = slice(1, WPAD - 1)
GLA_HALVES = (64, 32, 16)
GLA_BASE = 16
GLA_CLAMP = 80.0
ORDER = ((0, 1, 2), (0, 2, 1))

CHW = 2048
RING = 6
N_ADA = 12
N_FFN = 3 * FT // 2
UNIT = CHW // 2
FFN_UNITS = 3 * FT
HI_FFN = 6
HI_PROJ = 2
HI_OUT = 2
N_FEAT = 10
N_TOKM = 5
N_OUT = 4
OUT_ORDER = (2, 3, 4, 5, 6, 7, 0, 1)
N_CHUNKS = NMIX * N_ADA + 2 * N_FFN + N_FEAT + N_TOKM + N_OUT


PSH = (2, 3, 4, 5, 6, 7, 8, 0, 9, 1)


def pcol(g):
    return 1 + P * g + (g > 0)


CONST = {}
_at = 0
for _name, _width in (("ident", 128), ("ones_blk", 128), ("rope_rot", 128), ("rope_cos", LAT), ("rope_sin", LAT),
                      ("rw_mask", 2 * 256), ("halves", 2 * 7 * 128), ("gla_base", 2 * 128), ("rw_keep", 2 * WPAD),
                      ("gla_keep", 2 * TOK), ("gla_blk", 256), ("sel", 256)):
    CONST[_name] = slice(_at, _at + _width)
    _at += _width
N_CONST = _at

PAR = {}
_at = 0
for _name, _width in (("rw_up", 2 * 256), ("g_up", 2 * 256), ("gla_up", 128), ("b_mod", NMIX * 16), ("mu", 20),
                      ("k_k", 2), ("k_a", 2), ("w0", 4), ("a0", 4), ("gla_b", 2), ("r_k", 16), ("lam_init", 2)):
    PAR[_name] = slice(_at, _at + _width)
    _at += _width
N_PAR = _at

ROW = {}
_at = 0
for _name, _width in (("gn_g", 512), ("gn_b", 512), ("gla_g", 64), ("diff_g", 128), ("lam", 256)):
    ROW[_name] = slice(_at, _at + _width)
    _at += _width
N_ROW = _at


def shape_constants():
    out = np.zeros((P, N_CONST), np.float32)
    i = np.arange(P)
    s, t = i[:, None], i[None, :]
    out[:, CONST["ident"]] = s == t
    out[:, CONST["ones_blk"]] = s // 64 == t // 64
    rot = np.zeros((P, P), np.float32)
    for f in range(P):
        if f % 32 < 16:
            rot[f, f + 16] = -1.0
        else:
            rot[f, f - 16] = 1.0
    out[:, CONST["rope_rot"]] = rot.T
    tok = np.arange(LAT)
    inv = 10000.0 ** (-np.arange(16, dtype=np.float32) / np.float32(16))
    pos = np.where((i % 64 < 32)[:, None], (tok // GRID_W)[None, :], (tok % GRID_W)[None, :]).astype(np.float32)
    ang = pos * inv[i % 16][:, None].astype(np.float32)
    out[:, CONST["rope_cos"]] = np.cos(ang)
    out[:, CONST["rope_sin"]] = np.sin(ang)
    same = s // CHUNK == t // CHUNK
    masks = out[:, CONST["rw_mask"]].reshape(P, 2, 2, P)
    for d, (strict, incl) in enumerate(((s < t, s <= t), (s > t, s >= t))):
        masks[:, d, 0] = same & strict
        masks[:, d, 1] = same & incl
    halves = out[:, CONST["halves"]].reshape(P, 2, 7, P)
    for n in range(7):
        h = 1 << n
        one = s // (2 * h) == t // (2 * h)
        halves[:, 0, n] = one & (s % (2 * h) >= h) & (t % (2 * h) < h)
        halves[:, 1, n] = one & (s % (2 * h) < h) & (t % (2 * h) >= h)
    base = out[:, CONST["gla_base"]].reshape(P, 2, P)
    one = s // GLA_BASE == t // GLA_BASE
    base[:, 0] = one & (s <= t)
    base[:, 1] = one & (s >= t)
    keep = out[:, CONST["rw_keep"]].reshape(P, 2, WPAD)
    keep[:] = 1.0
    gkeep = out[:, CONST["gla_keep"]].reshape(P, 2, TOK)
    gkeep[:] = 1.0
    for g in range(GROUPS):
        gkeep[:, 0, P * g] = 0.0
        gkeep[:, 1, P * g + P - 1] = 0.0
        for c in range(P // CHUNK):
            keep[:, 0, pcol(g) + CHUNK * c] = 0.0
            keep[:, 1, pcol(g) + CHUNK * c + CHUNK - 1] = 0.0
    blk = out[:, CONST["gla_blk"]].reshape(P, HEADS, 64)
    for h in range(HEADS):
        blk[GLA_DK * h:GLA_DK * h + GLA_DK, h] = 1.0
    sel = out[:, CONST["sel"]].reshape(P, 2, P)
    sel[0, 0] = 1.0
    sel[1, 1] = 1.0
    return out


class Line:

    def __init__(self, eng, sem):
        self.eng, self.sem, self.n = eng, sem, 0

    def step(self, ins):
        ins.then_inc(self.sem, 1)
        self.n += 1

    def settle(self):
        self.eng.wait_ge(self.sem, self.n)

    def link(self, ins):
        self.step(ins)
        self.settle()


class Carve:

    def __init__(self, row, rounded_row):
        self.row, self.rounded_row, self.at, self.top = row, rounded_row, 0, 0

    def rounded(self, n):
        return self(n, self.rounded_row)

    def __call__(self, n, row=None):
        got = (self.row if row is None else row)[:, self.at:self.at + n]
        self.at += n
        self.top = max(self.top, self.at)
        assert self.top <= self.row.shape[1], self.top
        return got


def trunk_kernel(nc, x_in, c_in, consts, weights, w_ad, par_in, ln_in, row_in, bgate_in, rw_state_in, gla_state_in,
                 kc_in, vc_in, y_out, rw_out, gla_out, k_out, v_out, dumps=None):
    with ExitStack() as ctx:
        def sb(name, shape):
            return ctx.enter_context(nc.sbuf_tensor(name, shape, F32))

        every = []

        def sem(name, lasting=False):
            s = ctx.enter_context(nc.semaphore(name))
            if not lasting:
                every.append(s)
            return s

        ps = [ctx.enter_context(nc.psum_tensor(f"bank{i}", [P, 512], F32)) for i in range(8)]

        def with_rounded(name, shape):
            plain = sb(name, shape)
            end = nc.sbuf_base
            size = 4 * math.prod(shape[1:])
            return plain, nc.alloc_sbuf_tensor_at(name + "_r", shape, FR, offset=end - size)

        ring, ring_r = with_rounded("ring", [P, RING, CHW])
        x = sb("x", [P, GROUPS, DM])
        const = sb("const", [P, N_CONST])
        par = sb("par", [P, N_PAR])
        wad = sb("wad", [P, KT, 64])
        rows = sb("rows", [P, N_ROW])
        silu_c = sb("silu_c", [P, KT, 2])
        cond = sb("cond", [P, 16, 2])
        gate_row = sb("gate_row", [2, DM])
        gate = sb("gate", [P, 2, DM])
        lnrow, lnrow_r = with_rounded("lnrow", [P, 2, DM])
        ln_stat = sb("ln_stat", [P, GROUPS, 12])
        ln_mv = sb("ln_mv", [P, GROUPS, 2])
        ln_r = sb("ln_r", [P, GROUPS, 3])
        small = sb("small", [P, 192])
        arena, arena_r = with_rounded("arena", [P, 23660])

        def con(name):
            return const[:, CONST[name]]

        ident = con("ident")
        halves = con("halves").rearrange("p (d n t) -> p d n t", d=2, n=7)
        rw_mask = con("rw_mask").rearrange("p (d m) -> p d m", d=2)
        rw_keep = con("rw_keep").rearrange("p (d m) -> p d m", d=2)
        gla_keep = con("gla_keep").rearrange("p (d m) -> p d m", d=2)
        gla_base = con("gla_base").rearrange("p (d m) -> p d m", d=2)
        sel = con("sel").rearrange("p (c m) -> p c m", c=2)

        def prm(name):
            return par[:, PAR[name]]

        def row(name):
            return rows[:, ROW[name]]

        rw_up = prm("rw_up").rearrange("p (d m) -> p d m", d=2)
        g_up = prm("g_up").rearrange("p (d m) -> p d m", d=2)
        b_mod = prm("b_mod").rearrange("p (j m) -> p j m", j=NMIX)
        mu = prm("mu").rearrange("p (m i) -> p m i", m=2)
        w0 = prm("w0").rearrange("p (d i) -> p d i", d=2)
        a0 = prm("a0").rearrange("p (d i) -> p d i", d=2)
        r_k = prm("r_k").rearrange("p (d i h) -> p d i h", d=2, i=2)

        put = Carve(arena, arena_r)
        h_hi = put.rounded(KT * TOK).rearrange("p (k t) -> p k t", k=KT)
        ffn_mark = put.at
        h_lo = put.rounded(KT * TOK).rearrange("p (k t) -> p k t", k=KT)
        h_mark = put.at
        h_full = put(KT * TOK).rearrange("p (k t) -> p k t", k=KT)
        put.at = h_mark
        act = put(2 * TOK).rearrange("p (b t) -> p b t", b=2)
        act_hi = put.rounded(2 * TOK).rearrange("p (b t) -> p b t", b=2)
        act_lo = put.rounded(2 * TOK).rearrange("p (b t) -> p b t", b=2)
        sgt = put(2 * TOK).rearrange("p (b t) -> p b t", b=2)
        w_hi = put.rounded(HI_FFN * UNIT).rearrange("p (s n) -> p s n", s=HI_FFN)
        put.at = ffn_mark
        mod_row = put(2 * DM)
        put.at = h_mark
        res_tmp = put(GROUPS * DM).rearrange("p (g n) -> p g n", g=GROUPS)
        put.at = ffn_mark
        psh = put(10 * WPAD).rearrange("p (i t) -> p i t", i=10)
        mixed = put(GROUPS * DM).rearrange("p (g n) -> p g n", g=GROUPS)
        put.at -= GROUPS * DM
        mix_h_lo = put.rounded(KT * TOK).rearrange("p (k t) -> p k t", k=KT)
        mixer_mark = put.at
        qg = put(TOK)
        kg = put(TOK)
        vg = put(GROUPS * GLA_W).rearrange("p (g n) -> p g n", g=GROUPS)
        gd = put(2 * GROUPS * GLA_W).rearrange("p (d g n) -> p d g n", d=2, g=GROUPS)
        adT = put(TOK)
        diff_mark = put.at
        praw = put(10 * WPAD).rearrange("p (i t) -> p i t", i=10)
        att_mark = put.at
        mix_h_full = put(KT * TOK).rearrange("p (k t) -> p k t", k=KT)
        put.at = att_mark
        qd = put(HEADS * TOK).rearrange("p (h t) -> p h t", h=HEADS)
        kd = put(HEADS * TOK).rearrange("p (h t) -> p h t", h=HEADS)
        vd = put(GROUPS * DIFF_W).rearrange("p (g n) -> p g n", g=GROUPS)
        kc = put(HEADS * PAST).rearrange("p (h t) -> p h t", h=HEADS)
        vc = put(DIFF_W)
        put.at = diff_mark
        e_sb = put(2 * 2 * TOK).rearrange("p (b c t) -> p b c t", b=2, c=2)
        att = put(2 * TOK).rearrange("p (b t) -> p b t", b=2)
        attT = put(2 * TOK).rearrange("p (b t) -> p b t", b=2)
        rope_tmp = put(LAT)
        assert put.at <= att_mark
        put.at = diff_mark
        gb = put(2 * TOK).rearrange("p (d t) -> p d t", d=2)
        gz = put(2 * TOK).rearrange("p (d t) -> p d t", d=2)
        ge = put(2 * TOK).rearrange("p (d t) -> p d t", d=2)
        put.at -= 4 * TOK
        g_sq = put(2 * GROUPS * GLA_W).rearrange("p (d g n) -> p d g n", d=2, g=GROUPS)
        g_dist = put(2 * TOK).rearrange("p (b t) -> p b t", b=2)
        g_klt = g_dist
        g_att = put(2 * HEADS * TOK).rearrange("p (d h t) -> p d h t", d=2, h=HEADS)
        g_q0 = put(2 * TOK).rearrange("p (d t) -> p d t", d=2)
        g_e0 = put(2 * TOK).rearrange("p (d t) -> p d t", d=2)
        g_kl = put(2 * TOK).rearrange("p (d t) -> p d t", d=2)
        g_o = put(2 * GROUPS * GLA_W).rearrange("p (d g n) -> p d g n", d=2, g=GROUPS)
        g_st = lnrow[:, 0, :].rearrange("p (d s n) -> p d s n", d=2, s=2)
        put.at = 0
        g_exp = put(2 * 2 * TOK).rearrange("p (b s t) -> p b s t", b=2, s=2)
        g_qk = put(2 * 2 * TOK).rearrange("p (b s t) -> p b s t", b=2, s=2)
        assert put.at <= ffn_mark
        put.at = mixer_mark
        kr = put(2 * 2 * 2 * WPAD).rearrange("p (d i s t) -> p d i s t", d=2, i=2, s=2)
        be = put(2 * 2 * WPAD).rearrange("p (d i t) -> p d i t", d=2, i=2)
        kh = put(2 * 2 * WPAD).rearrange("p (d i t) -> p d i t", d=2, i=2)
        vt = put(GROUPS * RW_W).rearrange("p (g n) -> p g n", g=GROUPS)
        pend = put(2 * 2 * 6).rearrange("p (d i c) -> p d i c", d=2, i=2)
        st = put(2 * 2 * 256).rearrange("p (d s n) -> p d s n", d=2, s=2)
        yall = put(2 * GROUPS * RW_W).rearrange("p (d g n) -> p d g n", d=2, g=GROUPS)
        unit_mark = put.at

        def wide():
            return put(2 * WPAD).rearrange("p (i t) -> p i t", i=2)

        pp, kk, kn, rkd = wide(), wide(), wide(), wide()
        put.at = 0
        sw, sa, cs = wide(), wide(), wide()
        assert put.at <= ffn_mark
        put.at = unit_mark
        m4 = put(2 * HEADS * 512).rearrange("p (d h n) -> p d h n", d=2, h=HEADS)
        put.at = 0
        xz = put(2 * 2 * 512).rearrange("p (s d h n) -> p s d h n", s=2, d=2, h=HEADS)
        off = put(2 * 512).rearrange("p (d h n) -> p d h n", d=2, h=HEADS)
        assert put.at <= ffn_mark
        put.at = ffn_mark + 2 * WPAD
        am = put(2 * 512).rearrange("p (d h n) -> p d h n", d=2, h=HEADS)
        wsb = put(2 * 512).rearrange("p (d h n) -> p d h n", d=2, h=HEADS)
        bk = put(2 * 512).rearrange("p (d n) -> p d n", d=2)
        assert put.at <= ffn_mark + 10 * WPAD
        spare = lnrow[:, :, :].rearrange("p s (a n) -> p (s a) n", n=512)
        rsb = spare[:, 0, :].rearrange("p (d n) -> p d n", d=2)
        usb = spare[:, 1, :].rearrange("p (d n) -> p d n", d=2)
        stmp = spare[:, 2, :].rearrange("p (d n) -> p d n", d=2)
        put.at = unit_mark
        gtmp = put(1536).rearrange("p (d g n) -> p d g n", d=2, g=GROUPS)
        gtmp2 = put(1536).rearrange("p (d g n) -> p d g n", d=2, g=GROUPS)
        out_w_hi = [put.rounded(UNIT)]
        put.at = mixer_mark + KT * TOK
        out_w_hi.append(put.rounded(UNIT))
        ggate = put(1536).rearrange("p (d g n) -> p d g n", d=2, g=GROUPS)
        put.at = 0
        mixT = put(KT * TOK).rearrange("p (k t) -> p k t", k=KT)
        mixT_hi = put.rounded(KT * TOK).rearrange("p (k t) -> p k t", k=KT)
        assert put.at <= ffn_mark + 10 * WPAD
        put.at = mixer_mark
        mixT_lo = put.rounded(KT * TOK).rearrange("p (k t) -> p k t", k=KT)
        proj_w_hi = lnrow_r[:, :, :]

        neg_lam = small[:, 0:1]
        lam4 = small[:, 1:5]
        c0 = small[:, 8:18]
        ka1 = small[:, 18:20]
        att_max = small[:, 20:24].rearrange("p (b c) -> p b c", b=2)
        att_r = small[:, 24:28].rearrange("p (b c) -> p b c", b=2)
        att_sum = small[:, 28:52].rearrange("p (u c) -> p u c", c=2)
        diff_ss = small[:, 52:64]
        gla_ss = small[:, 64:88]
        gn_mean = small[:, 88:112]
        gn_var = small[:, 112:136]
        bonus = small[:, 136:160]
        diff_gn = lnrow[:, 1, 0:P]
        eps_col = sb("eps_col", [P, 1])

        arrived = [sem(f"arrived{s}") for s in range(RING)]
        used = sem("used")
        x_loaded = sem("x_loaded", True)
        y_stored = sem("y_stored", True)
        par_loaded = sem("par_loaded", True)
        lnrow_loaded = sem("lnrow_loaded", True)
        gate_bias_loaded = sem("gate_bias_loaded", True)
        meeting = sem("meeting")
        mods_done = sem("mods_done")
        cond_ready = sem("cond_ready")
        mod_row_mm = sem("mod_row_mm")
        mod_row_ready = sem("mod_row_ready")
        gate_row_ready = sem("gate_row_ready")
        gate_wide = sem("gate_wide")
        gate_ready = sem("gate_ready")
        acc_done = sem("acc_done")
        acc_read = sem("acc_read")
        stats_ready = sem("stats_ready")
        std_ready = sem("std_ready")
        rstd_ready = sem("rstd_ready")
        normed = sem("normed")
        scaled = sem("scaled")
        x_ready = sem("x_ready")
        turned = sem("turned")
        turn_even = sem("turn_even")
        turn_odd = sem("turn_odd")
        h_rounded = sem("h_rounded")
        h_ready = sem("h_ready")
        w_rounded = sem("w_rounded")
        w_ready = sem("w_ready")
        act_rounded = sem("act_rounded")
        act_split = sem("act_split")
        mix_rounded = sem("mix_rounded")
        mix_split = sem("mix_split")
        tokm_half = sem("tokm_half")
        out_mm = sem("out_mm")
        gate_mm = sem("gate_mm")
        up_mm = sem("up_mm")
        silu_done = sem("silu_done")
        act_ready = sem("act_ready")
        c0_ready = sem("c0_ready")
        feat_mm = sem("feat_mm")
        feat_out = sem("feat_out")
        tokm_mm = sem("tokm_mm")
        tokm_out = sem("tokm_out")
        stored = sem("stored")
        rope_mm = sem("rope_mm")
        rope_done = sem("rope_done")
        scores_mm = sem("scores_mm")
        max_ready = sem("max_ready")
        exp_done = sem("exp_done")
        weights_ready = sem("weights_ready")
        weights_turned = sem("weights_turned")
        weightsT_ready = sem("weightsT_ready")
        att_mm = sem("att_mm")
        att_out = sem("att_out")
        att_var = sem("att_var")
        att_std = sem("att_std")
        lam_dots = sem("lam_dots")
        lam_exp = sem("lam_exp")
        gla_log_mm = sem("gla_log_mm")
        gla_log_abs = sem("gla_log_abs")
        gla_b_ready = sem("gla_b_ready")
        gla_dist = sem("gla_dist")
        gla_exp = sem("gla_exp")
        gla_scaled = sem("gla_scaled")
        gla_att_mm = sem("gla_att_mm")
        gla_att_read = sem("gla_att_read")
        gla_last = sem("gla_last")
        gla_last_exp = sem("gla_last_exp")
        gla_keys = sem("gla_keys")
        gla_keys_mm = sem("gla_keys_mm")
        gla_keysT = sem("gla_keysT")
        gla_out_mm = sem("gla_out_mm")
        gla_out_read = sem("gla_out_read")
        gla_state_mm = sem("gla_state_mm")
        gla_state = sem("gla_state")
        gla_loaded = sem("gla_loaded", True)
        rw_loaded = sem("rw_loaded", True)
        gla_silu = sem("gla_silu")
        gla_var = sem("gla_var")
        gla_std = sem("gla_std")
        squares = sem("squares")
        norm_mm = sem("norm_mm")
        norm_sq = sem("norm_sq")
        norm_root = sem("norm_root")
        values_mm = sem("values_mm")
        values_out = sem("values_out")
        lora_in = sem("lora_in")
        lora_mm = sem("lora_mm")
        rates_ready = sem("rates_ready")
        cum_ready = sem("cum_ready")
        decay_exp = sem("decay_exp")
        decay_used = sem("decay_used")
        bonus_in = sem("bonus_in")
        bonus_mm = sem("bonus_mm")
        prod_mm = sem("prod_mm")
        prod_ready = sem("prod_ready")
        raw_mm = sem("raw_mm")
        bk_ready = sem("bk_ready")
        inv_ready = sem("inv_ready")
        off_ready = sem("off_ready")
        lx_mm = sem("lx_mm")
        lx_ready = sem("lx_ready")
        xlx_mm = sem("xlx_mm")
        r_mm = sem("r_mm")
        r_ready = sem("r_ready")
        u_mm = sem("u_mm")
        u_ready = sem("u_ready")
        state_mm = sem("state_mm")
        state_ready = sem("state_ready")
        unit_read = sem("unit_read")
        gates_mm = sem("gates_mm")
        gates_out = sem("gates_out")
        rw_var = sem("rw_var")
        rw_std = sem("rw_std")
        mix_turned = sem("mix_turned")
        mix_read = sem("mix_read")
        heads_out = sem("heads_out")
        line_v = sem("line_v")
        line_s = sem("line_s")
        line_g = sem("line_g")

        def ring_tile(n):
            return ring[:, n % RING, :].rearrange("p (k n) -> p k n", k=KT)

        def unit_of(n0, u):
            return ring[:, (n0 + u // 2) % RING, (u % 2) * UNIT:(u % 2) * UNIT + UNIT]

        def low_unit(n0, u):
            return ring_r[:, (n0 + u // 2) % RING, (u % 2) * UNIT:(u % 2) * UNIT + UNIT]

        class Meeting:

            def __init__(self, eng):
                self.eng, self.n = eng, 0

            def __call__(self):
                self.n += 4
                self.eng.drain().then_inc(meeting, 1)
                self.eng.wait_ge(meeting, self.n)

        FIRST = {"ada0": 0}
        pos = 0
        for name, n in (("ada0", N_ADA), ("ffn0", N_FFN), ("ada1", N_ADA), ("feat", N_FEAT), ("tokm", N_TOKM),
                        ("out", N_OUT), ("ada2", N_ADA), ("ffn2", N_FFN)):
            FIRST[name] = pos
            pos += n
        UNITS = {"ffn0": 0, "feat": FFN_UNITS}
        UNITS["tokm"] = UNITS["feat"] + 2 * N_FEAT
        UNITS["out"] = UNITS["tokm"] + 2 * N_TOKM
        UNITS["ffn2"] = UNITS["out"] + 2 * N_OUT

        GLA_LEVELS = len(GLA_HALVES) + 1
        RW_LEVELS = 6
        FIRST_DMAS = 3
        LAYER_DMAS = 5

        with nc.Block() as block:
            @block.scalar
            def _(sc):
                sc.dma_start(silu_c[:, :, :], c_in).then_inc(x_loaded, 16)
                sc.dma_start(const[:, :], consts).then_inc(x_loaded, 16)
                sc.dma_start(x[:, :, :], x_in).then_inc(x_loaded, 16)
                sc.wait_ge(x_loaded, 16 * FIRST_DMAS)
                sc.activation(silu_c[:, :, :], silu_c[:, :, :], ACT.Silu)

            @block.vector
            def _(ve):
                ve.memset(eps_col[:, :], LN_EPS)

        with nc.Fori(0, DEPTH) as l:
            with nc.Block() as block:
                @block.sync
                def _(sp):
                    rounds = N_CHUNKS // RING

                    def load(n, slot):
                        sp.dma_start(ring[:, slot, :], weights[l, n]).then_inc(arrived[slot], 16)

                    for s in range(RING):
                        load(s, s)
                    with sp.Fori(1, rounds) as r:
                        for s in range(RING):
                            sp.wait_ge(used, r * RING + (s - RING + 1))
                            load(r * RING + s, s)
                    for n in range(rounds * RING, N_CHUNKS):
                        sp.wait_ge(used, n - RING + 1)
                        load(n, n % RING)

                @block.tensor
                def _(pe):
                    def chunk(n, turn=0):
                        pe.wait_ge(arrived[n % RING], 16 * (n // RING + 1) + 16 * turn)

                    def modulation(j):
                        n0 = FIRST[f"ada{j}"]
                        if j > 0:
                            pe.wait_ge(acc_read, j)
                        for q in range(N_ADA):
                            chunk(n0 + q)
                            w = ring_tile(n0 + q)
                            for k in range(KT):
                                mm = pe.matmul(ps[q // 2][0:2, (q % 2) * 256:(q % 2) * 256 + 256], silu_c[:, k, :],
                                               w[:, k, :], start=(k == 0), stop=(k == KT - 1))
                                if k == 0 and q > 0:
                                    mm.then_inc(used, 1)
                            if q % 2 == 1:
                                mm.then_inc(mod_row_mm, 1)
                        pe.drain().then_inc(used, 1)
                        for i in range(16):
                            if i % 4 == 0:
                                pe.wait_ge(mod_row_ready, 4 * j + i // 4 + 1)
                            mm = pe.matmul(ps[6][:, 2 * i:2 * i + 2], mod_row[0:2, i * P:i * P + P], ident[0:2, 0:2],
                                           start=True, stop=True)
                        mm.then_inc(mods_done, 1)

                    def spread_gate(j):
                        pe.wait_ge(gate_row_ready, j + 1)
                        pe.wait_ge(turn_even, 4 * j + 4)
                        for c in range(2):
                            for n in range(2):
                                pe.matmul(ps[4 + 2 * c + n][:, :], sel[0:2, c, :], gate_row[:, n * 512:n * 512 + 512],
                                          start=True, stop=True).then_inc(gate_wide, 1)

                    def turn_x(j):
                        for k in range(KT):
                            bank = ps[7] if k % 2 == 0 else ps[1]
                            if k >= 2:
                                pe.wait_ge(turn_even if k % 2 == 0 else turn_odd, 4 * j + k // 2)
                            for g in range(GROUPS):
                                if k == 0 and j > 0:
                                    pe.wait_ge(x_ready, GROUPS * (j - 1) + g + 1)
                                mm = pe.transpose(bank[:, g * P:g * P + P], x[:, g, k * P:k * P + P], ident)
                            mm.then_inc(turned, 1)
                        spread_gate(j)

                    def three(out, ws, hs, start, stop, first_inc=None):
                        (w_h, w_l), (h_h, h_l) = ws, hs
                        mm = pe.matmul(out, w_h, h_h, start=start, stop=False, skip_group_check=True)
                        if first_inc is not None:
                            mm.then_inc(first_inc, 1)
                        pe.matmul(out, w_h, h_l, start=False, stop=False, skip_group_check=True)
                        return pe.matmul(out, w_l, h_h, start=False, stop=stop, skip_group_check=True)

                    def feed_forward(j):
                        n0, u0 = FIRST[f"ffn{j}"], UNITS[f"ffn{j}"]
                        i0 = FT * (j // 2)

                        def unit(u, du):
                            pe.wait_ge(w_ready, du + (u0 + u + 1))
                            lo = low_unit(n0, u)
                            return w_hi[:, u % HI_FFN, :], lo, used if u % 2 == 0 and u > 0 else None

                        def widen(bank, u, du, done, fresh=False):
                            hi, lo, free = unit(u, du)
                            for k in range(KT):
                                if fresh:
                                    pe.wait_ge(h_ready, KT * j + k + 1)
                                c = slice(k * P, k * P + P)
                                mm = three(bank[:, 0:TOK], (hi[:, c], lo[:, c]), (h_hi[:, k, :], h_lo[:, k, :]), k == 0,
                                           k == KT - 1, free if k == 0 else None)
                            mm.then_inc(done, 1)

                        def tile_up(f, du, df, first=False):
                            u = 0 if f == 0 else 3 * f - 1
                            if not first:
                                pe.wait_ge(silu_done, df + (i0 + f))
                            widen(ps[0], u, du, gate_mm, fresh=(f == 0))
                            if not first:
                                pe.wait_ge(act_ready, df + (i0 + f))
                            widen(ps[1], u + 1, du, up_mm)

                        def tile_down(f, du, df, first=False, last=False):
                            hi, lo, free = unit(3 * f + 4 if not last else FFN_UNITS - 1, du)
                            pe.wait_ge(act_split, df + (i0 + f + 1))
                            for g in range(GROUPS):
                                t = slice(g * P, g * P + P)
                                a_hi, a_lo = act_hi[:, f % 2, t], act_lo[:, f % 2, t]
                                for a, w in ((a_hi, hi), (a_hi, lo), (a_lo, hi)):
                                    for n in range(2):
                                        mm = pe.matmul(ps[2 + 2 * g + n][:, :], a, w[:, n * 512:n * 512 + 512],
                                                       start=(first and a is a_hi and w is hi),
                                                       stop=(last and a is a_lo), skip_group_check=True)
                                        if free is not None:
                                            mm.then_inc(free, 1)
                                            free = None
                            if last:
                                mm.then_inc(acc_done, 1)

                        tile_up(0, 0, 0, first=(i0 == 0))
                        tile_up(1, 0, 0)
                        pe.wait_ge(gate_ready, 4 * j + 4)
                        tile_down(0, 0, 0, first=True)
                        with pe.Fori(0, (FT - 2) // 4) as r:
                            for f in range(2, 6):
                                tile_up(f, 12 * r, 4 * r)
                                tile_down(f - 1, 12 * r, 4 * r)
                        tile_down(FT - 1, 0, 0, last=True)
                        pe.drain().then_inc(used, 1)

                    def project():
                        n0 = FIRST["feat"]
                        for k in range(KT):
                            if k % 2 == 0:
                                pe.wait_ge(turn_even, KT // 2 + k // 2 + 1)
                            else:
                                pe.wait_ge(turn_odd, KT // 2 + k // 2 + 1)
                            mm = pe.matmul(ps[0][0:64, 0:TOK], wad[:, k, :], mix_h_full[:, k, :], start=(k == 0),
                                           stop=(k == KT - 1))
                        mm.then_inc(feat_mm, 1)
                        for f in range(2 * N_FEAT):
                            if f >= 3:
                                pe.wait_ge(feat_out, f - 2)
                            pe.wait_ge(w_ready, UNITS["feat"] + f + 1)
                            hi, lo = proj_w_hi[:, f % HI_PROJ, :], low_unit(n0, f)
                            for k in range(KT):
                                if f == 0:
                                    pe.wait_ge(h_ready, KT + k + 1)
                                c = slice(k * P, k * P + P)
                                mm = three(ps[(f + 1) % 4][:, 0:TOK], (hi[:, c], lo[:, c]),
                                           (h_hi[:, k, :], mix_h_lo[:, k, :]), k == 0, k == KT - 1,
                                           used if k == 0 and f % 2 == 0 and f > 0 else None)
                            mm.then_inc(feat_mm, 1)
                        for m in range(2 * N_TOKM):
                            q, n0 = m // 2, FIRST["tokm"]
                            if m == 0:
                                pe.wait_ge(gate_ready, 8)
                            pe.wait_ge(w_ready, UNITS["tokm"] + m + 1)
                            hi, lo = proj_w_hi[:, m % HI_PROJ, :], low_unit(n0, m)
                            for g in range(GROUPS):
                                bank = ps[(2 if q % 2 else 5) + g]
                                if m % 2 == 0:
                                    if q >= 2:
                                        pe.wait_ge(tokm_out, GROUPS * (q - 2) + g + 1)
                                    elif q == 1 and g == 0:
                                        pe.wait_ge(feat_out, 2 * N_FEAT + 1)
                                for i in range(4):
                                    k = 4 * (m % 2) + i
                                    c = slice(i * 256, i * 256 + 256)
                                    t = slice(g * P, g * P + P)
                                    mm = three(bank[:, 0:256], (h_hi[:, k, t], mix_h_lo[:, k, t]), (hi[:, c], lo[:, c]),
                                               k == 0, k == KT - 1,
                                               used if k == 0 and g == 0 else None)
                                if m % 2 == 1:
                                    mm.then_inc(tokm_mm, 1)
                            if m % 2 == 0:
                                mm.then_inc(tokm_half, 1)
                        pe.drain().then_inc(used, 1)

                    def attention():
                        for u in range(8):
                            src = (qd if u < 4 else kd)[:, u % 4, P:TOK]
                            pe.matmul(ps[u][:, 0:LAT], con("rope_rot"), src, start=True, stop=True).then_inc(rope_mm, 1)
                        pe.wait_ge(rope_done, 8)

                        def scores(u):
                            g, h = u // HEADS, u % HEADS
                            if u >= 3:
                                pe.wait_ge(exp_done, u - 2)
                            for c in range(2):
                                bank, lo = ps[2 * (u % 3) + c], 64 * c
                                q = qd[lo:lo + 64, h, g * P:g * P + P]
                                if g == 0:
                                    mm = pe.matmul(bank[:, 0:P], q, kd[lo:lo + 64, h, 0:P], start=True, stop=True)
                                else:
                                    pe.matmul(bank[:, 0:LAT], q, kd[lo:lo + 64, h, P:TOK], start=True, stop=True)
                                    mm = pe.matmul(bank[:, LAT:TOK], q, kc[lo:lo + 64, h, :], start=True, stop=True)
                            mm.then_inc(scores_mm, 1)

                        def turn(u):
                            pe.wait_ge(weights_ready, u + 1)
                            if u >= 1:
                                pe.wait_ge(weightsT_ready, u)
                            for b in range(1 if u < HEADS else 3):
                                mm = pe.transpose(ps[6][:, b * P:b * P + P], att[:, u % 2, b * P:b * P + P], ident)
                            mm.then_inc(weights_turned, 1)

                        def values(u):
                            g, h = u // HEADS, u % HEADS
                            pe.wait_ge(weightsT_ready, u + 1)
                            if u >= 1:
                                pe.wait_ge(att_out, u)
                            blocks = [vd[:, 0, :]] if g == 0 else [vd[:, 1, :], vd[:, 2, :], vc]
                            for b, v in enumerate(blocks):
                                mm = pe.matmul(ps[7][:, 0:P], attT[:, u % 2, b * P:b * P + P],
                                               v[:, h * P:h * P + P], start=(b == 0), stop=(b == len(blocks) - 1))
                            mm.then_inc(att_mm, 1)

                        for i in range(GROUPS * HEADS + 3):
                            if i < GROUPS * HEADS:
                                scores(i)
                            if 2 <= i < GROUPS * HEADS + 2:
                                turn(i - 2)
                            if i >= 3:
                                values(i - 3)

                    def gla():
                        for d in range(2):
                            pe.matmul(ps[6 + d][:, 0:TOK], prm("gla_up")[32 * d:32 * d + GLA_LORA, :],
                                      adT[32 * d:32 * d + GLA_LORA, :], start=True, stop=True).then_inc(gla_log_mm, 1)
                        pe.wait_ge(gla_log_abs, 2)
                        for u in range(2 * GLA_LEVELS):
                            pe.wait_ge(gla_scaled, u + 1)
                            if u >= 2:
                                pe.wait_ge(gla_att_read, u - 1)
                            for h in range(HEADS):
                                for g in range(GROUPS):
                                    lo, t = GLA_DK * h, slice(g * P, g * P + P)
                                    mm = pe.matmul(ps[4 * (u % 2) + h][:, t], g_qk[lo:lo + GLA_DK, u % 2, 1, t],
                                                   g_qk[lo:lo + GLA_DK, u % 2, 0, t], start=True, stop=True)
                            mm.then_inc(gla_att_mm, 1)
                        pe.wait_ge(gla_keys, 2)
                        pe.wait_ge(gla_att_read, 2 * GLA_LEVELS)
                        for d in range(2):
                            for g in range(GROUPS):
                                mm = pe.transpose(ps[6 + d][:, g * P:g * P + P], g_kl[:, d, g * P:g * P + P], ident)
                            mm.then_inc(gla_keys_mm, 1)
                        pe.wait_ge(gla_keysT, 2)
                        for i in range(GROUPS):
                            for d in range(2):
                                g = ORDER[d][i]
                                t = slice(g * P, g * P + P)
                                bank = ps[2 * (i % 2) + d]
                                if i == 1:
                                    pe.wait_ge(gla_loaded, 16 * l + 16)
                                if i == 2:
                                    pe.wait_ge(gla_state, 2 + d + 1)
                                    pe.wait_ge(gla_out_read, d + 1)
                                if i >= 1:
                                    pe.matmul(bank[:, 0:GLA_W], g_q0[:, d, t], g_st[:, d, 1, :], start=True, stop=False,
                                              skip_group_check=True)
                                for h in range(HEADS):
                                    mm = pe.matmul(bank[:, 64 * h:64 * h + 64], g_att[:, d, h, t],
                                                   vg[:, g, 64 * h:64 * h + 64], start=(i == 0 and h == 0), stop=True,
                                                   skip_group_check=True)
                                mm.then_inc(gla_out_mm, 1)
                                if i < 2:
                                    if i == 1:
                                        pe.wait_ge(gla_state, d + 1)
                                    pe.matmul(ps[4 + d][:, 0:GLA_W], g_klt[:, d, t], vg[:, g, :], start=True,
                                              stop=True).then_inc(gla_state_mm, 1)

                    def rwkv():
                        for g in range(GROUPS):
                            for i in range(2):
                                mm = pe.transpose(ps[6 + g // 2][:, g % 2 * 256 + i * P:g % 2 * 256 + i * P + P],
                                                  psh[:, 6 + i, pcol(g):pcol(g) + P], ident)
                        mm.then_inc(values_mm, 1)
                        pe.wait_ge(squares, 1)
                        for i in range(2):
                            mm = pe.matmul(ps[4 + i][:, 0:WPAD - 2], con("ones_blk"), kk[:, i, WIN], start=True, stop=True)
                        mm.then_inc(norm_mm, 1)
                        for d in range(2):
                            pe.wait_ge(lora_in, d + 1)
                            if d == 1:
                                pe.wait_ge(norm_sq, 1)
                                pe.wait_ge(values_out, 1)
                            for i in range(2):
                                for part in range(2):
                                    lo = 64 * part
                                    mm = pe.matmul(ps[4 * d + 2 * i + part][:, 0:WPAD - 2],
                                                   rw_up[lo:lo + 64, d, i * P:i * P + P],
                                                   psh[lo:lo + 64, 8 + d, WIN], start=True, stop=True)
                            mm.then_inc(lora_mm, 1)
                        for d in range(2):
                            pe.wait_ge(bonus_in, d + 1)
                            for g in range(GROUPS):
                                for i in range(2):
                                    mm = pe.matmul(ps[4 * d][:, 4 * g:4 * g + 4], rkd[:, i, pcol(g):pcol(g) + P],
                                                   r_k[:, d, i, :], start=(i == 0), stop=(i == 1))
                            mm.then_inc(bonus_mm, 1)

                    def rwkv_units():
                        for i in range(GROUPS):
                            for d in range(2):
                                t = slice(pcol(ORDER[d][i]), pcol(ORDER[d][i]) + P)
                                if i > 0:
                                    pe.wait_ge(unit_read, 2 * (i - 1) + d + 1)
                                for h in range(HEADS):
                                    lo, hp = 64 * (h % 2), h // 2
                                    both = kr[lo:lo + 64, d, hp, :, t]
                                    pe.matmul(ps[4 * d + h][:, 0:256], be[lo:lo + 64, d, hp, t], both, start=True, stop=True)
                                    mm = pe.matmul(ps[4 * d + h][:, 256:512], kh[lo:lo + 64, d, hp, t], both, start=True,
                                                   stop=True)
                                mm.then_inc(prod_mm, 1)
                            for d in range(2):
                                t = slice(pcol(ORDER[d][i]), pcol(ORDER[d][i]) + P)
                                pe.wait_ge(prod_ready, 2 * i + d + 1)
                                for h in range(HEADS):
                                    lo, hp = 64 * (h % 2), h // 2
                                    pe.matmul(ps[4 * d + h % 2][:, hp * P:hp * P + P], kr[lo:lo + 64, d, hp, 0, t],
                                              be[lo:lo + 64, d, hp, t], start=True, stop=True)
                                for hp in range(2):
                                    pe.transpose(ps[4 * d + 3][:, hp * P:hp * P + P], be[:, d, hp, t], ident)
                                    mm = pe.transpose(ps[4 * d + 3][:, 256 + hp * P:256 + hp * P + P], kh[:, d, hp, t], ident)
                                mm.then_inc(raw_mm, 1)
                            for v in range(1, RW_LEVELS):
                                for d in range(2):
                                    pe.wait_ge(inv_ready, 2 * (RW_LEVELS * i + v - 1) + d + 1)
                                    pe.wait_ge(off_ready, 2 * ((RW_LEVELS - 1) * i + v - 1) + d + 1)
                                    for h in range(HEADS):
                                        mm = pe.matmul(ps[4 * d][:, h * P:h * P + P], off[:, d, h, :], xz[:, 0, d, h, :],
                                                       start=True, stop=True)
                                    mm.then_inc(lx_mm, 1)
                                for d in range(2):
                                    pe.wait_ge(lx_ready, 2 * ((RW_LEVELS - 1) * i + v - 1) + d + 1)
                                    for h in range(HEADS):
                                        mm = pe.matmul(ps[4 * d + 1][:, h * P:h * P + P], xz[:, 1, d, h, :], wsb[:, d, h, :],
                                                       start=True, stop=True)
                                    if v < RW_LEVELS - 1:
                                        for h in range(HEADS):
                                            mm = pe.matmul(ps[4 * d + 2][:, h * P:h * P + P], wsb[:, d, h, :],
                                                           xz[:, 1, d, h, :], start=True, stop=True)
                                    mm.then_inc(xlx_mm, 1)
                            for d in range(2):
                                g = ORDER[d][i]
                                pe.wait_ge(inv_ready, 2 * (RW_LEVELS * i + RW_LEVELS - 1) + d + 1)
                                for h in range(HEADS):
                                    v = vt[:, g, 64 * h:64 * h + 64]
                                    pe.matmul(ps[4 * d][:, 64 * h:64 * h + 64], m4[:, d, h, 256:384], v, start=(h == 0),
                                              stop=True, skip_group_check=True)
                                    pe.matmul(ps[4 * d][:, 256 + 64 * h:256 + 64 * h + 64], m4[:, d, h, 384:512], v,
                                              start=False, stop=True, skip_group_check=True)
                            for s in range(2):
                                for d in range(2):
                                    lo = 64 * (s if d == 0 else 1 - s)
                                    t = slice(pcol(ORDER[d][i]) + lo, pcol(ORDER[d][i]) + lo + 64)
                                    if s == 1:
                                        pe.wait_ge(state_ready, 4 * i + d + 1)
                                    elif i == 1:
                                        pe.wait_ge(rw_loaded, 16 * l + 16)
                                    for part in range(2):
                                        for hp in range(2):
                                            o = 256 * part + hp * P
                                            mm = pe.matmul(ps[4 * d][lo:lo + 64, o:o + P], kr[:, d, hp, part, t],
                                                           st[:, d, min(i, 1), hp * P:hp * P + P], start=False, stop=True,
                                                           skip_group_check=True)
                                    mm.then_inc(r_mm, 1)
                                for d in range(2):
                                    lo = 64 * (s if d == 0 else 1 - s)
                                    pe.wait_ge(r_ready, 4 * i + 2 * s + d + 1)
                                    for h in range(HEADS):
                                        mm = pe.matmul(ps[4 * d + 1][lo:lo + 64, 64 * h:64 * h + 64],
                                                       xz[lo:lo + 64, 0, d, h, lo:lo + 64],
                                                       rsb[lo:lo + 64, d, 64 * h:64 * h + 64], start=True, stop=True)
                                    mm.then_inc(u_mm, 1)
                                for d in range(2):
                                    lo, g = 64 * (s if d == 0 else 1 - s), ORDER[d][i]
                                    pe.wait_ge(u_ready, 4 * i + 2 * s + d + 1)
                                    for h in range(HEADS):
                                        pe.matmul(ps[4 * d][:, 256 + 64 * h:256 + 64 * h + 64], m4[lo:lo + 64, d, h, P:2 * P],
                                                  usb[lo:lo + 64, d, 64 * h:64 * h + 64], start=False, stop=True,
                                                  skip_group_check=True)
                                    if i == 0 and s == 0:
                                        pe.wait_ge(bk_ready, d + 1)
                                    elif s == 0:
                                        pe.wait_ge(bk_ready, 2 * i + d + 1)
                                    for hp in range(2):
                                        o = slice(256 + hp * P, 256 + hp * P + P)
                                        pe.matmul(ps[4 * d + 1][:, o], bk[lo:lo + 64, d, hp * P:hp * P + P],
                                                  usb[lo:lo + 64, d, hp * P:hp * P + P], start=(hp == 0), stop=False,
                                                  skip_group_check=True)
                                        mm = pe.matmul(ps[4 * d + 1][:, o], bk[lo:lo + 64, d, 256 + hp * P:256 + hp * P + P],
                                                       vt[lo:lo + 64, g, hp * P:hp * P + P], start=False, stop=True,
                                                       skip_group_check=True)
                                    mm.then_inc(state_mm, 1)

                    def rwkv_gates():
                        for d in range(2):
                            for g in range(GROUPS):
                                t = slice(pcol(g), pcol(g) + P)
                                pe.matmul(ps[1 + 3 * d + g][:, 0:256], psh[:, d, t], g_up[:, d, :], start=True,
                                          stop=True).then_inc(gates_mm, 1)

                    def mix_out():
                        def turn(n):
                            k = OUT_ORDER[n]
                            if n >= 2:
                                pe.wait_ge(mix_read, n - 1)
                            elif n == 1:
                                pe.wait_ge(gates_out, 1)
                            for g in range(GROUPS):
                                mm = pe.transpose(ps[n % 2][:, g * P:g * P + P], mixed[:, g, k * P:k * P + P], ident)
                            mm.then_inc(mix_turned, 1)

                        for n in range(6):
                            turn(n)
                        for n in range(KT):
                            k = OUT_ORDER[n]
                            if n == 5:
                                pe.wait_ge(heads_out, 1)
                                turn(6)
                                turn(7)
                            pe.wait_ge(w_ready, UNITS["out"] + n + 1)
                            pe.wait_ge(mix_split, n + 1)
                            hi, lo = out_w_hi[n % HI_OUT], low_unit(FIRST["out"], n)
                            for g in range(GROUPS):
                                t = slice(g * P, g * P + P)
                                for h in range(2):
                                    c = slice(h * 512, h * 512 + 512)
                                    mm = three(ps[2 + 2 * g + h][:, :], (mixT_hi[:, k, t], mixT_lo[:, k, t]),
                                               (hi[:, c], lo[:, c]), n == 0, n == KT - 1,
                                               used if n % 2 == 0 and n > 0 and g == 0 and h == 0 else None)
                            if n < KT - 1:
                                mm.then_inc(out_mm, 1)
                        mm.then_inc(acc_done, 1)
                        pe.drain().then_inc(used, 1)

                    meet = Meeting(pe)
                    pe.wait_ge(x_loaded, 16 * FIRST_DMAS)
                    modulation(0)
                    pe.wait_ge(par_loaded, 16 * LAYER_DMAS * l + 16 * LAYER_DMAS)
                    turn_x(0)
                    feed_forward(0)
                    modulation(1)
                    turn_x(1)
                    project()
                    meet()
                    attention()
                    meet()
                    gla()
                    meet()
                    rwkv()
                    meet()
                    rwkv_units()
                    meet()
                    rwkv_gates()
                    mix_out()
                    modulation(2)
                    turn_x(2)
                    feed_forward(2)

                @block.scalar
                def _(sc):
                    own = Line(sc, line_s)

                    def round_unit(stretch, u, place, turn=0, du=0):
                        n = FIRST[stretch] + u // 2
                        if u % 2 == 0:
                            sc.wait_ge(arrived[n % RING], 16 * (n // RING + 1) + 16 * turn)
                        sc.activation(place, unit_of(FIRST[stretch], u), ACT.Copy).then_inc(w_rounded, 1)

                    def modulation(j):
                        for b in range(4):
                            sc.wait_ge(mod_row_mm, 6 * j + b + 1)
                            sc.activation(mod_row[0:2, b * 512:b * 512 + 512], ps[b][0:2, :],
                                          ACT.Copy).then_inc(mod_row_ready, 1)

                    def gates(j):
                        for c in range(2):
                            for n in range(2):
                                sc.wait_ge(gate_wide, 4 * j + 2 * c + n + 1)
                                sc.activation(gate[:, c, n * 512:n * 512 + 512], ps[4 + 2 * c + n][:, :], ACT.Copy,
                                              scale=1.0 if j == 1 else 0.5).then_inc(gate_ready, 1)

                    def turn_x(j):
                        full = mix_h_full if j == 1 else h_full
                        sc.wait_ge(cond_ready, j + 1)
                        if j != 1:
                            for u in range(2):
                                round_unit(f"ffn{j}", u, w_hi[:, u, :])
                        for k in range(1, KT, 2):
                            sc.wait_ge(turned, KT * j + k + 1)
                            sc.activation(full[:, k, 0:P], ps[1][:, 0:P], ACT.Identity, bias=cond[:, k, 0:1],
                                          scale=cond[:, 8 + k, 0:1])
                            sc.activation(full[:, k, P:TOK], ps[1][:, P:TOK], ACT.Identity, bias=cond[:, k, 1:2],
                                          scale=cond[:, 8 + k, 1:2]).then_inc(turn_odd, 1)
                        for k in range(KT):
                            if k % 2 == 0:
                                sc.wait_ge(turn_even, 4 * j + k // 2 + 1)
                            else:
                                sc.wait_ge(turn_odd, 4 * j + k // 2 + 1)
                            sc.activation(h_hi[:, k, :], full[:, k, :], ACT.Copy).then_inc(h_rounded, 1)

                    def feed_forward(j):
                        i0 = FT * (j // 2)

                        def silu(b, i, first=False):
                            sc.wait_ge(gate_mm, i + 1)
                            if not first:
                                sc.wait_ge(act_ready, i)
                            sc.activation(sgt[:, b, :], ps[0][:, 0:TOK], ACT.Silu).then_inc(silu_done, 1)

                        for u in range(2, 5):
                            round_unit(f"ffn{j}", u, w_hi[:, u, :])
                        gates(j)
                        silu(0, i0, first=(i0 == 0))

                        def tile(f, r, last=False):
                            silu(f % 2, 4 * r + (i0 + f))
                            for u in range(3 * f + 2, 3 * f + (3 if last else 5)):
                                round_unit(f"ffn{j}", u, w_hi[:, u % HI_FFN, :], turn=r)

                        with sc.Fori(0, (FT - 2) // 4) as r:
                            for f in range(1, 5):
                                tile(f, r)
                        tile(FT - 1, 0, last=True)

                    def norm(j):
                        sc.wait_ge(stats_ready, j + 1)
                        sc.activation(ln_r[:, :, 0], ln_mv[:, :, 1], ACT.Sqrt, bias=eps_col[:, 0:1]).then_inc(std_ready, 1)
                        sc.wait_ge(rstd_ready, j + 1)
                        for g in range(GROUPS):
                            sc.activation(x[:, g, :], x[:, g, :], ACT.Identity, bias=ln_r[:, g, 2:3],
                                          scale=ln_r[:, g, 1:2]).then_inc(normed, 1)

                    def project():
                        def round_feat(f):
                            if f >= HI_PROJ:
                                sc.wait_ge(feat_mm, f - HI_PROJ + 2)
                            round_unit("feat", f, proj_w_hi[:, f % HI_PROJ, :])

                        def round_tokm(m):
                            if m < HI_PROJ:
                                sc.wait_ge(feat_mm, 2 * N_FEAT - HI_PROJ + m + 2)
                            elif m % 2 == 0:
                                sc.wait_ge(tokm_half, m // 2)
                            else:
                                sc.wait_ge(tokm_mm, GROUPS * (m // 2))
                            round_unit("tokm", m, proj_w_hi[:, m % HI_PROJ, :])

                        round_feat(0)
                        round_feat(1)
                        gates(1)
                        sc.wait_ge(feat_mm, 1)
                        sc.activation(adT[0:64, :], ps[0][0:64, 0:TOK], ACT.Copy).then_inc(feat_out, 1)
                        for i in range(2 * N_FEAT):
                            sc.wait_ge(feat_mm, i + 2)
                            if i + 2 < 2 * N_FEAT:
                                round_feat(i + 2)
                            else:
                                round_tokm(i + 2 - 2 * N_FEAT)
                            bank = ps[(i + 1) % 4]
                            if i < 10:
                                sc.activation(praw[:, i, 1:1 + P], bank[:, 0:P], ACT.Copy)
                                out = praw[:, i, pcol(1):pcol(1) + LAT]
                                src, scale = bank[:, P:TOK], 1.0
                            elif i < 12:
                                out, src, scale = (qg, bank[:, 0:TOK], GLA_DK ** -0.5) if i == 10 else (kg, bank[:, 0:TOK], 1.0)
                            elif i < 20:
                                out, src, scale = (qd if i < 16 else kd)[:, i % 4, :], bank[:, 0:TOK], 1.0
                            sc.activation(out, src, ACT.Copy, scale=scale).then_inc(feat_out, 1)
                        for u in range(GROUPS * N_TOKM):
                            q, g = u // GROUPS, u % GROUPS
                            if g == 0 and q < N_TOKM - 1:
                                round_tokm(2 * q + 2)
                            sc.wait_ge(tokm_mm, u + 1)
                            if g == 2 and q < N_TOKM - 1:
                                round_tokm(2 * q + 3)
                            out = vg[:, g, :] if q == 0 else gd[:, q - 1, g, :] if q < 3 else \
                                vd[:, g, (q - 3) * 256:(q - 3) * 256 + 256]
                            sc.activation(out, ps[(2 if q % 2 else 5) + g][:, 0:256], ACT.Copy).then_inc(tokm_out, 1)

                    def attention():
                        sc.dma_start(k_out[l], kd[:, :, 0:P]).then_inc(stored, 16)
                        sc.dma_start(v_out[l], vd[:, 0, :]).then_inc(stored, 16)
                        sc.wait_ge(lam_dots, 1)
                        sc.activation(lam4[:, 2:4], lam4[:, 0:2], ACT.Exp).then_inc(lam_exp, 1)

                        def exponents(u):
                            n = P if u < HEADS else TOK
                            sc.wait_ge(max_ready, u + 1)
                            if u >= 2:
                                sc.wait_ge(weights_ready, u - 1)
                            for c in range(2):
                                ins = sc.activation(e_sb[:, u % 2, c, 0:n], ps[2 * (u % 3) + c][:, 0:n], ACT.Exp,
                                                    bias=att_max[:, u % 2, c:c + 1], scale=DIFF_D ** -0.5,
                                                    accum_out=att_sum[:, u, c:c + 1])
                            ins.then_inc(exp_done, 1)

                        def weights_out(u):
                            n = P if u < HEADS else TOK
                            sc.wait_ge(weights_turned, u + 1)
                            if u >= 2:
                                sc.wait_ge(att_mm, u - 1)
                            sc.activation(attT[:, u % 2, 0:n], ps[6][:, 0:n], ACT.Copy).then_inc(weightsT_ready, 1)

                        def outputs(u):
                            g, h = u // HEADS, u % HEADS
                            sc.wait_ge(att_mm, u + 1)
                            own.link(sc.activation(rope_tmp[:, 0:P], ps[7][:, 0:P], ACT.Square,
                                                   accum_out=diff_ss[:, u:u + 1]))
                            sc.activation(mixed[:, g, 512 + h * P:512 + h * P + P], ps[7][:, 0:P],
                                          ACT.Copy).then_inc(att_out, 1)

                        for i in range(GROUPS * HEADS + 3):
                            if i < GROUPS * HEADS:
                                exponents(i)
                            if 2 <= i < GROUPS * HEADS + 2:
                                weights_out(i - 2)
                            if i >= 3:
                                outputs(i - 3)
                        sc.wait_ge(att_var, 1)
                        sc.activation(diff_ss, diff_ss, ACT.Sqrt).then_inc(att_std, 1)
                        sc.wait_ge(stored, 32)

                    def gla():
                        for d in range(2):
                            sc.wait_ge(gla_log_mm, d + 1)
                            own.step(sc.activation(gz[:, d, :], ps[6 + d][:, 0:TOK], ACT.Identity,
                                                   bias=prm("gla_b")[:, d:d + 1]))
                        own.settle()
                        own.link(sc.activation(ge[:, :, :], gz[:, :, :], ACT.Abs))
                        own.link(sc.activation(ge[:, :, :], ge[:, :, :], ACT.Exp, scale=-1.0))
                        for d in range(2):
                            sc.activation(ge[:, d, :], ge[:, d, :], ACT.Ln, bias=1.0).then_inc(gla_log_abs, 1)
                        for u in range(2 * GLA_LEVELS):
                            b = u % 2
                            sc.wait_ge(gla_dist, u + 1)
                            if u % GLA_LEVELS < GLA_LEVELS - 1:
                                own.link(sc.activation(g_exp[:, b, 0, :], g_dist[:, b, :], ACT.Abs))
                                sc.activation(g_exp[:, b, 0, :], g_exp[:, b, 0, :], ACT.Exp,
                                              scale=-1.0 / GLA_TAU).then_inc(gla_exp, 1)
                            else:
                                sc.activation(g_exp[:, b, 0, :], g_dist[:, b, :], ACT.Exp, scale=1.0 / GLA_TAU)
                                sc.activation(g_exp[:, b, 1, :], g_dist[:, b, :], ACT.Exp,
                                              scale=-1.0 / GLA_TAU).then_inc(gla_exp, 1)
                        for d in range(2):
                            sc.wait_ge(gla_last, d + 1)
                            sc.activation(g_e0[:, d, :], gb[:, d, :], ACT.Exp, scale=1.0 / GLA_TAU)
                            sc.activation(g_kl[:, d, :], g_kl[:, d, :], ACT.Exp, scale=1.0 / GLA_TAU).then_inc(gla_last_exp, 1)
                        for d in range(2):
                            sc.wait_ge(gla_keys_mm, d + 1)
                            sc.activation(g_klt[:, d, :], ps[6 + d][:, 0:TOK], ACT.Copy).then_inc(gla_keysT, 1)
                        for i in range(GROUPS):
                            for d in range(2):
                                sc.wait_ge(gla_out_mm, 2 * i + d + 1)
                                sc.activation(g_o[:, d, ORDER[d][i], :], ps[2 * (i % 2) + d][:, 0:GLA_W],
                                              ACT.Copy).then_inc(gla_out_read, 1)
                        sc.activation(gd[:, :, :, :], gd[:, :, :, :], ACT.Silu).then_inc(gla_silu, 1)
                        sc.wait_ge(gla_state, 2)
                        sc.dma_start(gla_out[l], g_st[:, :, 0, :]).then_inc(stored, 16)
                        sc.wait_ge(gla_var, 1)
                        sc.activation(gla_ss, gla_ss, ACT.Sqrt).then_inc(gla_std, 1)
                        sc.wait_ge(stored, 48)

                    def rwkv():
                        for d in range(2):
                            sc.activation(psh[0:64, 8 + d, WIN], psh[0:64, 8 + d, WIN], ACT.Tanh).then_inc(lora_in, 1)
                        for d in range(2):
                            sc.activation(psh[:, d, WIN], psh[:, d, WIN], ACT.Sigmoid)
                        sc.wait_ge(values_mm, 1)
                        for g in range(GROUPS):
                            ins = sc.activation(vt[:, g, :], ps[6 + g // 2][:, g % 2 * 256:g % 2 * 256 + 256], ACT.Copy)
                        ins.then_inc(values_out, 1)
                        sc.wait_ge(norm_sq, 1)
                        sc.activation(pp[:, :, WIN], pp[:, :, WIN], ACT.Sqrt).then_inc(norm_root, 1)
                        for d in range(2):
                            sc.wait_ge(lora_mm, d + 1)
                            if d == 1:
                                sc.wait_ge(decay_used, 1)
                            for i in range(2):
                                sc.activation(sw[:, i, WIN], ps[4 * d + 2 * i][:, 0:WPAD - 2], ACT.Sigmoid,
                                              bias=w0[:, d, i:i + 1])
                                ins = sc.activation(sa[:, i, WIN], ps[4 * d + 2 * i + 1][:, 0:WPAD - 2], ACT.Sigmoid,
                                                    bias=a0[:, d, i:i + 1])
                            ins.then_inc(rates_ready, 1)
                            sc.wait_ge(cum_ready, d + 1)
                            sc.activation(pp[:, :, WIN], cs[:, :, WIN], ACT.Exp, scale=DECAY)
                            own.link(sc.activation(sw[:, :, WIN], sw[:, :, WIN], ACT.Exp, scale=DECAY))
                            sc.activation(cs[:, :, WIN], cs[:, :, WIN], ACT.Exp, scale=-DECAY).then_inc(decay_exp, 1)

                    def rwkv_units():
                        for i in range(GROUPS):
                            for d in range(2):
                                sc.wait_ge(raw_mm, 2 * i + d + 1)
                                sc.activation(bk[:, d, :], ps[4 * d + 3][:, :], ACT.Copy).then_inc(bk_ready, 1)
                            for v in range(1, RW_LEVELS):
                                for d in range(2):
                                    sc.wait_ge(lx_mm, 2 * ((RW_LEVELS - 1) * i + v - 1) + d + 1)
                                    sc.activation(wsb[:, d, :, :], ps[4 * d][:, :], ACT.Copy).then_inc(lx_ready, 1)

                    def rwkv_gates():
                        sc.dma_start(rw_out[l], st[:, :, 0, :]).then_inc(stored, 16)
                        for d in range(2):
                            for g in range(GROUPS):
                                sc.wait_ge(gates_mm, GROUPS * d + g + 1)
                                ins = sc.activation(ggate[:, d, g, :], ps[1 + 3 * d + g][:, 0:256], ACT.Copy)
                        ins.then_inc(gates_out, 1)

                    def mix_out():
                        def turn(n):
                            sc.wait_ge(mix_turned, n + 1)
                            sc.activation(mixT[:, OUT_ORDER[n], :], ps[n % 2][:, 0:TOK], ACT.Copy).then_inc(mix_read, 1)

                        def high(n):
                            k = OUT_ORDER[n]
                            sc.wait_ge(mix_read, n + 1)
                            sc.activation(mixT_hi[:, k, :], mixT[:, k, :], ACT.Copy).then_inc(mix_rounded, 1)

                        def weight(m):
                            if m >= HI_OUT:
                                sc.wait_ge(out_mm, m - HI_OUT + 1)
                            round_unit("out", m, out_w_hi[m % HI_OUT])

                        weight(0)
                        for n in range(0, 6, 2):
                            turn(n)
                            turn(n + 1)
                            high(n)
                            high(n + 1)
                        weight(1)
                        sc.wait_ge(rw_var, 1)
                        sc.activation(gn_var, gn_var, ACT.Sqrt).then_inc(rw_std, 1)
                        for m in range(2, 6):
                            weight(m)
                        for n in range(6, KT):
                            turn(n)
                        for n in range(6, KT):
                            high(n)
                            weight(n)
                        sc.wait_ge(stored, 64)

                    meet = Meeting(sc)
                    modulation(0)
                    turn_x(0)
                    feed_forward(0)
                    norm(0)
                    modulation(1)
                    turn_x(1)
                    project()
                    meet()
                    attention()
                    meet()
                    gla()
                    meet()
                    rwkv()
                    meet()
                    rwkv_units()
                    meet()
                    rwkv_gates()
                    mix_out()
                    norm(1)
                    modulation(2)
                    turn_x(2)
                    feed_forward(2)
                    norm(2)

                @block.vector
                def _(ve):
                    own = Line(ve, line_v)

                    def rest_unit(stretch, u, place, du=0):
                        ve.wait_ge(w_rounded, du + (UNITS[stretch] + u + 1))
                        raw = unit_of(FIRST[stretch], u)
                        ve.tensor_tensor(low_unit(FIRST[stretch], u), raw, place.bitcast(F32), ALU.subtract).then_inc(w_ready, 1)

                    def modulation(j):
                        ve.wait_ge(gate_bias_loaded, 16 * NMIX * l + 16 * (j + 1))
                        for n in range(2):
                            ve.wait_ge(mod_row_mm, 6 * j + 5 + n)
                            ins = ve.tensor_tensor(gate_row[:, n * 512:n * 512 + 512], ps[4 + n][0:2, :],
                                                   gate_row[:, n * 512:n * 512 + 512], ALU.add)
                        ins.then_inc(gate_row_ready, 1)
                        ve.wait_ge(mods_done, j + 1)
                        own.link(ve.tensor_tensor(cond[:, :, :], ps[6][:, 0:32].rearrange("p (i c) -> p i c", c=2),
                                                  b_mod[:, j, :].unsqueeze(2).to_broadcast([P, 16, 2]), ALU.add))
                        ve.tensor_scalar(cond[:, 8:16, :], cond[:, 8:16, :], 1.0, None, ALU.add).then_inc(cond_ready, 1)

                    def turn_x(j):
                        ve.wait_ge(cond_ready, j + 1)
                        full, low = (mix_h_full, mix_h_lo) if j == 1 else (h_full, h_lo)
                        if j != 1:
                            for u in range(2):
                                rest_unit(f"ffn{j}", u, w_hi[:, u, :])
                        for k in range(0, KT, 2):
                            ve.wait_ge(turned, KT * j + k + 1)
                            ve.tensor_scalar(full[:, k, 0:P], ps[7][:, 0:P], cond[:, 8 + k, 0:1], cond[:, k, 0:1],
                                             ALU.mult, ALU.add)
                            ve.tensor_scalar(full[:, k, P:TOK], ps[7][:, P:TOK], cond[:, 8 + k, 1:2], cond[:, k, 1:2],
                                             ALU.mult, ALU.add).then_inc(turn_even, 1)
                        for k in range(KT):
                            ve.wait_ge(h_rounded, KT * j + k + 1)
                            ve.tensor_tensor(low[:, k, :], full[:, k, :], h_hi[:, k, :].bitcast(F32),
                                             ALU.subtract).then_inc(h_ready, 1)

                    def feed_forward(j):
                        i0 = FT * (j // 2)

                        def product(b, i):
                            ve.wait_ge(silu_done, i + 1)
                            ve.wait_ge(up_mm, i + 1)
                            ve.tensor_tensor(act[:, b, :], sgt[:, b, :], ps[1][:, 0:TOK], ALU.mult).then_inc(act_ready, 1)
                            ve.wait_ge(act_ready, i + 1)
                            ve.tensor_copy(act_hi[:, b, :], act[:, b, :]).then_inc(act_rounded, 1)
                            ve.wait_ge(act_rounded, i + 1)
                            ve.tensor_tensor(act_lo[:, b, :], act[:, b, :], act_hi[:, b, :].bitcast(F32),
                                             ALU.subtract).then_inc(act_split, 1)

                        for u in range(2, 5):
                            rest_unit(f"ffn{j}", u, w_hi[:, u, :])
                        product(0, i0)
                        with ve.Fori(0, (FT - 2) // 4) as r:
                            for f in range(1, 5):
                                for u in range(3 * f + 2, 3 * f + 5):
                                    rest_unit(f"ffn{j}", u, w_hi[:, u % HI_FFN, :], du=12 * r)
                                product(f % 2, 4 * r + (i0 + f))
                        rest_unit(f"ffn{j}", FFN_UNITS - 1, w_hi[:, (FFN_UNITS - 1) % HI_FFN, :])
                        product((FT - 1) % 2, i0 + FT - 1)

                    def norm(j):
                        ve.wait_ge(acc_done, j + 1)
                        for g in range(GROUPS):
                            for n in range(2):
                                ins = ve.tensor_tensor(res_tmp[:, g, n * 512:n * 512 + 512], ps[2 + 2 * g + n][:, :],
                                                       gate[:, min(g, 1), n * 512:n * 512 + 512], ALU.mult)
                        ins.then_inc(acc_read, 1)
                        ve.wait_ge(acc_read, j + 1)
                        for g in range(GROUPS):
                            own.step(ve.scalar_tensor_tensor(x[:, g, :], x[:, g, :], ALPHA, res_tmp[:, g, :], ALU.mult, ALU.add))
                        own.settle()
                        for g in range(GROUPS):
                            for n in range(2):
                                own.step(ve.bn_stats(ln_stat[:, g, 6 * n:6 * n + 6], x[:, g, n * 512:n * 512 + 512]))
                        own.settle()
                        for g in range(GROUPS):
                            ins = ve.bn_aggr(ln_mv[:, g, :], ln_stat[:, g, :])
                        ins.then_inc(stats_ready, 1)
                        ve.wait_ge(std_ready, j + 1)
                        own.link(ve.reciprocal(ln_r[:, :, 1], ln_r[:, :, 0]))
                        ve.scalar_tensor_tensor(ln_r[:, :, 2], ln_mv[:, :, 0], -1.0, ln_r[:, :, 1], ALU.mult,
                                                ALU.mult).then_inc(rstd_ready, 1)
                        ve.wait_ge(lnrow_loaded, 16 * NMIX * l + 16 * (j + 1))
                        for g in range(GROUPS):
                            ve.wait_ge(normed, GROUPS * j + g + 1)
                            ve.tensor_tensor(x[:, g, :], x[:, g, :], lnrow[:, 0, :], ALU.mult).then_inc(scaled, 1)

                    def project():
                        own.link(ve.tensor_tensor(c0, mu[:, 0, :], mu[:, 1, :], ALU.add))
                        own.step(ve.tensor_scalar(c0, c0, -1.0, 1.0, ALU.mult, ALU.add))
                        for col in (0, P + 1, WPAD - 1):
                            own.step(ve.memset(praw[:, :, col:col + 1], 0.0))
                        own.settle()
                        rest_unit("feat", 0, proj_w_hi[:, 0, :])
                        rest_unit("feat", 1, proj_w_hi[:, 1, :])
                        for i in range(10):
                            out = psh[:, PSH[i], WIN]
                            rest_unit("feat", i + 2, proj_w_hi[:, i % HI_PROJ, :])
                            ve.wait_ge(feat_out, i + 2)
                            own.link(ve.tensor_scalar(out, praw[:, i, WIN], c0[:, i:i + 1], None, ALU.mult))
                            own.link(ve.scalar_tensor_tensor(out, praw[:, i, 0:WPAD - 2], mu[:, 0, i:i + 1], out,
                                                             ALU.mult, ALU.add))
                            own.link(ve.scalar_tensor_tensor(out, praw[:, i, 2:WPAD], mu[:, 1, i:i + 1], out,
                                                             ALU.mult, ALU.add))
                        for f in range(12, 2 * N_FEAT):
                            rest_unit("feat", f, proj_w_hi[:, f % HI_PROJ, :])
                        for m in range(2 * N_TOKM):
                            rest_unit("tokm", m, proj_w_hi[:, m % HI_PROJ, :])

                    def attention():
                        lam = row("lam").rearrange("p (m s n) -> p m s n", m=2, s=2)
                        prod = rope_tmp[:, 0:P].rearrange("p (m n) -> p m n", m=2)
                        own.link(ve.tensor_tensor(prod, lam[:, :, 0, :], lam[:, :, 1, :], ALU.mult))
                        ve.tensor_reduce(lam4[:, 0:2], prod, AX, ALU.add).then_inc(lam_dots, 1)
                        ve.wait_ge(lam_exp, 1)
                        own.step(ve.scalar_tensor_tensor(neg_lam, lam4[:, 3:4], prm("lam_init")[:, 0:1], lam4[:, 2:3],
                                                         ALU.subtract, ALU.subtract))
                        own.step(ve.tensor_scalar(diff_gn, row("diff_g"), prm("lam_init")[:, 1:2], None, ALU.mult))
                        own.settle()
                        for u in range(8):
                            part = (qd if u < 4 else kd)[:, u % 4, P:TOK]
                            ve.wait_ge(rope_mm, u + 1)
                            own.step(ve.tensor_tensor(rope_tmp, ps[u][:, 0:LAT], con("rope_sin"), ALU.mult))
                            own.link(ve.tensor_tensor(part, part, con("rope_cos"), ALU.mult))
                            ve.tensor_tensor(part, part, rope_tmp, ALU.add).then_inc(rope_done, 1)
                            ve.wait_ge(rope_done, u + 1)

                        def maxima(u):
                            n = P if u < HEADS else TOK
                            ve.wait_ge(scores_mm, u + 1)
                            if u >= 2:
                                ve.wait_ge(exp_done, u - 1)
                            for c in range(2):
                                own.step(ve.tensor_reduce(att_max[:, u % 2, c:c + 1], ps[2 * (u % 3) + c][:, 0:n], AX, ALU.max))
                            own.settle()
                            ve.tensor_scalar(att_max[:, u % 2, :], att_max[:, u % 2, :], -DIFF_D ** -0.5, None,
                                             ALU.mult).then_inc(max_ready, 1)

                        def weights(u):
                            n, b = P if u < HEADS else TOK, u % 2
                            ve.wait_ge(exp_done, u + 1)
                            own.link(ve.reciprocal(att_r[:, b, :], att_sum[:, u, :]))
                            own.link(ve.tensor_scalar(att_r[:, b, 1:2], att_r[:, b, 1:2], neg_lam, None, ALU.mult))
                            if u >= 2:
                                ve.wait_ge(weights_turned, u - 1)
                            own.link(ve.tensor_scalar(att[:, b, 0:n], e_sb[:, b, 0, 0:n], att_r[:, b, 0:1], None, ALU.mult))
                            ve.scalar_tensor_tensor(att[:, b, 0:n], e_sb[:, b, 1, 0:n], att_r[:, b, 1:2], att[:, b, 0:n],
                                                    ALU.mult, ALU.add).then_inc(weights_ready, 1)

                        for i in range(GROUPS * HEADS + 1):
                            if i < GROUPS * HEADS:
                                maxima(i)
                            if i >= 1:
                                weights(i - 1)
                        ve.wait_ge(att_out, GROUPS * HEADS)
                        ve.tensor_scalar(diff_ss, diff_ss, 1.0 / P, NORM_EPS, ALU.mult, ALU.add).then_inc(att_var, 1)
                        ve.wait_ge(att_std, 1)
                        own.link(ve.reciprocal(diff_ss, diff_ss))
                        for u in range(GROUPS * HEADS):
                            part = mixed[:, u // HEADS, 512 + (u % HEADS) * P:512 + (u % HEADS) * P + P]
                            own.step(ve.scalar_tensor_tensor(part, part, diff_ss[:, u:u + 1], diff_gn, ALU.mult, ALU.mult))

                    def gla():
                        own.step(ve.memset(g_att[:, :, :, :], 0.0))
                        for d in range(2):
                            ve.wait_ge(gla_log_abs, d + 1)
                            own.link(ve.scalar_tensor_tensor(gz[:, d, :], gz[:, d, :], 0.0, ge[:, d, :], ALU.min, ALU.subtract))
                            a, b, keep = gb[:, d, :], gz[:, d, :], gla_keep[:, d, :]
                            if d == 1:
                                a, b, keep = a[:, ::-1], b[:, ::-1], keep[:, ::-1]
                            own.link(ve.tensor_tensor_scan(a, keep, b, 0.0, ALU.mult, ALU.add))

                        def distance(u):
                            d, v = u // GLA_LEVELS, u % GLA_LEVELS
                            if v < GLA_LEVELS - 1:
                                width, at = 2 * GLA_HALVES[v], GLA_HALVES[v] - 1 + d
                            else:
                                width, at = GLA_BASE, max(GLA_BASE // 2 - 1 + d, 0)
                            b = gb[:, d, :].rearrange("p (n w) -> p n w", w=width)
                            out = g_dist[:, u % 2, :].rearrange("p (n w) -> p n w", w=width)
                            ins = ve.tensor_tensor(out, b, b[:, :, at:at + 1].to_broadcast([P, TOK // width, width]),
                                                   ALU.subtract)
                            if v == GLA_LEVELS - 1:
                                own.link(ins)
                                ins = ve.tensor_scalar(g_dist[:, u % 2, :], g_dist[:, u % 2, :], -GLA_CLAMP * GLA_TAU,
                                                       GLA_CLAMP * GLA_TAU, ALU.max, ALU.min)
                            ins.then_inc(gla_dist, 1)

                        def scale(u):
                            b, last = u % 2, u % GLA_LEVELS == GLA_LEVELS - 1
                            ve.wait_ge(gla_exp, u + 1)
                            if u >= 2:
                                ve.wait_ge(gla_att_mm, u - 1)
                            ve.tensor_tensor(g_qk[:, b, 0, :], qg, g_exp[:, b, 0, :], ALU.mult)
                            ve.tensor_tensor(g_qk[:, b, 1, :], kg, g_exp[:, b, 1 if last else 0, :],
                                             ALU.mult).then_inc(gla_scaled, 1)

                        def read(u):
                            d, v = u // GLA_LEVELS, u % GLA_LEVELS
                            mask = gla_base[:, d, :] if v == GLA_LEVELS - 1 else halves[:, 1 - d, GLA_HALVES[v].bit_length() - 1, :]
                            mask = mask.bitcast(I32).unsqueeze(1).to_broadcast([P, GROUPS, P])
                            ve.wait_ge(gla_att_mm, u + 1)
                            for h in range(HEADS):
                                own.step(ve.copy_predicated(g_att[:, d, h, :].rearrange("p (g t) -> p g t", g=GROUPS), mask,
                                                            ps[4 * (u % 2) + h][:, 0:TOK].rearrange("p (g t) -> p g t", g=GROUPS)))
                            own.settle()
                            ve.sem_inc(gla_att_read, 1)

                        n = 2 * GLA_LEVELS
                        distance(0)
                        for u in range(n + 1):
                            if u + 1 < n:
                                distance(u + 1)
                            if u < n:
                                scale(u)
                            if u >= 1:
                                read(u - 1)
                        for d in range(2):
                            b = gb[:, d, :].rearrange("p (g t) -> p g t", g=GROUPS)
                            last = b[:, :, P - 1:P] if d == 0 else b[:, :, 0:1]
                            ve.tensor_tensor(g_kl[:, d, :].rearrange("p (g t) -> p g t", g=GROUPS),
                                             last.to_broadcast([P, GROUPS, P]), b, ALU.subtract).then_inc(gla_last, 1)
                        for d in range(2):
                            ve.wait_ge(gla_last_exp, d + 1)
                            ve.tensor_tensor(g_q0[:, d, :], qg, g_e0[:, d, :], ALU.mult)
                            ve.tensor_tensor(g_kl[:, d, :], kg, g_kl[:, d, :], ALU.mult).then_inc(gla_keys, 1)
                        for i in range(2):
                            for d in range(2):
                                ve.wait_ge(gla_state_mm, 2 * i + d + 1)
                                if i == 0:
                                    ve.tensor_tensor(g_st[:, d, 0, :], ps[4 + d][:, 0:GLA_W], con("gla_blk"),
                                                     ALU.mult).then_inc(gla_state, 1)
                                else:
                                    end = P * ORDER[d][i] + (P - 1 if d == 0 else 0)
                                    own.link(ve.tensor_tensor(g_sq[:, d, 0, :], ps[4 + d][:, 0:GLA_W], con("gla_blk"), ALU.mult))
                                    ve.scalar_tensor_tensor(g_st[:, d, 1, :], g_st[:, d, 1, :], g_e0[:, d, end:end + 1],
                                                            g_sq[:, d, 0, :], ALU.mult, ALU.add).then_inc(gla_state, 1)
                        ve.wait_ge(gla_out_read, 2 * GROUPS)
                        ve.wait_ge(gla_state, 4)
                        own.link(ve.tensor_tensor(g_sq[:, :, :, :], g_o[:, :, :, :], g_o[:, :, :, :], ALU.mult))
                        heads = [P, 2 * GROUPS * HEADS, 64]
                        o = g_o[:, :, :, :].rearrange("p d g (h n) -> p (d g h) n", h=HEADS)
                        sq = g_sq[:, :, :, :].rearrange("p d g (h n) -> p (d g h) n", h=HEADS)
                        own.link(ve.tensor_reduce(gla_ss, sq, AX, ALU.add))
                        ve.tensor_scalar(gla_ss, gla_ss, 1.0 / 64, NORM_EPS, ALU.mult, ALU.add).then_inc(gla_var, 1)
                        ve.wait_ge(gla_std, 1)
                        own.link(ve.reciprocal(gla_ss, gla_ss))
                        own.link(ve.tensor_tensor(o, o, gla_ss.unsqueeze(2).to_broadcast(heads), ALU.mult))
                        own.link(ve.tensor_tensor(o, o, row("gla_g").unsqueeze(1).to_broadcast(heads), ALU.mult))
                        ve.wait_ge(gla_silu, 1)
                        own.link(ve.tensor_tensor(g_o[:, :, :, :], g_o[:, :, :, :], gd[:, :, :, :], ALU.mult))
                        own.step(ve.tensor_tensor(mixed[:, :, 256:512], g_o[:, 0, :, :], g_o[:, 1, :, :], ALU.add))

                    def rwkv():
                        own.step(ve.memset(st[:, :, 0, :], 0.0))
                        own.step(ve.tensor_scalar(ka1, prm("k_a"), -1.0, 1.0, ALU.mult, ALU.add))
                        for i in range(2):
                            own.step(ve.tensor_scalar(kn[:, i, WIN], psh[:, 4 + i, WIN], prm("k_k")[:, i:i + 1], None, ALU.mult))
                        own.settle()
                        ve.tensor_tensor(kk[:, :, WIN], kn[:, :, WIN], kn[:, :, WIN], ALU.mult).then_inc(squares, 1)
                        ve.wait_ge(norm_mm, 1)
                        for i in range(2):
                            ins = ve.tensor_scalar(pp[:, i, WIN], ps[4 + i][:, 0:WPAD - 2], 1e-24, None, ALU.max)
                        ins.then_inc(norm_sq, 1)
                        ve.wait_ge(norm_root, 1)
                        own.link(ve.reciprocal(pp[:, :, WIN], pp[:, :, WIN]))
                        own.link(ve.tensor_tensor(kk[:, :, WIN], kn[:, :, WIN], pp[:, :, WIN], ALU.mult))
                        k_, r_ = psh[:, 4:6, WIN], psh[:, 2:4, WIN]
                        for d in range(2):
                            ve.wait_ge(rates_ready, d + 1)
                            for i in range(2):
                                a, b, keep = cs[:, i, WIN], sw[:, i, WIN], rw_keep[:, d, WIN]
                                if d == 1:
                                    a, b, keep = a[:, ::-1], b[:, ::-1], keep[:, ::-1]
                                own.step(ve.tensor_tensor_scan(a, keep, b, 0.0, ALU.mult, ALU.add))
                            own.settle()
                            ve.tensor_tensor(sw[:, :, WIN], cs[:, :, WIN], sw[:, :, WIN], ALU.subtract).then_inc(cum_ready, 1)
                            for i in range(2):
                                own.step(ve.tensor_scalar(kn[:, i, WIN], sa[:, i, WIN], prm("k_a")[:, i:i + 1], ka1[:, i:i + 1],
                                                          ALU.mult, ALU.add))
                            own.settle()
                            own.link(ve.tensor_tensor(kn[:, :, WIN], kn[:, :, WIN], k_, ALU.mult))
                            ve.tensor_tensor(rkd[:, :, WIN], r_, kn[:, :, WIN], ALU.mult).then_inc(bonus_in, 1)
                            own.step(ve.tensor_tensor(sa[:, :, WIN], sa[:, :, WIN], kk[:, :, WIN], ALU.mult))
                            own.settle()
                            ve.wait_ge(decay_exp, d + 1)
                            own.step(ve.tensor_tensor(kh[:, d, :, WIN], kn[:, :, WIN], cs[:, :, WIN], ALU.mult))
                            own.step(ve.tensor_tensor(be[:, d, :, WIN], sa[:, :, WIN], cs[:, :, WIN], ALU.mult))
                            own.step(ve.tensor_tensor(kr[:, d, :, 0, WIN], kk[:, :, WIN], sw[:, :, WIN], ALU.mult))
                            own.step(ve.tensor_tensor(kr[:, d, :, 1, WIN], r_, pp[:, :, WIN], ALU.mult))
                            for g in range(GROUPS):
                                first = pcol(g) + (CHUNK - 1 if d == 0 else 0)
                                own.step(ve.tensor_copy(pend[:, d, :, 2 * g:2 * g + 2], pp[:, :, first:first + CHUNK + 1:CHUNK]))
                            own.settle()
                            ve.wait_ge(bonus_mm, d + 1)
                            own.link(ve.tensor_copy(bonus[:, 12 * d:12 * d + 12], ps[4 * d][:, 0:12]))
                            ve.sem_inc(decay_used, 1)

                    def rwkv_units():
                        for i in range(GROUPS):
                            for d in range(2):
                                ve.wait_ge(prod_mm, 2 * i + d + 1)
                                mask = rw_mask[:, d, :].unsqueeze(1).to_broadcast([P, 2, 256])
                                for h in range(HEADS):
                                    own.step(ve.tensor_tensor(m4[:, d, h, :].rearrange("p (s n) -> p s n", s=2),
                                                              ps[4 * d + h][:, :].rearrange("p (s n) -> p s n", s=2), mask,
                                                              ALU.mult))
                                own.settle()
                                ve.sem_inc(prod_ready, 1)
                            for d in range(2):
                                ve.wait_ge(raw_mm, 2 * i + d + 1)
                                for h in range(2):
                                    own.step(ve.tensor_copy(am[:, d, h::2, :], ps[4 * d + h][:, 0:256].rearrange(
                                        "p (h n) -> p h n", h=2)))
                                own.settle()
                                wide = [P, HEADS, P]
                                m0 = halves[:, d, 0, :].unsqueeze(1).to_broadcast(wide)
                                m0t = halves[:, 1 - d, 0, :].unsqueeze(1).to_broadcast(wide)
                                one = ident.unsqueeze(1).to_broadcast(wide)
                                own.step(ve.tensor_tensor(xz[:, 0, d, :, :], m4[:, d, :, 0:P], m0t, ALU.mult))
                                own.step(ve.tensor_tensor(xz[:, 1, d, :, :], am[:, d, :, :], m0, ALU.mult))
                                own.settle()
                                own.step(ve.tensor_tensor(xz[:, 0, d, :, :], one, xz[:, 0, d, :, :], ALU.subtract))
                                ve.tensor_tensor(xz[:, 1, d, :, :], one, xz[:, 1, d, :, :], ALU.subtract).then_inc(inv_ready, 1)
                            for v in range(1, RW_LEVELS):
                                for d in range(2):
                                    ve.wait_ge(inv_ready, 2 * (RW_LEVELS * i + v - 1) + d + 1)
                                    ve.wait_ge(xlx_mm, 2 * ((RW_LEVELS - 1) * i + v - 1) + d + 1)
                                    n = 2 if v < RW_LEVELS - 1 else 1
                                    for s in range(n):
                                        ins = ve.tensor_tensor(xz[:, s, d, :, :], xz[:, s, d, :, :],
                                                               ps[4 * d + 1 + s][:, :].rearrange("p (h n) -> p h n", h=HEADS),
                                                               ALU.subtract)
                                    ins.then_inc(inv_ready, 1)
                            for s in range(2):
                                for d in range(2):
                                    lo = 64 * (s if d == 0 else 1 - s)
                                    ve.wait_ge(r_mm, 4 * i + 2 * s + d + 1)
                                    ve.tensor_copy(rsb[lo:lo + 64, d, :], ps[4 * d][lo:lo + 64, 0:256]).then_inc(r_ready, 1)
                                for d in range(2):
                                    lo = 64 * (s if d == 0 else 1 - s)
                                    ve.wait_ge(u_mm, 4 * i + 2 * s + d + 1)
                                    ve.tensor_scalar(usb[lo:lo + 64, d, :], ps[4 * d + 1][lo:lo + 64, 0:256], -1.0, None,
                                                     ALU.mult).then_inc(u_ready, 1)
                                for d in range(2):
                                    c = s if d == 0 else 1 - s
                                    g = ORDER[d][i]
                                    state = st[:, d, min(i, 1), :]
                                    ve.wait_ge(state_mm, 4 * i + 2 * s + d + 1)
                                    blk = con("ones_blk").unsqueeze(1).to_broadcast([P, 2, P])
                                    own.link(ve.tensor_tensor(stmp[:, d, :].rearrange("p (i n) -> p i n", i=2),
                                                              ps[4 * d + 1][:, 256:512].rearrange("p (i n) -> p i n", i=2),
                                                              blk, ALU.mult))
                                    own.link(ve.tensor_tensor(stmp[:, d, :], stmp[:, d, :], state, ALU.add))
                                    for hp in range(2):
                                        own.step(ve.tensor_scalar(state[:, hp * P:hp * P + P], stmp[:, d, hp * P:hp * P + P],
                                                                  pend[:, d, hp, 2 * g + c:2 * g + c + 1], None, ALU.mult))
                                    own.settle()
                                    ve.sem_inc(state_ready, 1)
                            for d in range(2):
                                ve.tensor_copy(yall[:, d, ORDER[d][i], :], ps[4 * d][:, 256:512]).then_inc(unit_read, 1)

                    def mix_out():
                        def low(n):
                            k = OUT_ORDER[n]
                            ve.wait_ge(mix_rounded, n + 1)
                            ve.tensor_tensor(mixT_lo[:, k, :], mixT[:, k, :], mixT_hi[:, k, :].bitcast(F32),
                                             ALU.subtract).then_inc(mix_split, 1)

                        def weight(m):
                            rest_unit("out", m, out_w_hi[m % HI_OUT])

                        heads = [P, 2 * GROUPS * HEADS, 64]
                        y = yall[:, :, :, :].rearrange("p d g (h n) -> p (d g h) n", h=HEADS)
                        t = gtmp[:, :, :, :].rearrange("p d g (h n) -> p (d g h) n", h=HEADS)
                        own.link(ve.tensor_reduce(gn_mean, y, AX, ALU.add))
                        own.link(ve.tensor_scalar(gn_mean, gn_mean, 1.0 / 64, None, ALU.mult))
                        own.link(ve.tensor_tensor(y, y, gn_mean.unsqueeze(2).to_broadcast(heads), ALU.subtract))
                        own.link(ve.tensor_tensor(t, y, y, ALU.mult))
                        own.link(ve.tensor_reduce(gn_var, t, AX, ALU.add))
                        ve.tensor_scalar(gn_var, gn_var, 1.0 / 64, RW_GN_EPS, ALU.mult, ALU.add).then_inc(rw_var, 1)
                        weight(0)
                        low(0)
                        low(1)
                        weight(1)
                        for n in range(2, 6):
                            low(n)
                        for d in range(2):
                            own.step(ve.tensor_tensor(
                                gtmp2[:, d, :, :].rearrange("p g (h n) -> p (g h) n", h=HEADS),
                                vt[:, :, :].rearrange("p g (h n) -> p (g h) n", h=HEADS),
                                bonus[:, 12 * d:12 * d + 12].unsqueeze(2).to_broadcast([P, 12, 64]), ALU.mult))
                        ve.wait_ge(rw_std, 1)
                        own.link(ve.reciprocal(gn_var, gn_var))
                        own.link(ve.tensor_tensor(y, y, gn_var.unsqueeze(2).to_broadcast(heads), ALU.mult))
                        weight(2)
                        for d in range(2):
                            wide = [P, GROUPS, 256]
                            gain = row("gn_g")[:, 256 * d:256 * d + 256].unsqueeze(1).to_broadcast(wide)
                            shift = row("gn_b")[:, 256 * d:256 * d + 256].unsqueeze(1).to_broadcast(wide)
                            own.link(ve.tensor_tensor(yall[:, d, :, :], yall[:, d, :, :], gain, ALU.mult))
                            own.link(ve.tensor_tensor(yall[:, d, :, :], yall[:, d, :, :], shift, ALU.add))
                        weight(3)
                        own.link(ve.tensor_tensor(yall[:, :, :, :], yall[:, :, :, :], gtmp2[:, :, :, :], ALU.add))
                        ve.wait_ge(gates_out, 1)
                        own.link(ve.tensor_tensor(yall[:, :, :, :], yall[:, :, :, :], ggate[:, :, :, :], ALU.mult))
                        weight(4)
                        ve.tensor_tensor(mixed[:, :, 0:256], yall[:, 0, :, :], yall[:, 1, :, :],
                                         ALU.add).then_inc(heads_out, 1)
                        weight(5)
                        for n in range(6, KT):
                            low(n)
                            weight(n)

                    ve.wait_ge(par_loaded, 16 * LAYER_DMAS * l + 16 * LAYER_DMAS)
                    meet = Meeting(ve)
                    modulation(0)
                    turn_x(0)
                    feed_forward(0)
                    norm(0)
                    modulation(1)
                    turn_x(1)
                    project()
                    meet()
                    attention()
                    meet()
                    gla()
                    meet()
                    rwkv()
                    meet()
                    rwkv_units()
                    meet()
                    mix_out()
                    norm(1)
                    modulation(2)
                    turn_x(2)
                    feed_forward(2)
                    norm(2)

                @block.gpsimd
                def _(po):
                    def norm(j):
                        for g in range(GROUPS):
                            po.wait_ge(scaled, GROUPS * j + g + 1)
                            po.tensor_tensor(x[:, g, :], x[:, g, :], lnrow[:, 1, :], ALU.add).then_inc(x_ready, 1)
                        if j < NMIX - 1:
                            po.dma_start(gate_row[:, :], bgate_in[l, :, j + 1, :]).then_inc(gate_bias_loaded, 16)
                        if j == 1:
                            po.wait_ge(x_ready, GROUPS * (j + 1))
                            po.dma_start(lnrow[:, :, :], ln_in[l, j + 1].partition_broadcast(P)).then_inc(lnrow_loaded, 16)

                    def rwkv_units():
                        for i in range(GROUPS):
                            for v in range(1, RW_LEVELS):
                                for d in range(2):
                                    if v == 1:
                                        po.wait_ge(inv_ready, 2 * RW_LEVELS * i + d + 1)
                                    else:
                                        po.wait_ge(lx_mm, 2 * ((RW_LEVELS - 1) * i + v - 2) + d + 1)
                                    po.tensor_tensor(off[:, d, :, :], am[:, d, :, :],
                                                     halves[:, d, v, :].unsqueeze(1).to_broadcast([P, HEADS, P]),
                                                     ALU.mult).then_inc(off_ready, 1)

                    po.dma_start(par[:, :], par_in[l]).then_inc(par_loaded, 16)
                    po.dma_start(wad[:, :, :], w_ad[l]).then_inc(par_loaded, 16)
                    po.dma_start(rows[:, :], row_in[l].partition_broadcast(P)).then_inc(par_loaded, 16)
                    po.dma_start(gate_row[:, :], bgate_in[l, :, 0, :]).then_inc(gate_bias_loaded, 16)
                    po.dma_start(kc, kc_in[l]).then_inc(par_loaded, 16)
                    po.dma_start(vc, vc_in[l]).then_inc(par_loaded, 16)
                    po.dma_start(lnrow[:, :, :], ln_in[l, 0].partition_broadcast(P)).then_inc(lnrow_loaded, 16)
                    meet = Meeting(po)
                    norm(0)
                    meet()
                    meet()
                    po.dma_start(g_st[:, :, 1, :], gla_state_in[l]).then_inc(gla_loaded, 16)
                    meet()
                    po.dma_start(st[:, :, 1, :], rw_state_in[l]).then_inc(rw_loaded, 16)
                    meet()
                    rwkv_units()
                    meet()
                    po.dma_start(lnrow[:, :, :], ln_in[l, 1].partition_broadcast(P)).then_inc(lnrow_loaded, 16)
                    norm(1)
                    norm(2)

            for q in every:
                nc.gpsimd.sem_clear(q)
            nc.all_engine_barrier()

        with nc.Block() as block:
            @block.sync
            def _(sp):
                sp.dma_start(y_out, x[:, :, :]).then_inc(y_stored, 16)
                sp.wait_ge(y_stored, 16)


def kernel(**inputs):
    import concourse.bacc as _bacc
    from concourse.bass_utils import run_bass_kernel_spmd as _run

    a = {k: np.asarray(v) for k, v in inputs.items()}
    L = DEPTH

    def cols(w):
        n = w.shape[2] // 256
        return w.reshape(L, KT, P, n, 256).transpose(0, 3, 2, 1, 4).reshape(L, n, P, CHW)

    def ffn(f):
        g, u = (a[w][:, f].reshape(L, KT, P, FT, P).transpose(0, 3, 2, 1, 4).reshape(L, FT, P, UNIT)
                for w in ("ffn_w_gate", "ffn_w_up"))
        d = a["ffn_w_down"][:, f].reshape(L, FT, P, UNIT)
        order = [g[:, 0], u[:, 0]]
        for t in range(1, FT):
            order += [g[:, t], u[:, t], d[:, t - 1]]
        order.append(d[:, FT - 1])
        return np.stack([np.concatenate(order[i:i + 2], 2) for i in range(0, FFN_UNITS, 2)], 1)

    def tiles_(w):
        n = w.shape[2] // 256
        return w.reshape(L, KT, P, n, 2, P).transpose(0, 3, 2, 4, 1, 5).reshape(L, n, P, CHW)

    def rows_(w):
        n = w.shape[1] // 256
        return w.reshape(L, n, 2, P, DM).transpose(0, 1, 3, 2, 4).reshape(L, n, P, CHW)

    ada = cols(a["w_ada"]).reshape(L, NMIX, N_ADA, P, CHW)
    w_in = a["w_in"]
    gl, df = RW_IN, RW_IN + GLA_IN
    feat = tiles_(np.concatenate([w_in[:, :, 0:RW_IN + 2 * GLA_QK], w_in[:, :, df:df + 2 * DIFF_W]], 2))
    g0 = gl + 2 * GLA_QK + GLA_W
    half = GLA_LORA + GLA_W
    tokm = cols(np.concatenate([w_in[:, :, gl + 2 * GLA_QK:g0], w_in[:, :, g0 + GLA_LORA:g0 + half],
                                w_in[:, :, g0 + half + GLA_LORA:g0 + 2 * half], w_in[:, :, df + 2 * DIFF_W:]], 2))
    w_out = rows_(a["w_out"].reshape(L, KT, P, DM)[:, list(OUT_ORDER)].reshape(L, DM, DM))
    weights = np.concatenate([ada[:, 0], ffn(0), ada[:, 1], feat, tokm, w_out, ada[:, 2], ffn(1)], 1)
    assert weights.shape[1] == N_CHUNKS
    weights = np.ascontiguousarray(weights)
    ad = np.zeros((L, DM, 64), np.float32)
    for d in range(2):
        ad[:, :, 32 * d:32 * d + GLA_LORA] = w_in[:, :, g0 + d * half:g0 + d * half + GLA_LORA]
    ad = ad.reshape(L, KT, P, 64).transpose(0, 2, 1, 3)

    par = np.zeros((L, P, N_PAR), np.float32)

    def tiles(v, n):
        return np.moveaxis(v.reshape(L, -1, P), 2, 1)

    up = par[:, :, PAR["rw_up"]].reshape(L, P, 2, 256)
    up[:, 0:64] = a["rw_w_up"].transpose(0, 2, 1, 3)
    up[:, 64:128] = a["rw_a_up"].transpose(0, 2, 1, 3)
    par[:, :, PAR["rw_up"]] = up.reshape(L, P, 512)
    par[:, :, PAR["g_up"]] = a["rw_g_up"].transpose(0, 2, 1, 3).reshape(L, P, 512)
    for d in range(2):
        par[:, 32 * d:32 * d + GLA_LORA, PAR["gla_up"]] = a["gla_a_up"][:, d]
    b_ada = a["b_ada"].reshape(L, NMIX, 3, DM)
    par[:, :, PAR["b_mod"]] = tiles(b_ada[:, :, 0:2], 8)
    par[:, :, PAR["mu"]] = tiles(a["rw_mu"], 10)
    par[:, :, PAR["k_k"]] = tiles(a["rw_k_k"], 2)
    par[:, :, PAR["k_a"]] = tiles(a["rw_k_a"], 2)
    par[:, :, PAR["w0"]] = tiles(a["rw_w0"], 2)
    par[:, :, PAR["a0"]] = tiles(a["rw_a0"], 2)
    par[:, :, PAR["gla_b"]] = tiles(a["gla_a_b"], 1)
    rk = np.zeros((L, P, 2, 2, HEADS), np.float32)
    for h in range(HEADS):
        lo = 64 * (h % 2)
        rk[:, lo:lo + 64, :, h // 2, h] = a["rw_r_k"][:, :, h, :].transpose(0, 2, 1)
    par[:, :, PAR["r_k"]] = rk.reshape(L, P, 16)
    for l in range(L):
        par[l, :, PAR["lam_init"]] = (0.8 - 0.6 * math.exp(-0.3 * l), 1.0 - (0.8 - 0.6 * math.exp(-0.3 * l)))
    ln = np.concatenate([a["ln_g"], a["ln_b"]], 2)
    row = np.concatenate([a["rw_gn_g"].reshape(L, -1), a["rw_gn_b"].reshape(L, -1), a["gla_gn_g"], a["diff_gn_g"],
                          a["diff_lam"].reshape(L, -1)], 1)
    bg = np.stack([b_ada[:, :, 2]] * 2, 1)
    rw0 = np.zeros((L, P, 2, 2, P), np.float32)
    gl0 = np.zeros((L, P, 2, HEADS, 64), np.float32)
    for h in range(HEADS):
        lo = 64 * (h % 2)
        rw0[:, lo:lo + 64, :, h // 2, lo:lo + 64] = a["state_rwkv"][0, :, :, h].transpose(0, 3, 1, 2)
        gl0[:, GLA_DK * h:GLA_DK * h + GLA_DK, :, h, :] = a["state_gla"][0, :, :, h].transpose(0, 2, 1, 3)
    kc = a["cache_diff_k"][0].transpose(0, 3, 2, 1)
    vc = a["cache_diff_v"][0].reshape(L, PAST, DIFF_W)
    xx = np.concatenate([a["x_prompt"][0], a["x_sample"][0]], 0).reshape(GROUPS, P, DM).transpose(1, 0, 2)
    cc = np.stack([a["c_ctx"], a["c"][0]], 1).reshape(KT, P, 2).transpose(1, 0, 2)

    ins = {"x_in": xx, "c_in": cc, "consts": shape_constants(), "weights": weights, "w_ad": ad, "par_in": par,
           "ln_in": ln, "row_in": row, "bgate_in": bg, "rw_state": rw0.reshape(L, P, 2, 256),
           "gla_state": gl0.reshape(L, P, 2, 256), "kc_in": kc, "vc_in": vc}
    outs = {"y_out": (P, GROUPS, DM), "rw_out": (L, P, 2, 256), "gla_out": (L, P, 2, 256),
            "k_out": (L, P, HEADS, P), "v_out": (L, P, DIFF_W)}
    nc = _bacc.Bacc("TRN2", target_bir_lowering=False, num_devices=1)
    arrays = {k: np.ascontiguousarray(v) for k, v in ins.items()}
    args = [nc.dram_tensor(k, v.shape, F32, kind="ExternalInput").ap() for k, v in arrays.items()]
    args += [nc.dram_tensor(k, v, F32, kind="ExternalOutput").ap() for k, v in outs.items()]
    trunk_kernel(nc, *args)
    r = _run(nc, [arrays], core_ids=[0])
    got = {k: r.results[0][k] for k in outs}

    y = got["y_out"].transpose(1, 0, 2)
    new_rw = np.stack([got["rw_out"].reshape(L, P, 2, 2, P)[:, 64 * (h % 2):64 * (h % 2) + 64, :, h // 2,
                                                             64 * (h % 2):64 * (h % 2) + 64].transpose(0, 2, 3, 1)
                       for h in range(HEADS)], 2)
    new_gla = np.stack([got["gla_out"].reshape(L, P, 2, HEADS, 64)[:, GLA_DK * h:GLA_DK * h + GLA_DK, :, h]
                        .transpose(0, 2, 1, 3) for h in range(HEADS)], 2)
    new_k = got["k_out"].transpose(0, 3, 2, 1)
    new_v = got["v_out"].reshape(L, P, HEADS, P)
    return (y[0][None], y[1:].reshape(1, LAT, DM), new_rw[None], new_gla[None], new_k[None], new_v[None])
```

```python
import math
from contextlib import ExitStack

import numpy as np

import concourse.bass as bass
from concourse import mybir

F32 = mybir.dt.float32
I32 = mybir.dt.int32
FR = mybir.dt.float32r
ALU = mybir.AluOpType
ACT = mybir.ActivationFunctionType
AX = mybir.AxisListType.X

P = 128
DM = 1024
KT = DM // P
DEPTH = 2
GROUPS = 3
TOK = GROUPS * P
LAT = TOK - P
GRID_W = 64
PAST = 128
NMIX = 3
D_FF = 2816
FT = D_FF // P
RW_W = 256
RW_IN = 1280
GLA_QK = 128
GLA_W = 256
GLA_DK = 32
GLA_LORA = 16
GLA_TAU = 16.0
GLA_IN = 1056
DIFF_D = 64
DIFF_W = 512
HEADS = 4
ALPHA = (2 * DEPTH) ** 0.25
LN_EPS = 1e-5
NORM_EPS = 1e-6
RW_GN_EPS = 64e-5
DECAY = -math.exp(-0.5)
CHUNK = 64
WPAD = TOK + 3
WIN = slice(1, WPAD - 1)
GLA_HALVES = (64, 32, 16)
GLA_BASE = 16
GLA_CLAMP = 80.0
ORDER = ((0, 1, 2), (0, 2, 1))

CHW = 2048
RING = 6
N_ADA = 12
N_FFN = 3 * FT // 2
UNIT = CHW // 2
FFN_UNITS = 3 * FT
HI_FFN = 6
HI_PROJ = 2
HI_OUT = 2
N_FEAT = 10
N_TOKM = 5
N_OUT = 4
OUT_ORDER = (2, 3, 4, 5, 6, 7, 0, 1)
N_CHUNKS = NMIX * N_ADA + 2 * N_FFN + N_FEAT + N_TOKM + N_OUT


ROPE_BANK = (2, 3, 6, 7)
PSH = (2, 3, 4, 5, 6, 7, 8, 0, 9, 1)


def pcol(g):
    return 1 + P * g + (g > 0)


CONST = {}
_at = 0
for _name, _width in (("ident", 128), ("ones_blk", 128), ("rope_rot", 128), ("rope_cos", LAT), ("rope_sin", LAT),
                      ("rw_mask", 2 * 256), ("halves", 2 * 7 * 128), ("gla_base", 2 * 128), ("rw_keep", 2 * WPAD),
                      ("gla_keep", 2 * TOK), ("gla_blk", 256), ("sel", 256)):
    CONST[_name] = slice(_at, _at + _width)
    _at += _width
N_CONST = _at

PAR = {}
_at = 0
for _name, _width in (("rw_up", 2 * 256), ("g_up", 2 * 256), ("gla_up", 128), ("b_mod", NMIX * 16), ("mu", 20),
                      ("k_k", 2), ("k_a", 2), ("w0", 4), ("a0", 4), ("gla_b", 2), ("r_k", 16), ("lam_init", 2)):
    PAR[_name] = slice(_at, _at + _width)
    _at += _width
N_PAR = _at

ROW = {}
_at = 0
for _name, _width in (("gn_g", 512), ("gn_b", 512), ("gla_g", 64), ("diff_g", 128), ("lam", 256)):
    ROW[_name] = slice(_at, _at + _width)
    _at += _width
N_ROW = _at


def shape_constants():
    out = np.zeros((P, N_CONST), np.float32)
    i = np.arange(P)
    s, t = i[:, None], i[None, :]
    out[:, CONST["ident"]] = s == t
    out[:, CONST["ones_blk"]] = s // 64 == t // 64
    rot = np.zeros((P, P), np.float32)
    for f in range(P):
        if f % 32 < 16:
            rot[f, f + 16] = -1.0
        else:
            rot[f, f - 16] = 1.0
    out[:, CONST["rope_rot"]] = rot.T
    tok = np.arange(LAT)
    inv = 10000.0 ** (-np.arange(16, dtype=np.float32) / np.float32(16))
    pos = np.where((i % 64 < 32)[:, None], (tok // GRID_W)[None, :], (tok % GRID_W)[None, :]).astype(np.float32)
    ang = pos * inv[i % 16][:, None].astype(np.float32)
    out[:, CONST["rope_cos"]] = np.cos(ang)
    out[:, CONST["rope_sin"]] = np.sin(ang)
    same = s // CHUNK == t // CHUNK
    masks = out[:, CONST["rw_mask"]].reshape(P, 2, 2, P)
    for d, (strict, incl) in enumerate(((s < t, s <= t), (s > t, s >= t))):
        masks[:, d, 0] = same & strict
        masks[:, d, 1] = same & incl
    halves = out[:, CONST["halves"]].reshape(P, 2, 7, P)
    for n in range(7):
        h = 1 << n
        one = s // (2 * h) == t // (2 * h)
        halves[:, 0, n] = one & (s % (2 * h) >= h) & (t % (2 * h) < h)
        halves[:, 1, n] = one & (s % (2 * h) < h) & (t % (2 * h) >= h)
    base = out[:, CONST["gla_base"]].reshape(P, 2, P)
    one = s // GLA_BASE == t // GLA_BASE
    base[:, 0] = one & (s <= t)
    base[:, 1] = one & (s >= t)
    keep = out[:, CONST["rw_keep"]].reshape(P, 2, WPAD)
    keep[:] = 1.0
    gkeep = out[:, CONST["gla_keep"]].reshape(P, 2, TOK)
    gkeep[:] = 1.0
    for g in range(GROUPS):
        gkeep[:, 0, P * g] = 0.0
        gkeep[:, 1, P * g + P - 1] = 0.0
        for c in range(P // CHUNK):
            keep[:, 0, pcol(g) + CHUNK * c] = 0.0
            keep[:, 1, pcol(g) + CHUNK * c + CHUNK - 1] = 0.0
    blk = out[:, CONST["gla_blk"]].reshape(P, HEADS, 64)
    for h in range(HEADS):
        blk[GLA_DK * h:GLA_DK * h + GLA_DK, h] = 1.0
    sel = out[:, CONST["sel"]].reshape(P, 2, P)
    sel[0, 0] = 1.0
    sel[1, 1] = 1.0
    return out


class Line:

    def __init__(self, eng, sem):
        self.eng, self.sem, self.n = eng, sem, 0

    def step(self, ins):
        ins.then_inc(self.sem, 1)
        self.n += 1

    def settle(self):
        self.eng.wait_ge(self.sem, self.n)

    def link(self, ins):
        self.step(ins)
        self.settle()


class Carve:

    def __init__(self, row, rounded_row):
        self.row, self.rounded_row, self.at, self.top = row, rounded_row, 0, 0

    def rounded(self, n):
        return self(n, self.rounded_row)

    def __call__(self, n, row=None):
        got = (self.row if row is None else row)[:, self.at:self.at + n]
        self.at += n
        self.top = max(self.top, self.at)
        assert self.top <= self.row.shape[1], self.top
        return got


def trunk_kernel(nc, x_in, c_in, consts, weights, w_ad, par_in, ln_in, row_in, bgate_in, rw_state_in, gla_state_in,
                 kc_in, vc_in, first_ada, b_first, y_out, rw_out, gla_out, k_out, v_out, dumps=None):
    with ExitStack() as ctx:
        def sb(name, shape):
            return ctx.enter_context(nc.sbuf_tensor(name, shape, F32))

        every = []

        def sem(name, lasting=False):
            s = ctx.enter_context(nc.semaphore(name))
            if not lasting:
                every.append(s)
            return s

        ps = [ctx.enter_context(nc.psum_tensor(f"bank{i}", [P, 512], F32)) for i in range(8)]

        def with_rounded(name, shape):
            plain = sb(name, shape)
            end = nc.sbuf_base
            size = 4 * math.prod(shape[1:])
            return plain, nc.alloc_sbuf_tensor_at(name + "_r", shape, FR, offset=end - size)

        ring, ring_r = with_rounded("ring", [P, RING, CHW])
        x = sb("x", [P, GROUPS, DM])
        const = sb("const", [P, N_CONST])
        par = sb("par", [P, N_PAR])
        wad = sb("wad", [P, KT, 64])
        rows = sb("rows", [P, N_ROW])
        silu_c = sb("silu_c", [P, KT, 2])
        cond = sb("cond", [P, 16, 2])
        gate_row = sb("gate_row", [2, DM])
        gate = sb("gate", [P, 2, DM])
        lnrow, lnrow_r = with_rounded("lnrow", [P, 2, DM])
        ln_stat = sb("ln_stat", [P, GROUPS, 12])
        ln_mv = sb("ln_mv", [P, GROUPS, 2])
        ln_r = sb("ln_r", [P, GROUPS, 3])
        small = sb("small", [P, 192])
        arena, arena_r = with_rounded("arena", [P, 23660])

        def con(name):
            return const[:, CONST[name]]

        ident = con("ident")
        halves = con("halves").rearrange("p (d n t) -> p d n t", d=2, n=7)
        rw_mask = con("rw_mask").rearrange("p (d m) -> p d m", d=2)
        rw_keep = con("rw_keep").rearrange("p (d m) -> p d m", d=2)
        gla_keep = con("gla_keep").rearrange("p (d m) -> p d m", d=2)
        gla_base = con("gla_base").rearrange("p (d m) -> p d m", d=2)
        sel = con("sel").rearrange("p (c m) -> p c m", c=2)

        def prm(name):
            return par[:, PAR[name]]

        def row(name):
            return rows[:, ROW[name]]

        rw_up = prm("rw_up").rearrange("p (d m) -> p d m", d=2)
        g_up = prm("g_up").rearrange("p (d m) -> p d m", d=2)
        b_mod = prm("b_mod").rearrange("p (j m) -> p j m", j=NMIX)
        mu = prm("mu").rearrange("p (m i) -> p m i", m=2)
        w0 = prm("w0").rearrange("p (d i) -> p d i", d=2)
        a0 = prm("a0").rearrange("p (d i) -> p d i", d=2)
        r_k = prm("r_k").rearrange("p (d i h) -> p d i h", d=2, i=2)

        put = Carve(arena, arena_r)
        h_hi = put.rounded(KT * TOK).rearrange("p (k t) -> p k t", k=KT)
        ffn_mark = put.at
        h_lo = put.rounded(KT * TOK).rearrange("p (k t) -> p k t", k=KT)
        h_mark = put.at
        h_full = put(KT * TOK).rearrange("p (k t) -> p k t", k=KT)
        put.at = h_mark
        act = put(2 * TOK).rearrange("p (b t) -> p b t", b=2)
        act_hi = put.rounded(2 * TOK).rearrange("p (b t) -> p b t", b=2)
        act_lo = put.rounded(2 * TOK).rearrange("p (b t) -> p b t", b=2)
        sgt = put(2 * TOK).rearrange("p (b t) -> p b t", b=2)
        w_hi = put.rounded(HI_FFN * UNIT).rearrange("p (s n) -> p s n", s=HI_FFN)
        put.at = ffn_mark
        mod_row = put(2 * DM)
        put.at = h_mark
        res_tmp = put(GROUPS * DM).rearrange("p (g n) -> p g n", g=GROUPS)
        put.at = ffn_mark
        psh = put(10 * WPAD).rearrange("p (i t) -> p i t", i=10)
        mixed = put(GROUPS * DM).rearrange("p (g n) -> p g n", g=GROUPS)
        put.at -= GROUPS * DM
        mix_h_lo = put.rounded(KT * TOK).rearrange("p (k t) -> p k t", k=KT)
        mixer_mark = put.at
        qg = put(TOK)
        kg = put(TOK)
        vg = put(GROUPS * GLA_W).rearrange("p (g n) -> p g n", g=GROUPS)
        gd = put(2 * GROUPS * GLA_W).rearrange("p (d g n) -> p d g n", d=2, g=GROUPS)
        adT = put(TOK)
        diff_mark = put.at
        praw = put(10 * WPAD).rearrange("p (i t) -> p i t", i=10)
        att_mark = put.at
        mix_h_full = put(KT * TOK).rearrange("p (k t) -> p k t", k=KT)
        put.at = att_mark
        qd = put(HEADS * TOK).rearrange("p (h t) -> p h t", h=HEADS)
        kd = put(HEADS * TOK).rearrange("p (h t) -> p h t", h=HEADS)
        vd = put(GROUPS * DIFF_W).rearrange("p (g n) -> p g n", g=GROUPS)
        kc = put(HEADS * PAST).rearrange("p (h t) -> p h t", h=HEADS)
        vc = put(DIFF_W)
        put.at = diff_mark
        e_sb = put(2 * 2 * TOK).rearrange("p (b c t) -> p b c t", b=2, c=2)
        att = put(2 * TOK).rearrange("p (b t) -> p b t", b=2)
        attT = put(2 * TOK).rearrange("p (b t) -> p b t", b=2)
        rope_tmp = put(2 * LAT).rearrange("p (h t) -> p h t", h=2)
        squares_tmp = wad[:, :, :].rearrange("p k n -> p (k n)")[:, 0:P]
        assert put.at <= att_mark
        put.at = diff_mark
        gb = put(2 * TOK).rearrange("p (d t) -> p d t", d=2)
        gz = mixed[:, :, 0:256]
        ge = mixed[:, :, 256:512]
        g_sq = put(2 * GROUPS * GLA_W).rearrange("p (d g n) -> p d g n", d=2, g=GROUPS)
        g_dist = put(2 * TOK).rearrange("p (b t) -> p b t", b=2)
        g_klt = g_dist
        g_att = put(2 * HEADS * TOK).rearrange("p (d h t) -> p d h t", d=2, h=HEADS)
        g_q0 = put(2 * TOK).rearrange("p (d t) -> p d t", d=2)
        g_e0 = put(2 * TOK).rearrange("p (d t) -> p d t", d=2)
        g_kl = put(2 * TOK).rearrange("p (d t) -> p d t", d=2)
        g_o = put(2 * GROUPS * GLA_W).rearrange("p (d g n) -> p d g n", d=2, g=GROUPS)
        g_st = lnrow[:, 0, :].rearrange("p (d s n) -> p d s n", d=2, s=2)
        put.at = 0
        g_exp = put(2 * 2 * TOK).rearrange("p (b s t) -> p b s t", b=2, s=2)
        g_qk = put(2 * 2 * TOK).rearrange("p (b s t) -> p b s t", b=2, s=2)
        assert put.at <= ffn_mark
        put.at = mixer_mark
        kr = put(2 * 2 * 2 * WPAD).rearrange("p (d i s t) -> p d i s t", d=2, i=2, s=2)
        be = put(2 * 2 * WPAD).rearrange("p (d i t) -> p d i t", d=2, i=2)
        kh = put(2 * 2 * WPAD).rearrange("p (d i t) -> p d i t", d=2, i=2)
        vt = put(GROUPS * RW_W).rearrange("p (g n) -> p g n", g=GROUPS)
        pend = put(2 * 2 * 6).rearrange("p (d i c) -> p d i c", d=2, i=2)
        st = put(2 * 2 * 256).rearrange("p (d s n) -> p d s n", d=2, s=2)
        yall = put(2 * GROUPS * RW_W).rearrange("p (d g n) -> p d g n", d=2, g=GROUPS)
        unit_mark = put.at

        def wide():
            return put(2 * WPAD).rearrange("p (i t) -> p i t", i=2)

        pp, kk, kn, rkd = wide(), wide(), wide(), wide()
        put.at = 0
        sw, sa, cs = wide(), wide(), wide()
        assert put.at <= ffn_mark
        put.at = unit_mark
        m4 = put(2 * HEADS * 512).rearrange("p (d h n) -> p d h n", d=2, h=HEADS)
        put.at = 0
        xz = put(2 * 2 * 512).rearrange("p (s d h n) -> p s d h n", s=2, d=2, h=HEADS)
        off = put(2 * 512).rearrange("p (d h n) -> p d h n", d=2, h=HEADS)
        assert put.at <= ffn_mark
        put.at = ffn_mark + 2 * WPAD
        am = put(2 * 512).rearrange("p (d h n) -> p d h n", d=2, h=HEADS)
        wsb = put(2 * 512).rearrange("p (d h n) -> p d h n", d=2, h=HEADS)
        bk = put(2 * 512).rearrange("p (d n) -> p d n", d=2)
        assert put.at <= ffn_mark + 10 * WPAD
        spare = lnrow[:, :, :].rearrange("p s (a n) -> p (s a) n", n=512)
        rsb = spare[:, 0, :].rearrange("p (d n) -> p d n", d=2)
        usb = spare[:, 1, :].rearrange("p (d n) -> p d n", d=2)
        stmp = spare[:, 2, :].rearrange("p (d n) -> p d n", d=2)
        put.at = unit_mark
        gtmp = put(1536).rearrange("p (d g n) -> p d g n", d=2, g=GROUPS)
        gtmp2 = put(1536).rearrange("p (d g n) -> p d g n", d=2, g=GROUPS)
        out_w_hi = [put.rounded(UNIT)]
        put.at = mixer_mark + KT * TOK
        out_w_hi.append(put.rounded(UNIT))
        ggate = put(1536).rearrange("p (d g n) -> p d g n", d=2, g=GROUPS)
        put.at = 0
        mixT = put(KT * TOK).rearrange("p (k t) -> p k t", k=KT)
        mixT_hi = put.rounded(KT * TOK).rearrange("p (k t) -> p k t", k=KT)
        assert put.at <= ffn_mark + 10 * WPAD
        put.at = mixer_mark
        mixT_lo = put.rounded(KT * TOK).rearrange("p (k t) -> p k t", k=KT)
        proj_w_hi = lnrow_r[:, :, :]

        neg_lam = small[:, 0:1]
        lam4 = small[:, 1:5]
        c0 = small[:, 8:18]
        ka1 = small[:, 18:20]
        att_max = small[:, 20:24].rearrange("p (b c) -> p b c", b=2)
        att_r = small[:, 24:28].rearrange("p (b c) -> p b c", b=2)
        att_sum = small[:, 28:52].rearrange("p (u c) -> p u c", c=2)
        diff_ss = small[:, 52:64]
        gla_ss = small[:, 64:88]
        gn_mean = small[:, 88:112]
        gn_var = small[:, 112:136]
        bonus = small[:, 136:160]
        first_bias = small[:, 160:176]
        diff_gn = lnrow[:, 1, 0:P]
        eps_col = sb("eps_col", [P, 1])

        arrived = [sem(f"arrived{s}") for s in range(RING)]
        used = sem("used")
        x_loaded = sem("x_loaded", True)
        y_stored = sem("y_stored", True)
        c_loaded = sem("c_loaded", True)
        silu_ready = sem("silu_ready", True)
        first_bias_loaded = sem("first_bias_loaded", True)
        par_loaded = sem("par_loaded", True)
        lnrow_loaded = sem("lnrow_loaded", True)
        gate_bias_loaded = sem("gate_bias_loaded", True)
        meeting = sem("meeting")
        mods_done = sem("mods_done")
        cond_sum = sem("cond_sum")
        cond_ready = sem("cond_ready")
        mod_row_mm = sem("mod_row_mm")
        mod_row_ready = sem("mod_row_ready")
        gate_row_ready = sem("gate_row_ready")
        gate_wide = sem("gate_wide")
        gate_ready = sem("gate_ready")
        acc_done = sem("acc_done")
        acc_read = sem("acc_read")
        stats_ready = sem("stats_ready")
        std_ready = sem("std_ready")
        rstd_ready = sem("rstd_ready")
        normed = sem("normed")
        scaled = sem("scaled")
        x_ready = sem("x_ready")
        x_last_ready = sem("x_last_ready")
        turned = sem("turned")
        turn_even = sem("turn_even")
        turn_odd = sem("turn_odd")
        h_rounded = sem("h_rounded")
        h_ready = sem("h_ready")
        w_rounded = sem("w_rounded")
        w_ready = sem("w_ready")
        act_rounded = sem("act_rounded")
        act_split = sem("act_split")
        mix_rounded = sem("mix_rounded")
        mix_split = sem("mix_split")
        tokm_half = sem("tokm_half")
        out_mm = sem("out_mm")
        gate_mm = sem("gate_mm")
        up_mm = sem("up_mm")
        silu_done = sem("silu_done")
        act_ready = sem("act_ready")
        c0_ready = sem("c0_ready")
        feat_mm = sem("feat_mm")
        feat_out = sem("feat_out")
        tokm_mm = sem("tokm_mm")
        tokm_out = sem("tokm_out")
        stored = sem("stored")
        rope_mm = sem("rope_mm")
        rope_done = sem("rope_done")
        scores_mm = sem("scores_mm")
        max_ready = sem("max_ready")
        exp_done = sem("exp_done")
        weights_ready = sem("weights_ready")
        weights_turned = sem("weights_turned")
        weightsT_ready = sem("weightsT_ready")
        att_mm = sem("att_mm")
        att_out = sem("att_out")
        att_var = sem("att_var")
        att_std = sem("att_std")
        lam_dots = sem("lam_dots")
        lam_exp = sem("lam_exp")
        gla_log_mm = sem("gla_log_mm")
        gla_cleared = sem("gla_cleared")
        gla_log_read = sem("gla_log_read")
        gla_log_abs = sem("gla_log_abs")
        gla_b_ready = sem("gla_b_ready")
        gla_dist = sem("gla_dist")
        gla_exp = sem("gla_exp")
        gla_scaled = sem("gla_scaled")
        gla_att_mm = sem("gla_att_mm")
        gla_att_read = sem("gla_att_read")
        gla_last = sem("gla_last")
        gla_last_exp = sem("gla_last_exp")
        gla_keys = sem("gla_keys")
        gla_keys_mm = sem("gla_keys_mm")
        gla_keysT = sem("gla_keysT")
        gla_out_mm = sem("gla_out_mm")
        gla_out_read = sem("gla_out_read")
        gla_state_mm = sem("gla_state_mm")
        gla_state = sem("gla_state")
        gla_loaded = sem("gla_loaded", True)
        rw_loaded = sem("rw_loaded", True)
        gla_silu = sem("gla_silu")
        gla_var = sem("gla_var")
        gla_std = sem("gla_std")
        squares = sem("squares")
        norm_mm = sem("norm_mm")
        norm_sq = sem("norm_sq")
        norm_root = sem("norm_root")
        kk_ready = sem("kk_ready")
        keys_ready = sem("keys_ready")
        rate_kk = sem("rate_kk")
        values_mm = sem("values_mm")
        values_out = sem("values_out")
        lora_in = sem("lora_in")
        lora_mm = sem("lora_mm")
        rates_ready = sem("rates_ready")
        cum_ready = sem("cum_ready")
        decay_exp = sem("decay_exp")
        decay_used = sem("decay_used")
        bonus_in = sem("bonus_in")
        bonus_mm = sem("bonus_mm")
        prod_mm = sem("prod_mm")
        prod_ready = sem("prod_ready")
        raw_mm = sem("raw_mm")
        bk_ready = sem("bk_ready")
        inv_first = sem("inv_first")
        inv_ready = sem("inv_ready")
        off_ready = sem("off_ready")
        lx_mm = sem("lx_mm")
        lx_ready = sem("lx_ready")
        xlx_mm = sem("xlx_mm")
        r_mm = sem("r_mm")
        r_ready = sem("r_ready")
        u_mm = sem("u_mm")
        u_ready = sem("u_ready")
        state_mm = sem("state_mm")
        state_ready = sem("state_ready")
        unit_read = sem("unit_read")
        gates_mm = sem("gates_mm")
        gates_out = sem("gates_out")
        rw_var = sem("rw_var")
        rw_std = sem("rw_std")
        mix_turned = sem("mix_turned")
        mix_read = sem("mix_read")
        heads_out = sem("heads_out")
        line_v = sem("line_v")
        line_s = sem("line_s")
        line_g = sem("line_g")

        def ring_tile(n):
            return ring[:, n % RING, :].rearrange("p (k n) -> p k n", k=KT)

        def unit_of(n0, u):
            return ring[:, (n0 + u // 2) % RING, (u % 2) * UNIT:(u % 2) * UNIT + UNIT]

        def low_unit(n0, u):
            return ring_r[:, (n0 + u // 2) % RING, (u % 2) * UNIT:(u % 2) * UNIT + UNIT]

        class Meeting:

            def __init__(self, eng):
                self.eng, self.n = eng, 0

            def __call__(self):
                self.n += 4
                self.eng.drain().then_inc(meeting, 1)
                self.eng.wait_ge(meeting, self.n)

        FIRST = {}
        pos = 0
        for name, n in (("ffn0", N_FFN), ("ada1", N_ADA), ("feat", N_FEAT), ("tokm", N_TOKM),
                        ("out", N_OUT), ("ada2", N_ADA), ("ffn2", N_FFN),
                        ("ada3", N_ADA)):
            FIRST[name] = pos
            pos += n
        UNITS = {"ffn0": 0, "feat": FFN_UNITS}
        UNITS["tokm"] = UNITS["feat"] + 2 * N_FEAT
        UNITS["out"] = UNITS["tokm"] + 2 * N_TOKM
        UNITS["ffn2"] = UNITS["out"] + 2 * N_OUT

        GLA_LEVELS = len(GLA_HALVES) + 1
        RW_LEVELS = 6
        LAYER_DMAS = 5

        def row_product(pe, n0, q, k):
            if k == 0:
                pe.wait_ge(arrived[(n0 + q) % RING], 16 * ((n0 + q) // RING + 1))
            mm = pe.matmul(ps[q // 2][0:2, (q % 2) * 256:(q % 2) * 256 + 256], silu_c[:, k, :],
                           ring_tile(n0 + q)[:, k, :], start=(k == 0), stop=(k == KT - 1))
            if k == 0 and q > 0:
                mm.then_inc(used, 1)
            elif k == KT - 1 and q % 2 == 1:
                mm.then_inc(mod_row_mm, 1)

        def modulation_rows(pe, j, n0):
            m = max(j - 1, 0)
            for q in range(8):
                if j > 0 and q == 4:
                    pe.wait_ge(acc_read, j)
                for k in range(KT):
                    row_product(pe, n0, q, k)
            if j == 0:
                pe.wait_ge(x_loaded, 32)
            for i in range(16):
                if i % 4 == 0:
                    pe.wait_ge(mod_row_ready, 4 * m + i // 4 + 1)
                mm = pe.matmul(ps[6][:, 2 * i:2 * i + 2], mod_row[0:2, i * P:i * P + P], ident[0:2, 0:2],
                               start=True, stop=True)
            mm.then_inc(mods_done, 1)

        def gate_rows(pe, n0, steps):
            for s in steps:
                row_product(pe, n0, 8 + s // KT, s % KT)
            if s == 4 * KT - 1:
                pe.drain().then_inc(used, 1)

        def modulation_copies(sc, j):
            m = max(j - 1, 0)
            for b in range(4):
                sc.wait_ge(mod_row_mm, 6 * m + b + 1)
                sc.activation(mod_row[0:2, b * 512:b * 512 + 512], ps[b][0:2, :],
                              ACT.Copy).then_inc(mod_row_ready, 1)

        def modulation_sums(ve, j, bias):
            m = max(j - 1, 0)
            ve.wait_ge(mods_done, m + 1)
            ve.tensor_tensor(cond[:, :, :], ps[6][:, 0:32].rearrange("p (i c) -> p i c", c=2),
                             bias.unsqueeze(2).to_broadcast([P, 16, 2]), ALU.add).then_inc(cond_sum, 1)
            ve.wait_ge(cond_sum, m + 1)
            ve.tensor_scalar(cond[:, 8:16, :], cond[:, 8:16, :], 1.0, None, ALU.add).then_inc(cond_ready, 1)

        def gate_sums(ve, j, l):
            m = max(j - 1, 0)
            ve.wait_ge(gate_bias_loaded, 16 * NMIX * l + 16 * (j + 1))
            for n in range(2):
                ve.wait_ge(mod_row_mm, 6 * m + 5 + n)
                ins = ve.tensor_tensor(gate_row[:, n * 512:n * 512 + 512], ps[4 + n][0:2, :],
                                       gate_row[:, n * 512:n * 512 + 512], ALU.add)
            ins.then_inc(gate_row_ready, 1)

        def clear(sems):
            for q in sems:
                nc.gpsimd.sem_clear(q)
            nc.all_engine_barrier()

        with nc.Block() as block:
            @block.sync
            def _(sp):
                for n in range(N_ADA):
                    if n >= RING:
                        sp.wait_ge(used, n - RING + 1)
                    sp.dma_start(ring[:, n % RING, :], first_ada[n]).then_inc(arrived[n % RING], 16)

            @block.tensor
            def _(pe):
                pe.wait_ge(silu_ready, 1)
                modulation_rows(pe, 0, 0)
                gate_rows(pe, 0, range(4 * KT))

            @block.scalar
            def _(sc):
                sc.dma_start(silu_c[:, :, :], c_in).then_inc(c_loaded, 16)
                sc.wait_ge(c_loaded, 16)
                sc.activation(silu_c[:, :, :], silu_c[:, :, :], ACT.Silu).then_inc(silu_ready, 1)
                sc.dma_start(const[:, :], consts).then_inc(x_loaded, 16)
                sc.dma_start(x[:, :, :], x_in).then_inc(x_loaded, 16)
                modulation_copies(sc, 0)

            @block.vector
            def _(ve):
                ve.memset(eps_col[:, :], LN_EPS)
                ve.wait_ge(first_bias_loaded, 16)
                modulation_sums(ve, 0, first_bias)
                gate_sums(ve, 0, 0)

            @block.gpsimd
            def _(po):
                po.dma_start(gate_row[:, :], bgate_in[0, :, 0, :]).then_inc(gate_bias_loaded, 16)
                po.dma_start(first_bias, b_first).then_inc(first_bias_loaded, 16)

        clear([*arrived, used, mod_row_mm, mod_row_ready, mods_done, cond_sum, cond_ready, gate_row_ready])

        def layer(l, last):
            with nc.Block() as block:
                @block.sync
                def _(sp):
                    chunks = N_CHUNKS - (N_ADA if last else 0)
                    rounds = chunks // RING

                    def load(n, slot):
                        sp.dma_start(ring[:, slot, :], weights[l, n]).then_inc(arrived[slot], 16)

                    for s in range(RING):
                        load(s, s)
                    with sp.Fori(1, rounds) as r:
                        for s in range(RING):
                            sp.wait_ge(used, r * RING + (s - RING + 1))
                            load(r * RING + s, s)
                    for n in range(rounds * RING, chunks):
                        sp.wait_ge(used, n - RING + 1)
                        load(n, n % RING)
                    if last:
                        for g in range(GROUPS):
                            if g < 2:
                                sp.wait_ge(x_ready, 2 * (NMIX - 1) + g + 1)
                            else:
                                sp.wait_ge(x_last_ready, NMIX)
                            sp.dma_start(y_out[:, g, :], x[:, g, :]).then_inc(y_stored, 16)
                        sp.wait_ge(y_stored, 16 * GROUPS)

                @block.tensor
                def _(pe):
                    def chunk(n, turn=0):
                        pe.wait_ge(arrived[n % RING], 16 * (n // RING + 1) + 16 * turn)

                    def spread_gate(j):
                        if j > 0:
                            pe.wait_ge(gate_row_ready, j)
                        pe.wait_ge(turn_even, 4 * j + 4)
                        for c in range(2):
                            for n in range(2):
                                pe.matmul(ps[4 + 2 * c + n][:, :], sel[0:2, c, :], gate_row[:, n * 512:n * 512 + 512],
                                          start=True, stop=True).then_inc(gate_wide, 1)

                    def turn_x(j):
                        for k in range(KT):
                            bank = ps[7] if k % 2 == 0 else ps[1]
                            if k >= 2:
                                pe.wait_ge(turn_even if k % 2 == 0 else turn_odd, 4 * j + k // 2)
                            for g in range(GROUPS):
                                if k == 0 and j > 0:
                                    if g < 2:
                                        pe.wait_ge(x_ready, 2 * (j - 1) + g + 1)
                                    else:
                                        pe.wait_ge(x_last_ready, j)
                                mm = pe.transpose(bank[:, g * P:g * P + P], x[:, g, k * P:k * P + P], ident)
                            mm.then_inc(turned, 1)
                            if j > 0:
                                gate_rows(pe, FIRST[f"ada{j}"], range(4 * k, 4 * k + 4))

                    def three(out, ws, hs, start, stop, first_inc=None):
                        (w_h, w_l), (h_h, h_l) = ws, hs
                        mm = pe.matmul(out, w_h, h_h, start=start, stop=False, skip_group_check=True)
                        if first_inc is not None:
                            mm.then_inc(first_inc, 1)
                        pe.matmul(out, w_h, h_l, start=False, stop=False, skip_group_check=True)
                        return pe.matmul(out, w_l, h_h, start=False, stop=stop, skip_group_check=True)

                    def feed_forward(j):
                        n0, u0 = FIRST[f"ffn{j}"], UNITS[f"ffn{j}"]
                        i0 = FT * (j // 2)

                        def unit(u, du):
                            pe.wait_ge(w_ready, du + (u0 + u + 1))
                            lo = low_unit(n0, u)
                            return w_hi[:, u % HI_FFN, :], lo, used if u % 2 == 0 and u > 0 else None

                        def widen(bank, u, du, done, fresh=False):
                            hi, lo, free = unit(u, du)
                            for k in range(KT):
                                if fresh:
                                    pe.wait_ge(h_ready, KT * j + k + 1)
                                c = slice(k * P, k * P + P)
                                mm = three(bank[:, 0:TOK], (hi[:, c], lo[:, c]), (h_hi[:, k, :], h_lo[:, k, :]), k == 0,
                                           k == KT - 1, free if k == 0 else None)
                            mm.then_inc(done, 1)

                        def tile_up(f, du, df, first=False):
                            u = 0 if f == 0 else 3 * f - 1
                            if not first:
                                pe.wait_ge(silu_done, df + (i0 + f))
                            widen(ps[0], u, du, gate_mm, fresh=(f == 0))
                            if not first:
                                pe.wait_ge(act_ready, df + (i0 + f))
                            widen(ps[1], u + 1, du, up_mm)

                        def tile_down(f, du, df, first=False, last=False):
                            hi, lo, free = unit(3 * f + 4 if not last else FFN_UNITS - 1, du)
                            pe.wait_ge(act_split, df + (i0 + f + 1))
                            for g in range(GROUPS):
                                t = slice(g * P, g * P + P)
                                a_hi, a_lo = act_hi[:, f % 2, t], act_lo[:, f % 2, t]
                                for a, w in ((a_hi, hi), (a_hi, lo), (a_lo, hi)):
                                    for n in range(2):
                                        mm = pe.matmul(ps[2 + 2 * g + n][:, :], a, w[:, n * 512:n * 512 + 512],
                                                       start=(first and a is a_hi and w is hi),
                                                       stop=(last and a is a_lo), skip_group_check=True)
                                        if free is not None:
                                            mm.then_inc(free, 1)
                                            free = None
                            if last:
                                mm.then_inc(acc_done, 1)

                        tile_up(0, 0, 0, first=(i0 == 0))
                        spread_gate(j)
                        tile_up(1, 0, 0)
                        pe.wait_ge(gate_ready, 4 * j + 4)
                        tile_down(0, 0, 0, first=True)
                        with pe.Fori(0, (FT - 2) // 4) as r:
                            for f in range(2, 6):
                                tile_up(f, 12 * r, 4 * r)
                                tile_down(f - 1, 12 * r, 4 * r)
                        tile_down(FT - 1, 0, 0, last=True)
                        pe.drain().then_inc(used, 1)

                    def project():
                        n0 = FIRST["feat"]
                        for k in range(KT):
                            if k % 2 == 0:
                                pe.wait_ge(turn_even, KT // 2 + k // 2 + 1)
                            else:
                                pe.wait_ge(turn_odd, KT // 2 + k // 2 + 1)
                            mm = pe.matmul(ps[0][0:64, 0:TOK], wad[:, k, :], mix_h_full[:, k, :], start=(k == 0),
                                           stop=(k == KT - 1))
                        mm.then_inc(feat_mm, 1)
                        for f in range(2 * N_FEAT):
                            if f == 1:
                                spread_gate(1)
                            if f >= 3:
                                pe.wait_ge(feat_out, f - 2)
                            pe.wait_ge(w_ready, UNITS["feat"] + f + 1)
                            hi, lo = proj_w_hi[:, f % HI_PROJ, :], low_unit(n0, f)
                            for k in range(KT):
                                if f == 0:
                                    pe.wait_ge(h_ready, KT + k + 1)
                                c = slice(k * P, k * P + P)
                                mm = three(ps[(f + 1) % 4][:, 0:TOK], (hi[:, c], lo[:, c]),
                                           (h_hi[:, k, :], mix_h_lo[:, k, :]), k == 0, k == KT - 1,
                                           used if k == 0 and f % 2 == 0 and f > 0 else None)
                            mm.then_inc(feat_mm, 1)
                        for m in range(2 * N_TOKM):
                            q, n0 = m // 2, FIRST["tokm"]
                            if m == 0:
                                pe.wait_ge(gate_ready, 8)
                            pe.wait_ge(w_ready, UNITS["tokm"] + m + 1)
                            hi, lo = proj_w_hi[:, m % HI_PROJ, :], low_unit(n0, m)
                            for g in range(GROUPS):
                                bank = ps[(2 if q % 2 else 5) + g]
                                if m % 2 == 0:
                                    if q >= 2:
                                        pe.wait_ge(tokm_out, GROUPS * (q - 2) + g + 1)
                                    elif q == 1 and g == 0:
                                        pe.wait_ge(feat_out, 2 * N_FEAT + 1)
                                for i in range(4):
                                    k = 4 * (m % 2) + i
                                    c = slice(i * 256, i * 256 + 256)
                                    t = slice(g * P, g * P + P)
                                    mm = three(bank[:, 0:256], (h_hi[:, k, t], mix_h_lo[:, k, t]), (hi[:, c], lo[:, c]),
                                               k == 0, k == KT - 1,
                                               used if k == 0 and g == 0 else None)
                                if m % 2 == 1:
                                    mm.then_inc(tokm_mm, 1)
                            if m % 2 == 0:
                                mm.then_inc(tokm_half, 1)
                        pe.drain().then_inc(used, 1)

                    def attention():
                        for d in range(2):
                            pe.matmul(ps[4 + d][:, 0:TOK], prm("gla_up")[32 * d:32 * d + GLA_LORA, :],
                                      adT[32 * d:32 * d + GLA_LORA, :], start=True, stop=True).then_inc(gla_log_mm, 1)
                        for p in range(4):
                            src = (qd if p < 2 else kd)[:, 2 * (p % 2):2 * (p % 2) + 2, P:TOK]
                            pe.matmul(ps[ROPE_BANK[p]][:, :].rearrange("p (h t) -> p h t", h=2), con("rope_rot"), src,
                                      start=True, stop=True).then_inc(rope_mm, 1)

                        def scores(u):
                            g, h = u // HEADS, u % HEADS
                            if u == 1:
                                pe.wait_ge(rope_done, 2)
                            elif u == 2:
                                pe.wait_ge(gla_log_read, 2)
                            elif u >= 3:
                                pe.wait_ge(exp_done, u - 2)
                            if u == HEADS:
                                pe.wait_ge(rope_done, 4)
                            for c in range(2):
                                bank, lo = ps[2 * (u % 3) + c], 64 * c
                                q = qd[lo:lo + 64, h, g * P:g * P + P]
                                if g == 0:
                                    mm = pe.matmul(bank[:, 0:P], q, kd[lo:lo + 64, h, 0:P], start=True, stop=True)
                                else:
                                    pe.matmul(bank[:, 0:LAT], q, kd[lo:lo + 64, h, P:TOK], start=True, stop=True)
                                    mm = pe.matmul(bank[:, LAT:TOK], q, kc[lo:lo + 64, h, :], start=True, stop=True)
                            mm.then_inc(scores_mm, 1)

                        def turn(u):
                            pe.wait_ge(weights_ready, u + 1)
                            if u == 0:
                                pe.wait_ge(rope_done, 3)
                            else:
                                pe.wait_ge(weightsT_ready, u)
                            for b in range(1 if u < HEADS else 3):
                                mm = pe.transpose(ps[6][:, b * P:b * P + P], att[:, u % 2, b * P:b * P + P], ident)
                            mm.then_inc(weights_turned, 1)

                        def values(u):
                            g, h = u // HEADS, u % HEADS
                            pe.wait_ge(weightsT_ready, u + 1)
                            if u == 0:
                                pe.wait_ge(rope_done, 4)
                            else:
                                pe.wait_ge(att_out, u)
                            blocks = [vd[:, 0, :]] if g == 0 else [vd[:, 1, :], vd[:, 2, :], vc]
                            for b, v in enumerate(blocks):
                                mm = pe.matmul(ps[7][:, 0:P], attT[:, u % 2, b * P:b * P + P],
                                               v[:, h * P:h * P + P], start=(b == 0), stop=(b == len(blocks) - 1))
                            mm.then_inc(att_mm, 1)

                        for i in range(GROUPS * HEADS + 3):
                            if i < GROUPS * HEADS:
                                scores(i)
                            if 2 <= i < GROUPS * HEADS + 2:
                                turn(i - 2)
                            if i >= 3:
                                values(i - 3)

                    def gla():
                        for u in range(2 * GLA_LEVELS):
                            pe.wait_ge(gla_scaled, u + 1)
                            if u >= 2:
                                pe.wait_ge(gla_att_read, u - 1)
                            for h in range(HEADS):
                                for g in range(GROUPS):
                                    lo, t = GLA_DK * h, slice(g * P, g * P + P)
                                    mm = pe.matmul(ps[4 * (u % 2) + h][:, t], g_qk[lo:lo + GLA_DK, u % 2, 1, t],
                                                   g_qk[lo:lo + GLA_DK, u % 2, 0, t], start=True, stop=True)
                            mm.then_inc(gla_att_mm, 1)
                        pe.wait_ge(gla_keys, 2)
                        pe.wait_ge(gla_att_read, 2 * GLA_LEVELS)
                        for d in range(2):
                            for g in range(GROUPS):
                                mm = pe.transpose(ps[6 + d][:, g * P:g * P + P], g_kl[:, d, g * P:g * P + P], ident)
                            mm.then_inc(gla_keys_mm, 1)
                        pe.wait_ge(gla_keysT, 2)
                        for i in range(GROUPS):
                            for d in range(2):
                                g = ORDER[d][i]
                                t = slice(g * P, g * P + P)
                                bank = ps[2 * (i % 2) + d]
                                if i == 1:
                                    pe.wait_ge(gla_loaded, 16 * l + 16)
                                if i == 2:
                                    pe.wait_ge(gla_state, 2 + d + 1)
                                    pe.wait_ge(gla_out_read, d + 1)
                                if i >= 1:
                                    pe.matmul(bank[:, 0:GLA_W], g_q0[:, d, t], g_st[:, d, 1, :], start=True, stop=False,
                                              skip_group_check=True)
                                for h in range(HEADS):
                                    mm = pe.matmul(bank[:, 64 * h:64 * h + 64], g_att[:, d, h, t],
                                                   vg[:, g, 64 * h:64 * h + 64], start=(i == 0 and h == 0), stop=True,
                                                   skip_group_check=True)
                                mm.then_inc(gla_out_mm, 1)
                                if i < 2:
                                    if i == 1:
                                        pe.wait_ge(gla_state, d + 1)
                                    pe.matmul(ps[4 + d][:, 0:GLA_W], g_klt[:, d, t], vg[:, g, :], start=True,
                                              stop=True).then_inc(gla_state_mm, 1)

                    def products(i, d, heads):
                        t = slice(pcol(ORDER[d][i]), pcol(ORDER[d][i]) + P)
                        for h in heads:
                            lo, hp = 64 * (h % 2), h // 2
                            both = kr[lo:lo + 64, d, hp, :, t]
                            pe.matmul(ps[4 * d + h][:, 0:256], be[lo:lo + 64, d, hp, t], both, start=True, stop=True)
                            mm = pe.matmul(ps[4 * d + h][:, 256:512], kh[lo:lo + 64, d, hp, t], both, start=True,
                                           stop=True)
                        return mm

                    def rwkv():
                        def lora(d):
                            pe.wait_ge(lora_in, d + 1)
                            for i in range(2):
                                for part in range(2):
                                    lo = 64 * part
                                    mm = pe.matmul(ps[4 * d + 2 * i + part][:, 0:WPAD - 2],
                                                   rw_up[lo:lo + 64, d, i * P:i * P + P],
                                                   psh[lo:lo + 64, 8 + d, WIN], start=True, stop=True)
                            mm.then_inc(lora_mm, 1)

                        pe.wait_ge(gla_out_read, 2 * GROUPS)
                        pe.wait_ge(gla_state, 4)
                        pe.wait_ge(squares, 1)
                        for i in range(2):
                            mm = pe.matmul(ps[4 + i][:, 0:WPAD - 2], con("ones_blk"), kk[:, i, WIN], start=True, stop=True)
                        mm.then_inc(norm_mm, 1)
                        lora(0)
                        for g in range(GROUPS):
                            for i in range(2):
                                mm = pe.transpose(ps[6 + g // 2][:, g % 2 * 256 + i * P:g % 2 * 256 + i * P + P],
                                                  psh[:, 6 + i, pcol(g):pcol(g) + P], ident)
                        mm.then_inc(values_mm, 1)
                        pe.wait_ge(norm_sq, 1)
                        pe.wait_ge(values_out, 1)
                        lora(1)
                        pe.wait_ge(decay_used, 1)
                        products(0, 0, range(HEADS)).then_inc(prod_mm, 1)
                        pe.wait_ge(rates_ready, 2)
                        for d in range(2):
                            pe.wait_ge(bonus_in, d + 1)
                            for g in range(GROUPS):
                                for i in range(2):
                                    mm = pe.matmul(ps[4 + d][:, 4 * g:4 * g + 4], rkd[:, i, pcol(g):pcol(g) + P],
                                                   r_k[:, d, i, :], start=(i == 0), stop=(i == 1))
                            mm.then_inc(bonus_mm, 1)

                    def rwkv_units():
                        for i in range(GROUPS):
                            for d in range(2):
                                if i > 0:
                                    pe.wait_ge(unit_read, 2 * (i - 1) + d + 1)
                                    products(i, d, (0, 1)).then_inc(prod_mm, 1)
                                elif d == 1:
                                    products(i, d, range(HEADS)).then_inc(prod_mm, 1)
                            for d in range(2):
                                t = slice(pcol(ORDER[d][i]), pcol(ORDER[d][i]) + P)
                                pe.wait_ge(prod_ready, 2 * i + d + 1)
                                for h in range(HEADS):
                                    lo, hp = 64 * (h % 2), h // 2
                                    pe.matmul(ps[4 * d + h % 2][:, hp * P:hp * P + P], kr[lo:lo + 64, d, hp, 0, t],
                                              be[lo:lo + 64, d, hp, t], start=True, stop=True)
                                for hp in range(2):
                                    pe.transpose(ps[4 * d + 3][:, hp * P:hp * P + P], be[:, d, hp, t], ident)
                                    mm = pe.transpose(ps[4 * d + 3][:, 256 + hp * P:256 + hp * P + P], kh[:, d, hp, t], ident)
                                mm.then_inc(raw_mm, 1)
                            for v in range(1, RW_LEVELS):
                                for d in range(2):
                                    pe.wait_ge(inv_first, 2 * ((RW_LEVELS - 1) * i + v - 1) + d + 1)
                                    pe.wait_ge(off_ready, 2 * ((RW_LEVELS - 1) * i + v - 1) + d + 1)
                                    for h in range(HEADS):
                                        mm = pe.matmul(ps[4 * d][:, h * P:h * P + P], off[:, d, h, :], xz[:, 0, d, h, :],
                                                       start=True, stop=True)
                                    mm.then_inc(lx_mm, 1)
                                for d in range(2):
                                    pe.wait_ge(lx_ready, 2 * ((RW_LEVELS - 1) * i + v - 1) + d + 1)
                                    pe.wait_ge(inv_ready, 2 * (RW_LEVELS * i + v - 1) + d + 1)
                                    for h in range(HEADS):
                                        mm = pe.matmul(ps[4 * d + 1][:, h * P:h * P + P], xz[:, 1, d, h, :], wsb[:, d, h, :],
                                                       start=True, stop=True)
                                    if v < RW_LEVELS - 1:
                                        for h in range(HEADS):
                                            mm = pe.matmul(ps[4 * d + 2][:, h * P:h * P + P], wsb[:, d, h, :],
                                                           xz[:, 1, d, h, :], start=True, stop=True)
                                    mm.then_inc(xlx_mm, 1)
                            for d in range(2):
                                g = ORDER[d][i]
                                pe.wait_ge(inv_ready, 2 * (RW_LEVELS * i + RW_LEVELS - 1) + d + 1)
                                for h in range(HEADS):
                                    v = vt[:, g, 64 * h:64 * h + 64]
                                    pe.matmul(ps[4 * d][:, 64 * h:64 * h + 64], m4[:, d, h, 256:384], v, start=(h == 0),
                                              stop=True, skip_group_check=True)
                                    pe.matmul(ps[4 * d][:, 256 + 64 * h:256 + 64 * h + 64], m4[:, d, h, 384:512], v,
                                              start=False, stop=True, skip_group_check=True)
                            for s in range(2):
                                for d in range(2):
                                    lo = 64 * (s if d == 0 else 1 - s)
                                    t = slice(pcol(ORDER[d][i]) + lo, pcol(ORDER[d][i]) + lo + 64)
                                    if s == 1:
                                        pe.wait_ge(state_ready, 4 * i + d + 1)
                                    elif i == 1:
                                        pe.wait_ge(rw_loaded, 16 * l + 16)
                                    for part in range(2):
                                        for hp in range(2):
                                            o = 256 * part + hp * P
                                            mm = pe.matmul(ps[4 * d][lo:lo + 64, o:o + P], kr[:, d, hp, part, t],
                                                           st[:, d, min(i, 1), hp * P:hp * P + P], start=False, stop=True,
                                                           skip_group_check=True)
                                    mm.then_inc(r_mm, 1)
                                if i < GROUPS - 1:
                                    products(i + 1, 0, (2 + s,))
                                for d in range(2):
                                    lo = 64 * (s if d == 0 else 1 - s)
                                    pe.wait_ge(r_ready, 4 * i + 2 * s + d + 1)
                                    for h in range(HEADS):
                                        mm = pe.matmul(ps[4 * d + 1][lo:lo + 64, 64 * h:64 * h + 64],
                                                       xz[lo:lo + 64, 0, d, h, lo:lo + 64],
                                                       rsb[lo:lo + 64, d, 64 * h:64 * h + 64], start=True, stop=True)
                                    mm.then_inc(u_mm, 1)
                                if i < GROUPS - 1:
                                    products(i + 1, 1, (2 + s,))
                                for d in range(2):
                                    lo, g = 64 * (s if d == 0 else 1 - s), ORDER[d][i]
                                    pe.wait_ge(u_ready, 4 * i + 2 * s + d + 1)
                                    for h in range(HEADS):
                                        pe.matmul(ps[4 * d][:, 256 + 64 * h:256 + 64 * h + 64], m4[lo:lo + 64, d, h, P:2 * P],
                                                  usb[lo:lo + 64, d, 64 * h:64 * h + 64], start=False, stop=True,
                                                  skip_group_check=True)
                                    if i == 0 and s == 0:
                                        pe.wait_ge(bk_ready, d + 1)
                                    elif s == 0:
                                        pe.wait_ge(bk_ready, 2 * i + d + 1)
                                    for hp in range(2):
                                        o = slice(256 + hp * P, 256 + hp * P + P)
                                        pe.matmul(ps[4 * d + 1][:, o], bk[lo:lo + 64, d, hp * P:hp * P + P],
                                                  usb[lo:lo + 64, d, hp * P:hp * P + P], start=(hp == 0), stop=False,
                                                  skip_group_check=True)
                                        mm = pe.matmul(ps[4 * d + 1][:, o], bk[lo:lo + 64, d, 256 + hp * P:256 + hp * P + P],
                                                       vt[lo:lo + 64, g, hp * P:hp * P + P], start=False, stop=True,
                                                       skip_group_check=True)
                                    mm.then_inc(state_mm, 1)

                    def rwkv_gates():
                        for d in range(2):
                            for g in range(GROUPS):
                                t = slice(pcol(g), pcol(g) + P)
                                pe.matmul(ps[1 + 3 * d + g][:, 0:256], psh[:, d, t], g_up[:, d, :], start=True,
                                          stop=True).then_inc(gates_mm, 1)

                    def mix_out():
                        def turn(n):
                            k = OUT_ORDER[n]
                            if n >= 2:
                                pe.wait_ge(mix_read, n - 1)
                            elif n == 1:
                                pe.wait_ge(gates_out, 1)
                            for g in range(GROUPS):
                                mm = pe.transpose(ps[n % 2][:, g * P:g * P + P], mixed[:, g, k * P:k * P + P], ident)
                            mm.then_inc(mix_turned, 1)

                        for n in range(6):
                            turn(n)
                        for n in range(KT):
                            k = OUT_ORDER[n]
                            if n == 5:
                                pe.wait_ge(heads_out, 1)
                                turn(6)
                                turn(7)
                            pe.wait_ge(w_ready, UNITS["out"] + n + 1)
                            pe.wait_ge(mix_split, n + 1)
                            hi, lo = out_w_hi[n % HI_OUT], low_unit(FIRST["out"], n)
                            for g in range(GROUPS):
                                t = slice(g * P, g * P + P)
                                for h in range(2):
                                    c = slice(h * 512, h * 512 + 512)
                                    mm = three(ps[2 + 2 * g + h][:, :], (mixT_hi[:, k, t], mixT_lo[:, k, t]),
                                               (hi[:, c], lo[:, c]), n == 0, n == KT - 1,
                                               used if n % 2 == 0 and n > 0 and g == 0 and h == 0 else None)
                            if n < KT - 1:
                                mm.then_inc(out_mm, 1)
                        mm.then_inc(acc_done, 1)
                        pe.drain().then_inc(used, 1)

                    meet = Meeting(pe)
                    turn_x(0)
                    feed_forward(0)
                    modulation_rows(pe, 1, FIRST["ada1"])
                    pe.wait_ge(par_loaded, 16 * LAYER_DMAS * l + 16 * LAYER_DMAS)
                    turn_x(1)
                    project()
                    meet()
                    attention()
                    meet()
                    gla()
                    rwkv()
                    meet()
                    rwkv_units()
                    meet()
                    rwkv_gates()
                    mix_out()
                    modulation_rows(pe, 2, FIRST["ada2"])
                    turn_x(2)
                    feed_forward(2)
                    if not last:
                        modulation_rows(pe, NMIX, FIRST["ada3"])
                        gate_rows(pe, FIRST["ada3"], range(4 * KT))

                @block.scalar
                def _(sc):
                    own = Line(sc, line_s)

                    def round_unit(stretch, u, place, turn=0, du=0):
                        n = FIRST[stretch] + u // 2
                        if u % 2 == 0:
                            sc.wait_ge(arrived[n % RING], 16 * (n // RING + 1) + 16 * turn)
                        sc.activation(place, unit_of(FIRST[stretch], u), ACT.Copy).then_inc(w_rounded, 1)

                    def gates(j):
                        for c in range(2):
                            for n in range(2):
                                sc.wait_ge(gate_wide, 4 * j + 2 * c + n + 1)
                                sc.activation(gate[:, c, n * 512:n * 512 + 512], ps[4 + 2 * c + n][:, :], ACT.Copy,
                                              scale=1.0 if j == 1 else 0.5).then_inc(gate_ready, 1)

                    def turn_x(j):
                        full = mix_h_full if j == 1 else h_full
                        if j > 0:
                            sc.wait_ge(cond_ready, j)
                        if j == 2:
                            for u in range(2):
                                round_unit(f"ffn{j}", u, w_hi[:, u, :])
                        for k in range(1, KT, 2):
                            sc.wait_ge(turned, KT * j + k + 1)
                            sc.activation(full[:, k, 0:P], ps[1][:, 0:P], ACT.Identity, bias=cond[:, k, 0:1],
                                          scale=cond[:, 8 + k, 0:1])
                            sc.activation(full[:, k, P:TOK], ps[1][:, P:TOK], ACT.Identity, bias=cond[:, k, 1:2],
                                          scale=cond[:, 8 + k, 1:2]).then_inc(turn_odd, 1)
                        if j == 0:
                            for u in range(2):
                                round_unit(f"ffn{j}", u, w_hi[:, u, :])
                        for k in range(KT):
                            if k % 2 == 0:
                                sc.wait_ge(turn_even, 4 * j + k // 2 + 1)
                            else:
                                sc.wait_ge(turn_odd, 4 * j + k // 2 + 1)
                            sc.activation(h_hi[:, k, :], full[:, k, :], ACT.Copy).then_inc(h_rounded, 1)

                    def feed_forward(j):
                        i0 = FT * (j // 2)

                        def silu(b, i, first=False):
                            sc.wait_ge(gate_mm, i + 1)
                            if not first:
                                sc.wait_ge(act_ready, i)
                            sc.activation(sgt[:, b, :], ps[0][:, 0:TOK], ACT.Silu).then_inc(silu_done, 1)

                        for u in range(2, 5):
                            round_unit(f"ffn{j}", u, w_hi[:, u, :])
                        silu(0, i0, first=(i0 == 0))
                        gates(j)

                        def tile(f, r, last=False):
                            silu(f % 2, 4 * r + (i0 + f))
                            for u in range(3 * f + 2, 3 * f + (3 if last else 5)):
                                round_unit(f"ffn{j}", u, w_hi[:, u % HI_FFN, :], turn=r)

                        with sc.Fori(0, (FT - 2) // 4) as r:
                            for f in range(1, 5):
                                tile(f, r)
                        tile(FT - 1, 0, last=True)

                    def norm(j):
                        def root(g):
                            sc.wait_ge(stats_ready, GROUPS * j + g + 1)
                            sc.activation(ln_r[:, g, 0:1], ln_mv[:, g, 1:2], ACT.Sqrt,
                                          bias=eps_col[:, 0:1]).then_inc(std_ready, 1)

                        def normalise(g):
                            sc.wait_ge(rstd_ready, GROUPS * j + g + 1)
                            sc.activation(x[:, g, :], x[:, g, :], ACT.Identity, bias=ln_r[:, g, 2:3],
                                          scale=ln_r[:, g, 1:2]).then_inc(normed, 1)

                        root(0)
                        root(1)
                        normalise(0)
                        root(2)
                        normalise(1)
                        normalise(2)

                    def project():
                        def round_feat(f):
                            if f >= HI_PROJ:
                                sc.wait_ge(feat_mm, f - HI_PROJ + 2)
                            round_unit("feat", f, proj_w_hi[:, f % HI_PROJ, :])

                        def round_tokm(m):
                            if m < HI_PROJ:
                                sc.wait_ge(feat_mm, 2 * N_FEAT - HI_PROJ + m + 2)
                            elif m % 2 == 0:
                                sc.wait_ge(tokm_half, m // 2)
                            else:
                                sc.wait_ge(tokm_mm, GROUPS * (m // 2))
                            round_unit("tokm", m, proj_w_hi[:, m % HI_PROJ, :])

                        round_feat(0)
                        round_feat(1)
                        sc.wait_ge(feat_mm, 1)
                        sc.activation(adT[0:64, :], ps[0][0:64, 0:TOK], ACT.Copy).then_inc(feat_out, 1)
                        gates(1)
                        for i in range(2 * N_FEAT):
                            sc.wait_ge(feat_mm, i + 2)
                            if i + 2 < 2 * N_FEAT:
                                round_feat(i + 2)
                            else:
                                round_tokm(i + 2 - 2 * N_FEAT)
                            bank = ps[(i + 1) % 4]
                            if i < 10:
                                sc.activation(praw[:, i, 1:1 + P], bank[:, 0:P], ACT.Copy)
                                out = praw[:, i, pcol(1):pcol(1) + LAT]
                                src, scale = bank[:, P:TOK], 1.0
                            elif i < 12:
                                out, src, scale = (qg, bank[:, 0:TOK], GLA_DK ** -0.5) if i == 10 else (kg, bank[:, 0:TOK], 1.0)
                            elif i < 20:
                                out, src, scale = (qd if i < 16 else kd)[:, i % 4, :], bank[:, 0:TOK], 1.0
                            sc.activation(out, src, ACT.Copy, scale=scale).then_inc(feat_out, 1)
                        for u in range(GROUPS * N_TOKM):
                            q, g = u // GROUPS, u % GROUPS
                            if g == 0 and q < N_TOKM - 1:
                                round_tokm(2 * q + 2)
                            sc.wait_ge(tokm_mm, u + 1)
                            if g == 2 and q < N_TOKM - 1:
                                round_tokm(2 * q + 3)
                            out = vg[:, g, :] if q == 0 else gd[:, q - 1, g, :] if q < 3 else \
                                vd[:, g, (q - 3) * 256:(q - 3) * 256 + 256]
                            sc.activation(out, ps[(2 if q % 2 else 5) + g][:, 0:256], ACT.Copy).then_inc(tokm_out, 1)

                    def attention():
                        sc.dma_start(k_out[l], kd[:, :, 0:P]).then_inc(stored, 16)
                        sc.dma_start(v_out[l], vd[:, 0, :]).then_inc(stored, 16)
                        sc.wait_ge(lam_dots, 1)
                        sc.activation(lam4[:, 2:4], lam4[:, 0:2], ACT.Exp).then_inc(lam_exp, 1)
                        for d in range(2):
                            sc.wait_ge(gla_log_mm, d + 1)
                            sc.activation(gz[:, :, d * P:d * P + P], ps[4 + d][:, 0:TOK].rearrange("p (g t) -> p g t", g=GROUPS),
                                          ACT.Identity, bias=prm("gla_b")[:, d:d + 1]).then_inc(gla_log_read, 1)
                        sc.wait_ge(gla_log_read, 2)
                        own.link(sc.activation(ge, gz, ACT.Abs))
                        own.link(sc.activation(ge, ge, ACT.Exp, scale=-1.0))
                        sc.activation(ge, ge, ACT.Ln, bias=1.0).then_inc(gla_log_abs, 1)

                        def exponents(u):
                            n = P if u < HEADS else TOK
                            sc.wait_ge(max_ready, u + 1)
                            if u >= 2:
                                sc.wait_ge(weights_ready, u - 1)
                            for c in range(2):
                                ins = sc.activation(e_sb[:, u % 2, c, 0:n], ps[2 * (u % 3) + c][:, 0:n], ACT.Exp,
                                                    bias=att_max[:, u % 2, c:c + 1], scale=DIFF_D ** -0.5,
                                                    accum_out=att_sum[:, u, c:c + 1])
                            ins.then_inc(exp_done, 1)

                        def weights_out(u):
                            n = P if u < HEADS else TOK
                            sc.wait_ge(weights_turned, u + 1)
                            if u >= 2:
                                sc.wait_ge(att_mm, u - 1)
                            sc.activation(attT[:, u % 2, 0:n], ps[6][:, 0:n], ACT.Copy).then_inc(weightsT_ready, 1)

                        def outputs(u):
                            g, h = u // HEADS, u % HEADS
                            sc.wait_ge(att_mm, u + 1)
                            own.link(sc.activation(squares_tmp, ps[7][:, 0:P], ACT.Square,
                                                   accum_out=diff_ss[:, u:u + 1]))
                            sc.activation(mixed[:, g, 512 + h * P:512 + h * P + P], ps[7][:, 0:P],
                                          ACT.Copy).then_inc(att_out, 1)

                        for i in range(GROUPS * HEADS + 3):
                            if i < GROUPS * HEADS:
                                exponents(i)
                            if 2 <= i < GROUPS * HEADS + 2:
                                weights_out(i - 2)
                            if i >= 3:
                                outputs(i - 3)
                        sc.wait_ge(stored, 32)

                    def gla():
                        for u in range(2 * GLA_LEVELS):
                            b = u % 2
                            sc.wait_ge(gla_dist, u + 1)
                            if u % GLA_LEVELS < GLA_LEVELS - 1:
                                own.link(sc.activation(g_exp[:, b, 0, :], g_dist[:, b, :], ACT.Abs))
                                sc.activation(g_exp[:, b, 0, :], g_exp[:, b, 0, :], ACT.Exp,
                                              scale=-1.0 / GLA_TAU).then_inc(gla_exp, 1)
                            else:
                                sc.activation(g_exp[:, b, 0, :], g_dist[:, b, :], ACT.Exp, scale=1.0 / GLA_TAU)
                                sc.activation(g_exp[:, b, 1, :], g_dist[:, b, :], ACT.Exp,
                                              scale=-1.0 / GLA_TAU).then_inc(gla_exp, 1)
                        sc.wait_ge(att_var, 1)
                        sc.activation(diff_ss, diff_ss, ACT.Sqrt).then_inc(att_std, 1)
                        for d in range(2):
                            sc.activation(psh[0:64, 8 + d, WIN], psh[0:64, 8 + d, WIN], ACT.Tanh).then_inc(lora_in, 1)
                        for d in range(2):
                            sc.activation(psh[:, d, WIN], psh[:, d, WIN], ACT.Sigmoid)
                        for d in range(2):
                            sc.wait_ge(gla_last, d + 1)
                            sc.activation(g_e0[:, d, :], gb[:, d, :], ACT.Exp, scale=1.0 / GLA_TAU)
                            sc.activation(g_kl[:, d, :], g_kl[:, d, :], ACT.Exp, scale=1.0 / GLA_TAU).then_inc(gla_last_exp, 1)
                        for d in range(2):
                            sc.wait_ge(gla_keys_mm, d + 1)
                            sc.activation(g_klt[:, d, :], ps[6 + d][:, 0:TOK], ACT.Copy).then_inc(gla_keysT, 1)
                        for i in range(GROUPS):
                            for d in range(2):
                                sc.wait_ge(gla_out_mm, 2 * i + d + 1)
                                sc.activation(g_o[:, d, ORDER[d][i], :], ps[2 * (i % 2) + d][:, 0:GLA_W],
                                              ACT.Copy).then_inc(gla_out_read, 1)
                        sc.activation(gd[:, :, :, :], gd[:, :, :, :], ACT.Silu).then_inc(gla_silu, 1)
                        sc.wait_ge(gla_state, 2)
                        sc.dma_start(gla_out[l], g_st[:, :, 0, :]).then_inc(stored, 16)
                        sc.wait_ge(gla_var, 1)
                        sc.activation(gla_ss, gla_ss, ACT.Sqrt).then_inc(gla_std, 1)

                    def rwkv():
                        def rates(d):
                            sc.wait_ge(lora_mm, d + 1)
                            if d == 1:
                                sc.wait_ge(decay_used, 1)
                                sc.wait_ge(rate_kk, 1)
                            for i in range(2):
                                sc.activation(sw[:, i, WIN], ps[4 * d + 2 * i][:, 0:WPAD - 2], ACT.Sigmoid,
                                              bias=w0[:, d, i:i + 1])
                                ins = sc.activation(sa[:, i, WIN], ps[4 * d + 2 * i + 1][:, 0:WPAD - 2], ACT.Sigmoid,
                                                    bias=a0[:, d, i:i + 1])
                            ins.then_inc(rates_ready, 1)

                        sc.wait_ge(norm_sq, 1)
                        sc.activation(pp[:, :, WIN], pp[:, :, WIN], ACT.Sqrt).then_inc(norm_root, 1)
                        rates(0)
                        sc.wait_ge(values_mm, 1)
                        for g in range(GROUPS):
                            ins = sc.activation(vt[:, g, :], ps[6 + g // 2][:, g % 2 * 256:g % 2 * 256 + 256], ACT.Copy)
                        ins.then_inc(values_out, 1)
                        for d in range(2):
                            if d == 1:
                                rates(1)
                            sc.wait_ge(cum_ready, d + 1)
                            own.link(sc.activation(sw[:, :, WIN], sw[:, :, WIN], ACT.Exp, scale=DECAY))
                            if d == 0:
                                sc.wait_ge(kk_ready, 1)
                            own.link(sc.activation(pp[:, :, WIN], cs[:, :, WIN], ACT.Exp, scale=DECAY))
                            sc.activation(cs[:, :, WIN], cs[:, :, WIN], ACT.Exp, scale=-DECAY).then_inc(decay_exp, 1)
                        sc.wait_ge(stored, 48)

                    def rwkv_units():
                        for i in range(GROUPS):
                            for d in range(2):
                                sc.wait_ge(raw_mm, 2 * i + d + 1)
                                sc.activation(bk[:, d, :], ps[4 * d + 3][:, :], ACT.Copy).then_inc(bk_ready, 1)
                            for v in range(1, RW_LEVELS):
                                for d in range(2):
                                    sc.wait_ge(lx_mm, 2 * ((RW_LEVELS - 1) * i + v - 1) + d + 1)
                                    sc.activation(wsb[:, d, :, :], ps[4 * d][:, :], ACT.Copy).then_inc(lx_ready, 1)

                    def rwkv_gates():
                        sc.dma_start(rw_out[l], st[:, :, 0, :]).then_inc(stored, 16)
                        for d in range(2):
                            for g in range(GROUPS):
                                sc.wait_ge(gates_mm, GROUPS * d + g + 1)
                                ins = sc.activation(ggate[:, d, g, :], ps[1 + 3 * d + g][:, 0:256], ACT.Copy)
                        ins.then_inc(gates_out, 1)

                    def mix_out():
                        def turn(n):
                            sc.wait_ge(mix_turned, n + 1)
                            sc.activation(mixT[:, OUT_ORDER[n], :], ps[n % 2][:, 0:TOK], ACT.Copy).then_inc(mix_read, 1)

                        def high(n):
                            k = OUT_ORDER[n]
                            sc.wait_ge(mix_read, n + 1)
                            sc.activation(mixT_hi[:, k, :], mixT[:, k, :], ACT.Copy).then_inc(mix_rounded, 1)

                        def weight(m):
                            if m >= HI_OUT:
                                sc.wait_ge(out_mm, m - HI_OUT + 1)
                            round_unit("out", m, out_w_hi[m % HI_OUT])

                        weight(0)
                        for n in range(0, 6, 2):
                            turn(n)
                            turn(n + 1)
                            high(n)
                            high(n + 1)
                        weight(1)
                        sc.wait_ge(rw_var, 1)
                        sc.activation(gn_var, gn_var, ACT.Sqrt).then_inc(rw_std, 1)
                        for m in range(2, 6):
                            weight(m)
                        for n in range(6, KT):
                            turn(n)
                        for n in range(6, KT):
                            high(n)
                            weight(n)
                        sc.wait_ge(stored, 64)

                    meet = Meeting(sc)
                    turn_x(0)
                    feed_forward(0)
                    norm(0)
                    modulation_copies(sc, 1)
                    turn_x(1)
                    project()
                    meet()
                    attention()
                    meet()
                    gla()
                    rwkv()
                    meet()
                    rwkv_units()
                    meet()
                    rwkv_gates()
                    mix_out()
                    norm(1)
                    modulation_copies(sc, 2)
                    turn_x(2)
                    feed_forward(2)
                    norm(2)
                    if not last:
                        modulation_copies(sc, NMIX)

                @block.vector
                def _(ve):
                    own = Line(ve, line_v)

                    def rest_unit(stretch, u, place, du=0):
                        ve.wait_ge(w_rounded, du + (UNITS[stretch] + u + 1))
                        raw = unit_of(FIRST[stretch], u)
                        ve.tensor_tensor(low_unit(FIRST[stretch], u), raw, place.bitcast(F32), ALU.subtract).then_inc(w_ready, 1)

                    def turn_x(j):
                        if j > 0:
                            ve.wait_ge(cond_ready, j)
                        full, low = (mix_h_full, mix_h_lo) if j == 1 else (h_full, h_lo)
                        if j == 2:
                            for u in range(2):
                                rest_unit(f"ffn{j}", u, w_hi[:, u, :])
                        for k in range(0, KT, 2):
                            ve.wait_ge(turned, KT * j + k + 1)
                            ve.tensor_scalar(full[:, k, 0:P], ps[7][:, 0:P], cond[:, 8 + k, 0:1], cond[:, k, 0:1],
                                             ALU.mult, ALU.add)
                            ve.tensor_scalar(full[:, k, P:TOK], ps[7][:, P:TOK], cond[:, 8 + k, 1:2], cond[:, k, 1:2],
                                             ALU.mult, ALU.add).then_inc(turn_even, 1)
                        if j == 0:
                            for u in range(2):
                                rest_unit(f"ffn{j}", u, w_hi[:, u, :])
                        for k in range(KT):
                            ve.wait_ge(h_rounded, KT * j + k + 1)
                            ve.tensor_tensor(low[:, k, :], full[:, k, :], h_hi[:, k, :].bitcast(F32),
                                             ALU.subtract).then_inc(h_ready, 1)
                        if j > 0:
                            gate_sums(ve, j, l)

                    def feed_forward(j):
                        i0 = FT * (j // 2)

                        def product(b, i):
                            ve.wait_ge(silu_done, i + 1)
                            ve.wait_ge(up_mm, i + 1)
                            ve.tensor_tensor(act[:, b, :], sgt[:, b, :], ps[1][:, 0:TOK], ALU.mult).then_inc(act_ready, 1)
                            ve.wait_ge(act_ready, i + 1)
                            ve.tensor_copy(act_hi[:, b, :], act[:, b, :]).then_inc(act_rounded, 1)
                            ve.wait_ge(act_rounded, i + 1)
                            ve.tensor_tensor(act_lo[:, b, :], act[:, b, :], act_hi[:, b, :].bitcast(F32),
                                             ALU.subtract).then_inc(act_split, 1)

                        for u in range(2, 5):
                            rest_unit(f"ffn{j}", u, w_hi[:, u, :])
                        product(0, i0)
                        with ve.Fori(0, (FT - 2) // 4) as r:
                            for f in range(1, 5):
                                for u in range(3 * f + 2, 3 * f + 5):
                                    rest_unit(f"ffn{j}", u, w_hi[:, u % HI_FFN, :], du=12 * r)
                                product(f % 2, 4 * r + (i0 + f))
                        rest_unit(f"ffn{j}", FFN_UNITS - 1, w_hi[:, (FFN_UNITS - 1) % HI_FFN, :])
                        product((FT - 1) % 2, i0 + FT - 1)

                    def norm(j):
                        def stats(g):
                            for n in range(2):
                                ins = ve.tensor_tensor(res_tmp[:, g, n * 512:n * 512 + 512], ps[2 + 2 * g + n][:, :],
                                                       gate[:, min(g, 1), n * 512:n * 512 + 512], ALU.mult)
                            if g == GROUPS - 1:
                                ins.then_inc(acc_read, 1)
                                ve.wait_ge(acc_read, j + 1)
                            else:
                                own.link(ins)
                            own.link(ve.scalar_tensor_tensor(x[:, g, :], x[:, g, :], ALPHA, res_tmp[:, g, :], ALU.mult,
                                                             ALU.add))
                            for n in range(2):
                                own.step(ve.bn_stats(ln_stat[:, g, 6 * n:6 * n + 6], x[:, g, n * 512:n * 512 + 512]))
                            own.settle()
                            ve.bn_aggr(ln_mv[:, g, :], ln_stat[:, g, :]).then_inc(stats_ready, 1)

                        def scale(g):
                            ve.wait_ge(std_ready, GROUPS * j + g + 1)
                            own.link(ve.reciprocal(ln_r[:, g, 1:2], ln_r[:, g, 0:1]))
                            ve.scalar_tensor_tensor(ln_r[:, g, 2:3], ln_mv[:, g, 0:1], -1.0, ln_r[:, g, 1:2], ALU.mult,
                                                    ALU.mult).then_inc(rstd_ready, 1)

                        def gain(g):
                            ve.wait_ge(normed, GROUPS * j + g + 1)
                            ve.tensor_tensor(x[:, g, :], x[:, g, :], lnrow[:, 0, :], ALU.mult).then_inc(scaled, 1)

                        ve.wait_ge(acc_done, j + 1)
                        stats(0)
                        stats(1)
                        scale(0)
                        stats(2)
                        scale(1)
                        ve.wait_ge(lnrow_loaded, 16 * NMIX * l + 16 * (j + 1))
                        gain(0)
                        scale(2)
                        gain(1)
                        gain(2)
                        ve.wait_ge(scaled, GROUPS * (j + 1))
                        ve.tensor_tensor(x[:, 2, :], x[:, 2, :], lnrow[:, 1, :], ALU.add).then_inc(x_last_ready, 1)

                    def project():
                        own.link(ve.tensor_tensor(c0, mu[:, 0, :], mu[:, 1, :], ALU.add))
                        own.step(ve.tensor_scalar(c0, c0, -1.0, 1.0, ALU.mult, ALU.add))
                        for col in (0, P + 1, WPAD - 1):
                            own.step(ve.memset(praw[:, :, col:col + 1], 0.0))
                        own.settle()
                        rest_unit("feat", 0, proj_w_hi[:, 0, :])
                        rest_unit("feat", 1, proj_w_hi[:, 1, :])
                        for i in range(10):
                            out = psh[:, PSH[i], WIN]
                            rest_unit("feat", i + 2, proj_w_hi[:, i % HI_PROJ, :])
                            ve.wait_ge(feat_out, i + 2)
                            own.link(ve.tensor_scalar(out, praw[:, i, WIN], c0[:, i:i + 1], None, ALU.mult))
                            own.link(ve.scalar_tensor_tensor(out, praw[:, i, 0:WPAD - 2], mu[:, 0, i:i + 1], out,
                                                             ALU.mult, ALU.add))
                            own.link(ve.scalar_tensor_tensor(out, praw[:, i, 2:WPAD], mu[:, 1, i:i + 1], out,
                                                             ALU.mult, ALU.add))
                        for f in range(12, 2 * N_FEAT):
                            rest_unit("feat", f, proj_w_hi[:, f % HI_PROJ, :])
                        for m in range(2 * N_TOKM):
                            rest_unit("tokm", m, proj_w_hi[:, m % HI_PROJ, :])

                    def attention():
                        lam = row("lam").rearrange("p (m s n) -> p m s n", m=2, s=2)
                        prod = rope_tmp[:, 0, 0:P].rearrange("p (m n) -> p m n", m=2)
                        own.link(ve.tensor_tensor(prod, lam[:, :, 0, :], lam[:, :, 1, :], ALU.mult))
                        ve.tensor_reduce(lam4[:, 0:2], prod, AX, ALU.add).then_inc(lam_dots, 1)
                        ve.wait_ge(lam_exp, 1)
                        own.step(ve.scalar_tensor_tensor(neg_lam, lam4[:, 3:4], prm("lam_init")[:, 0:1], lam4[:, 2:3],
                                                         ALU.subtract, ALU.subtract))
                        own.step(ve.tensor_scalar(diff_gn, row("diff_g"), prm("lam_init")[:, 1:2], None, ALU.mult))
                        own.settle()
                        def rope(p):
                            part = (qd if p < 2 else kd)[:, 2 * (p % 2):2 * (p % 2) + 2, P:TOK]
                            cos, sin = (con(n).unsqueeze(1).to_broadcast([P, 2, LAT]) for n in ("rope_cos", "rope_sin"))
                            ve.wait_ge(rope_mm, p + 1)
                            own.step(ve.tensor_tensor(rope_tmp, ps[ROPE_BANK[p]][:, :].rearrange("p (h t) -> p h t", h=2), sin,
                                                      ALU.mult))
                            own.link(ve.tensor_tensor(part, part, cos, ALU.mult))
                            ve.tensor_tensor(part, part, rope_tmp, ALU.add).then_inc(rope_done, 1)
                            ve.wait_ge(rope_done, p + 1)

                        def maxima(u):
                            n = P if u < HEADS else TOK
                            ve.wait_ge(scores_mm, u + 1)
                            if u >= 2:
                                ve.wait_ge(exp_done, u - 1)
                            for c in range(2):
                                own.step(ve.tensor_reduce(att_max[:, u % 2, c:c + 1], ps[2 * (u % 3) + c][:, 0:n], AX, ALU.max))
                            own.settle()
                            ve.tensor_scalar(att_max[:, u % 2, :], att_max[:, u % 2, :], -DIFF_D ** -0.5, None,
                                             ALU.mult).then_inc(max_ready, 1)

                        def weights(u):
                            n, b = P if u < HEADS else TOK, u % 2
                            ve.wait_ge(exp_done, u + 1)
                            own.link(ve.reciprocal(att_r[:, b, :], att_sum[:, u, :]))
                            own.link(ve.tensor_scalar(att_r[:, b, 1:2], att_r[:, b, 1:2], neg_lam, None, ALU.mult))
                            if u >= 2:
                                ve.wait_ge(weights_turned, u - 1)
                            own.link(ve.tensor_scalar(att[:, b, 0:n], e_sb[:, b, 0, 0:n], att_r[:, b, 0:1], None, ALU.mult))
                            ve.scalar_tensor_tensor(att[:, b, 0:n], e_sb[:, b, 1, 0:n], att_r[:, b, 1:2], att[:, b, 0:n],
                                                    ALU.mult, ALU.add).then_inc(weights_ready, 1)

                        for i in range(GROUPS * HEADS + 1):
                            if i < 4:
                                rope(i)
                            if i < GROUPS * HEADS:
                                maxima(i)
                            if i >= 1:
                                weights(i - 1)
                    def gla():
                        ve.wait_ge(gla_log_abs, 1)
                        own.link(ve.scalar_tensor_tensor(gz, gz, 0.0, ge, ALU.min, ALU.subtract))
                        for d in range(2):
                            for g in range(GROUPS):
                                t = slice(g * P, g * P + P)
                                a, b, keep = gb[:, d, t], gz[:, g, d * P:d * P + P], gla_keep[:, d, t]
                                if d == 1:
                                    a, b, keep = a[:, ::-1], b[:, ::-1], keep[:, ::-1]
                                own.step(ve.tensor_tensor_scan(a, keep, b, 0.0, ALU.mult, ALU.add))
                            own.settle()

                        def distance(u):
                            d, v = u // GLA_LEVELS, u % GLA_LEVELS
                            if v < GLA_LEVELS - 1:
                                width, at = 2 * GLA_HALVES[v], GLA_HALVES[v] - 1 + d
                            else:
                                width, at = GLA_BASE, max(GLA_BASE // 2 - 1 + d, 0)
                            b = gb[:, d, :].rearrange("p (n w) -> p n w", w=width)
                            out = g_dist[:, u % 2, :].rearrange("p (n w) -> p n w", w=width)
                            ins = ve.tensor_tensor(out, b, b[:, :, at:at + 1].to_broadcast([P, TOK // width, width]),
                                                   ALU.subtract)
                            if v == GLA_LEVELS - 1:
                                own.link(ins)
                                ins = ve.tensor_scalar(g_dist[:, u % 2, :], g_dist[:, u % 2, :], -GLA_CLAMP * GLA_TAU,
                                                       GLA_CLAMP * GLA_TAU, ALU.max, ALU.min)
                            ins.then_inc(gla_dist, 1)

                        def scale(u):
                            b, last = u % 2, u % GLA_LEVELS == GLA_LEVELS - 1
                            ve.wait_ge(gla_exp, u + 1)
                            if u >= 2:
                                ve.wait_ge(gla_att_mm, u - 1)
                            ve.tensor_tensor(g_qk[:, b, 0, :], qg, g_exp[:, b, 0, :], ALU.mult)
                            ve.tensor_tensor(g_qk[:, b, 1, :], kg, g_exp[:, b, 1 if last else 0, :],
                                             ALU.mult).then_inc(gla_scaled, 1)

                        def read(u):
                            d, v = u // GLA_LEVELS, u % GLA_LEVELS
                            mask = gla_base[:, d, :] if v == GLA_LEVELS - 1 else halves[:, 1 - d, GLA_HALVES[v].bit_length() - 1, :]
                            mask = mask.bitcast(I32).unsqueeze(1).to_broadcast([P, GROUPS, P])
                            if u == 0:
                                ve.wait_ge(gla_cleared, 1)
                            ve.wait_ge(gla_att_mm, u + 1)
                            for h in range(HEADS):
                                own.step(ve.copy_predicated(g_att[:, d, h, :].rearrange("p (g t) -> p g t", g=GROUPS), mask,
                                                            ps[4 * (u % 2) + h][:, 0:TOK].rearrange("p (g t) -> p g t", g=GROUPS)))
                            own.settle()
                            ve.sem_inc(gla_att_read, 1)

                        n = 2 * GLA_LEVELS
                        ve.tensor_scalar(diff_ss, diff_ss, 1.0 / P, NORM_EPS, ALU.mult, ALU.add).then_inc(att_var, 1)
                        distance(0)
                        for u in range(n + 1):
                            if u + 1 < n:
                                distance(u + 1)
                            if u < n:
                                scale(u)
                            if u >= 1:
                                read(u - 1)
                        for d in range(2):
                            b = gb[:, d, :].rearrange("p (g t) -> p g t", g=GROUPS)
                            last = b[:, :, P - 1:P] if d == 0 else b[:, :, 0:1]
                            ve.tensor_tensor(g_kl[:, d, :].rearrange("p (g t) -> p g t", g=GROUPS),
                                             last.to_broadcast([P, GROUPS, P]), b, ALU.subtract).then_inc(gla_last, 1)
                        for d in range(2):
                            ve.wait_ge(gla_last_exp, d + 1)
                            ve.tensor_tensor(g_q0[:, d, :], qg, g_e0[:, d, :], ALU.mult)
                            ve.tensor_tensor(g_kl[:, d, :], kg, g_kl[:, d, :], ALU.mult).then_inc(gla_keys, 1)
                        ve.wait_ge(att_std, 1)
                        own.link(ve.reciprocal(diff_ss, diff_ss))
                        for u in range(GROUPS * HEADS):
                            part = mixed[:, u // HEADS, 512 + (u % HEADS) * P:512 + (u % HEADS) * P + P]
                            own.step(ve.scalar_tensor_tensor(part, part, diff_ss[:, u:u + 1], diff_gn, ALU.mult, ALU.mult))
                        for i in range(2):
                            for d in range(2):
                                ve.wait_ge(gla_state_mm, 2 * i + d + 1)
                                if i == 0:
                                    ve.tensor_tensor(g_st[:, d, 0, :], ps[4 + d][:, 0:GLA_W], con("gla_blk"),
                                                     ALU.mult).then_inc(gla_state, 1)
                                else:
                                    end = P * ORDER[d][i] + (P - 1 if d == 0 else 0)
                                    own.link(ve.tensor_tensor(g_sq[:, d, 0, :], ps[4 + d][:, 0:GLA_W], con("gla_blk"), ALU.mult))
                                    ve.scalar_tensor_tensor(g_st[:, d, 1, :], g_st[:, d, 1, :], g_e0[:, d, end:end + 1],
                                                            g_sq[:, d, 0, :], ALU.mult, ALU.add).then_inc(gla_state, 1)
                        ve.wait_ge(gla_out_read, 2 * GROUPS)
                        ve.wait_ge(gla_state, 4)
                        own.step(ve.tensor_scalar(ka1, prm("k_a"), -1.0, 1.0, ALU.mult, ALU.add))
                        for i in range(2):
                            own.step(ve.tensor_scalar(kn[:, i, WIN], psh[:, 4 + i, WIN], prm("k_k")[:, i:i + 1], None, ALU.mult))
                        own.settle()
                        ve.tensor_tensor(kk[:, :, WIN], kn[:, :, WIN], kn[:, :, WIN], ALU.mult).then_inc(squares, 1)
                        own.link(ve.tensor_tensor(g_sq[:, :, :, :], g_o[:, :, :, :], g_o[:, :, :, :], ALU.mult))
                        heads = [P, 2 * GROUPS * HEADS, 64]
                        o = g_o[:, :, :, :].rearrange("p d g (h n) -> p (d g h) n", h=HEADS)
                        sq = g_sq[:, :, :, :].rearrange("p d g (h n) -> p (d g h) n", h=HEADS)
                        own.link(ve.tensor_reduce(gla_ss, sq, AX, ALU.add))
                        ve.tensor_scalar(gla_ss, gla_ss, 1.0 / 64, NORM_EPS, ALU.mult, ALU.add).then_inc(gla_var, 1)
                        ve.wait_ge(norm_mm, 1)
                        for i in range(2):
                            ins = ve.tensor_scalar(pp[:, i, WIN], ps[4 + i][:, 0:WPAD - 2], 1e-24, None, ALU.max)
                        ins.then_inc(norm_sq, 1)
                        ve.wait_ge(gla_std, 1)
                        own.link(ve.reciprocal(gla_ss, gla_ss))
                        own.link(ve.tensor_tensor(o, o, gla_ss.unsqueeze(2).to_broadcast(heads), ALU.mult))
                        own.link(ve.tensor_tensor(o, o, row("gla_g").unsqueeze(1).to_broadcast(heads), ALU.mult))
                        ve.wait_ge(gla_silu, 1)
                        own.link(ve.tensor_tensor(g_o[:, :, :, :], g_o[:, :, :, :], gd[:, :, :, :], ALU.mult))
                        own.link(ve.tensor_tensor(mixed[:, :, 256:512], g_o[:, 0, :, :], g_o[:, 1, :, :], ALU.add))

                    def rwkv():
                        ve.wait_ge(norm_root, 1)
                        own.link(ve.reciprocal(pp[:, :, WIN], pp[:, :, WIN]))
                        ve.tensor_tensor(kk[:, :, WIN], kn[:, :, WIN], pp[:, :, WIN], ALU.mult).then_inc(kk_ready, 1)
                        ve.wait_ge(kk_ready, 1)
                        k_, r_ = psh[:, 4:6, WIN], psh[:, 2:4, WIN]
                        for d in range(2):
                            ve.wait_ge(rates_ready, d + 1)
                            for i in range(2):
                                a, b, keep = cs[:, i, WIN], sw[:, i, WIN], rw_keep[:, d, WIN]
                                if d == 1:
                                    a, b, keep = a[:, ::-1], b[:, ::-1], keep[:, ::-1]
                                own.step(ve.tensor_tensor_scan(a, keep, b, 0.0, ALU.mult, ALU.add))
                            own.settle()
                            ve.tensor_tensor(sw[:, :, WIN], cs[:, :, WIN], sw[:, :, WIN], ALU.subtract).then_inc(cum_ready, 1)
                            if d == 1:
                                ve.wait_ge(bonus_in, 1)
                            for i in range(2):
                                own.step(ve.tensor_scalar(kn[:, i, WIN], sa[:, i, WIN], prm("k_a")[:, i:i + 1], ka1[:, i:i + 1],
                                                          ALU.mult, ALU.add))
                            own.settle()
                            ve.tensor_tensor(kn[:, :, WIN], kn[:, :, WIN], k_, ALU.mult).then_inc(keys_ready, 1)
                            ve.wait_ge(keys_ready, d + 1)
                            ve.wait_ge(decay_exp, d + 1)
                            own.step(ve.tensor_tensor(kr[:, d, :, 0, WIN], kk[:, :, WIN], sw[:, :, WIN], ALU.mult))
                            own.step(ve.tensor_tensor(kh[:, d, :, WIN], kn[:, :, WIN], cs[:, :, WIN], ALU.mult))
                            ve.wait_ge(rate_kk, d + 1)
                            own.step(ve.tensor_tensor(be[:, d, :, WIN], be[:, d, :, WIN], cs[:, :, WIN], ALU.mult))
                            own.step(ve.tensor_tensor(kr[:, d, :, 1, WIN], r_, pp[:, :, WIN], ALU.mult))
                            for g in range(GROUPS):
                                first = pcol(g) + (CHUNK - 1 if d == 0 else 0)
                                ins = ve.tensor_copy(pend[:, d, :, 2 * g:2 * g + 2], pp[:, :, first:first + CHUNK + 1:CHUNK])
                            ins.then_inc(decay_used, 1)
                        for d in range(2):
                            ve.wait_ge(bonus_mm, d + 1)
                            own.link(ve.tensor_copy(bonus[:, 12 * d:12 * d + 12], ps[4 + d][:, 0:12]))

                    def rwkv_units():
                        for i in range(GROUPS):
                            for d in range(2):
                                ve.wait_ge(prod_mm, 2 * i + d + 1)
                                mask = rw_mask[:, d, :].unsqueeze(1).to_broadcast([P, 2, 256])
                                for h in range(HEADS):
                                    own.step(ve.tensor_tensor(m4[:, d, h, :].rearrange("p (s n) -> p s n", s=2),
                                                              ps[4 * d + h][:, :].rearrange("p (s n) -> p s n", s=2), mask,
                                                              ALU.mult))
                                own.settle()
                                ve.sem_inc(prod_ready, 1)
                            for d in range(2):
                                ve.wait_ge(raw_mm, 2 * i + d + 1)
                                for h in range(2):
                                    own.step(ve.tensor_copy(am[:, d, h::2, :], ps[4 * d + h][:, 0:256].rearrange(
                                        "p (h n) -> p h n", h=2)))
                                own.settle()
                                wide = [P, HEADS, P]
                                m0 = halves[:, d, 0, :].unsqueeze(1).to_broadcast(wide)
                                m0t = halves[:, 1 - d, 0, :].unsqueeze(1).to_broadcast(wide)
                                one = ident.unsqueeze(1).to_broadcast(wide)
                                own.step(ve.tensor_tensor(xz[:, 0, d, :, :], m4[:, d, :, 0:P], m0t, ALU.mult))
                                own.step(ve.tensor_tensor(xz[:, 1, d, :, :], am[:, d, :, :], m0, ALU.mult))
                                own.settle()
                                ve.tensor_tensor(xz[:, 0, d, :, :], one, xz[:, 0, d, :, :],
                                                 ALU.subtract).then_inc(inv_first, 1)
                                ve.tensor_tensor(xz[:, 1, d, :, :], one, xz[:, 1, d, :, :], ALU.subtract).then_inc(inv_ready, 1)
                            for v in range(1, RW_LEVELS):
                                for d in range(2):
                                    ve.wait_ge(inv_ready, 2 * (RW_LEVELS * i + v - 1) + d + 1)
                                    ve.wait_ge(xlx_mm, 2 * ((RW_LEVELS - 1) * i + v - 1) + d + 1)
                                    n = 2 if v < RW_LEVELS - 1 else 1
                                    for s in range(n):
                                        ins = ve.tensor_tensor(xz[:, s, d, :, :], xz[:, s, d, :, :],
                                                               ps[4 * d + 1 + s][:, :].rearrange("p (h n) -> p h n", h=HEADS),
                                                               ALU.subtract)
                                        ins.then_inc(inv_first if s < n - 1 else inv_ready, 1)
                            for s in range(2):
                                for d in range(2):
                                    lo = 64 * (s if d == 0 else 1 - s)
                                    ve.wait_ge(r_mm, 4 * i + 2 * s + d + 1)
                                    ve.tensor_copy(rsb[lo:lo + 64, d, :], ps[4 * d][lo:lo + 64, 0:256]).then_inc(r_ready, 1)
                                for d in range(2):
                                    lo = 64 * (s if d == 0 else 1 - s)
                                    ve.wait_ge(u_mm, 4 * i + 2 * s + d + 1)
                                    ve.tensor_scalar(usb[lo:lo + 64, d, :], ps[4 * d + 1][lo:lo + 64, 0:256], -1.0, None,
                                                     ALU.mult).then_inc(u_ready, 1)
                                for d in range(2):
                                    c = s if d == 0 else 1 - s
                                    g = ORDER[d][i]
                                    state = st[:, d, min(i, 1), :]
                                    ve.wait_ge(state_mm, 4 * i + 2 * s + d + 1)
                                    blk = con("ones_blk").unsqueeze(1).to_broadcast([P, 2, P])
                                    own.link(ve.tensor_tensor(stmp[:, d, :].rearrange("p (i n) -> p i n", i=2),
                                                              ps[4 * d + 1][:, 256:512].rearrange("p (i n) -> p i n", i=2),
                                                              blk, ALU.mult))
                                    own.link(ve.tensor_tensor(stmp[:, d, :], stmp[:, d, :], state, ALU.add))
                                    for hp in range(2):
                                        own.step(ve.tensor_scalar(state[:, hp * P:hp * P + P], stmp[:, d, hp * P:hp * P + P],
                                                                  pend[:, d, hp, 2 * g + c:2 * g + c + 1], None, ALU.mult))
                                    own.settle()
                                    ve.sem_inc(state_ready, 1)
                            for d in range(2):
                                ve.tensor_copy(yall[:, d, ORDER[d][i], :], ps[4 * d][:, 256:512]).then_inc(unit_read, 1)

                    def mix_out():
                        def low(n):
                            k = OUT_ORDER[n]
                            ve.wait_ge(mix_rounded, n + 1)
                            ve.tensor_tensor(mixT_lo[:, k, :], mixT[:, k, :], mixT_hi[:, k, :].bitcast(F32),
                                             ALU.subtract).then_inc(mix_split, 1)

                        def weight(m):
                            rest_unit("out", m, out_w_hi[m % HI_OUT])

                        heads = [P, 2 * GROUPS * HEADS, 64]
                        y = yall[:, :, :, :].rearrange("p d g (h n) -> p (d g h) n", h=HEADS)
                        t = gtmp[:, :, :, :].rearrange("p d g (h n) -> p (d g h) n", h=HEADS)
                        own.link(ve.tensor_reduce(gn_mean, y, AX, ALU.add))
                        own.link(ve.tensor_scalar(gn_mean, gn_mean, 1.0 / 64, None, ALU.mult))
                        own.link(ve.tensor_tensor(y, y, gn_mean.unsqueeze(2).to_broadcast(heads), ALU.subtract))
                        own.link(ve.tensor_tensor(t, y, y, ALU.mult))
                        own.link(ve.tensor_reduce(gn_var, t, AX, ALU.add))
                        ve.tensor_scalar(gn_var, gn_var, 1.0 / 64, RW_GN_EPS, ALU.mult, ALU.add).then_inc(rw_var, 1)
                        weight(0)
                        low(0)
                        low(1)
                        weight(1)
                        for n in range(2, 6):
                            low(n)
                        for d in range(2):
                            own.step(ve.tensor_tensor(
                                gtmp2[:, d, :, :].rearrange("p g (h n) -> p (g h) n", h=HEADS),
                                vt[:, :, :].rearrange("p g (h n) -> p (g h) n", h=HEADS),
                                bonus[:, 12 * d:12 * d + 12].unsqueeze(2).to_broadcast([P, 12, 64]), ALU.mult))
                        ve.wait_ge(rw_std, 1)
                        own.link(ve.reciprocal(gn_var, gn_var))
                        own.link(ve.tensor_tensor(y, y, gn_var.unsqueeze(2).to_broadcast(heads), ALU.mult))
                        weight(2)
                        for d in range(2):
                            wide = [P, GROUPS, 256]
                            gain = row("gn_g")[:, 256 * d:256 * d + 256].unsqueeze(1).to_broadcast(wide)
                            shift = row("gn_b")[:, 256 * d:256 * d + 256].unsqueeze(1).to_broadcast(wide)
                            own.link(ve.tensor_tensor(yall[:, d, :, :], yall[:, d, :, :], gain, ALU.mult))
                            own.link(ve.tensor_tensor(yall[:, d, :, :], yall[:, d, :, :], shift, ALU.add))
                        weight(3)
                        own.link(ve.tensor_tensor(yall[:, :, :, :], yall[:, :, :, :], gtmp2[:, :, :, :], ALU.add))
                        ve.wait_ge(gates_out, 1)
                        own.link(ve.tensor_tensor(yall[:, :, :, :], yall[:, :, :, :], ggate[:, :, :, :], ALU.mult))
                        weight(4)
                        ve.tensor_tensor(mixed[:, :, 0:256], yall[:, 0, :, :], yall[:, 1, :, :],
                                         ALU.add).then_inc(heads_out, 1)
                        weight(5)
                        for n in range(6, KT):
                            low(n)
                            weight(n)

                    meet = Meeting(ve)
                    turn_x(0)
                    feed_forward(0)
                    norm(0)
                    ve.wait_ge(par_loaded, 16 * LAYER_DMAS * l + 16 * LAYER_DMAS)
                    modulation_sums(ve, 1, b_mod[:, 0, :])
                    turn_x(1)
                    project()
                    meet()
                    attention()
                    meet()
                    gla()
                    rwkv()
                    meet()
                    rwkv_units()
                    meet()
                    mix_out()
                    norm(1)
                    modulation_sums(ve, 2, b_mod[:, 1, :])
                    turn_x(2)
                    feed_forward(2)
                    norm(2)
                    if not last:
                        modulation_sums(ve, NMIX, b_mod[:, 2, :])
                        gate_sums(ve, NMIX, l)

                @block.gpsimd
                def _(po):
                    def norm(j):
                        for g in range(2):
                            po.wait_ge(scaled, GROUPS * j + g + 1)
                            po.tensor_tensor(x[:, g, :], x[:, g, :], lnrow[:, 1, :], ALU.add).then_inc(x_ready, 1)
                        if j < NMIX - 1:
                            po.dma_start(gate_row[:, :], bgate_in[l, :, j + 1, :]).then_inc(gate_bias_loaded, 16)
                        elif not last:
                            po.dma_start(gate_row[:, :], bgate_in[l + 1, :, 0, :]).then_inc(gate_bias_loaded, 16)
                        if j == 1:
                            po.wait_ge(x_ready, 2 * (j + 1))
                            po.wait_ge(x_last_ready, j + 1)
                            po.dma_start(lnrow[:, :, :], ln_in[l, j + 1].partition_broadcast(P)).then_inc(lnrow_loaded, 16)

                    def rwkv():
                        po.memset(st[:, :, 0, :], 0.0)
                        for d in range(2):
                            po.wait_ge(rates_ready, d + 1)
                            po.wait_ge(kk_ready, 1)
                            po.tensor_tensor(be[:, d, :, WIN], sa[:, :, WIN], kk[:, :, WIN], ALU.mult).then_inc(rate_kk, 1)
                            po.wait_ge(keys_ready, d + 1)
                            if d == 1:
                                po.wait_ge(bonus_mm, 1)
                            po.tensor_tensor(rkd[:, :, WIN], psh[:, 2:4, WIN], kn[:, :, WIN], ALU.mult).then_inc(bonus_in, 1)

                    def rwkv_units():
                        for i in range(GROUPS):
                            for v in range(1, RW_LEVELS):
                                for d in range(2):
                                    if v == 1:
                                        po.wait_ge(inv_ready, 2 * RW_LEVELS * i + d + 1)
                                    else:
                                        po.wait_ge(lx_mm, 2 * ((RW_LEVELS - 1) * i + v - 2) + d + 1)
                                    po.tensor_tensor(off[:, d, :, :], am[:, d, :, :],
                                                     halves[:, d, v, :].unsqueeze(1).to_broadcast([P, HEADS, P]),
                                                     ALU.mult).then_inc(off_ready, 1)

                    po.dma_start(par[:, :], par_in[l]).then_inc(par_loaded, 16)
                    po.dma_start(wad[:, :, :], w_ad[l]).then_inc(par_loaded, 16)
                    po.dma_start(rows[:, :], row_in[l].partition_broadcast(P)).then_inc(par_loaded, 16)
                    po.dma_start(kc, kc_in[l]).then_inc(par_loaded, 16)
                    po.dma_start(vc, vc_in[l]).then_inc(par_loaded, 16)
                    po.dma_start(lnrow[:, :, :], ln_in[l, 0].partition_broadcast(P)).then_inc(lnrow_loaded, 16)
                    meet = Meeting(po)
                    norm(0)
                    meet()
                    meet()
                    po.memset(g_att[:, :, :, :], 0.0).then_inc(gla_cleared, 1)
                    po.dma_start(g_st[:, :, 1, :], gla_state_in[l]).then_inc(gla_loaded, 16)
                    po.wait_ge(gla_out_read, 2 * GROUPS)
                    po.dma_start(st[:, :, 1, :], rw_state_in[l]).then_inc(rw_loaded, 16)
                    rwkv()
                    meet()
                    rwkv_units()
                    meet()
                    po.dma_start(lnrow[:, :, :], ln_in[l, 1].partition_broadcast(P)).then_inc(lnrow_loaded, 16)
                    norm(1)
                    norm(2)

            if not last:
                clear(every)

        with nc.Fori(0, DEPTH - 1) as l:
            layer(l, False)
        layer(DEPTH - 1, True)


def kernel(**inputs):
    import concourse.bacc as _bacc
    from concourse.bass_utils import run_bass_kernel_spmd as _run

    a = {k: np.asarray(v) for k, v in inputs.items()}
    L = DEPTH

    def cols(w):
        n = w.shape[2] // 256
        return w.reshape(L, KT, P, n, 256).transpose(0, 3, 2, 1, 4).reshape(L, n, P, CHW)

    def ffn(f):
        g, u = (a[w][:, f].reshape(L, KT, P, FT, P).transpose(0, 3, 2, 1, 4).reshape(L, FT, P, UNIT)
                for w in ("ffn_w_gate", "ffn_w_up"))
        d = a["ffn_w_down"][:, f].reshape(L, FT, P, UNIT)
        order = [g[:, 0], u[:, 0]]
        for t in range(1, FT):
            order += [g[:, t], u[:, t], d[:, t - 1]]
        order.append(d[:, FT - 1])
        return np.stack([np.concatenate(order[i:i + 2], 2) for i in range(0, FFN_UNITS, 2)], 1)

    def tiles_(w):
        n = w.shape[2] // 256
        return w.reshape(L, KT, P, n, 2, P).transpose(0, 3, 2, 4, 1, 5).reshape(L, n, P, CHW)

    def rows_(w):
        n = w.shape[1] // 256
        return w.reshape(L, n, 2, P, DM).transpose(0, 1, 3, 2, 4).reshape(L, n, P, CHW)

    ada = cols(a["w_ada"]).reshape(L, NMIX, N_ADA, P, CHW)
    w_in = a["w_in"]
    gl, df = RW_IN, RW_IN + GLA_IN
    feat = tiles_(np.concatenate([w_in[:, :, 0:RW_IN + 2 * GLA_QK], w_in[:, :, df:df + 2 * DIFF_W]], 2))
    g0 = gl + 2 * GLA_QK + GLA_W
    half = GLA_LORA + GLA_W
    tokm = cols(np.concatenate([w_in[:, :, gl + 2 * GLA_QK:g0], w_in[:, :, g0 + GLA_LORA:g0 + half],
                                w_in[:, :, g0 + half + GLA_LORA:g0 + 2 * half], w_in[:, :, df + 2 * DIFF_W:]], 2))
    w_out = rows_(a["w_out"].reshape(L, KT, P, DM)[:, list(OUT_ORDER)].reshape(L, DM, DM))
    weights = np.concatenate([ffn(0), ada[:, 1], feat, tokm, w_out, ada[:, 2], ffn(1),
                              np.roll(ada[:, 0], -1, axis=0)], 1)
    assert weights.shape[1] == N_CHUNKS
    weights = np.ascontiguousarray(weights)
    ad = np.zeros((L, DM, 64), np.float32)
    for d in range(2):
        ad[:, :, 32 * d:32 * d + GLA_LORA] = w_in[:, :, g0 + d * half:g0 + d * half + GLA_LORA]
    ad = ad.reshape(L, KT, P, 64).transpose(0, 2, 1, 3)

    par = np.zeros((L, P, N_PAR), np.float32)

    def tiles(v, n):
        return np.moveaxis(v.reshape(L, -1, P), 2, 1)

    up = par[:, :, PAR["rw_up"]].reshape(L, P, 2, 256)
    up[:, 0:64] = a["rw_w_up"].transpose(0, 2, 1, 3)
    up[:, 64:128] = a["rw_a_up"].transpose(0, 2, 1, 3)
    par[:, :, PAR["rw_up"]] = up.reshape(L, P, 512)
    par[:, :, PAR["g_up"]] = a["rw_g_up"].transpose(0, 2, 1, 3).reshape(L, P, 512)
    for d in range(2):
        par[:, 32 * d:32 * d + GLA_LORA, PAR["gla_up"]] = a["gla_a_up"][:, d]
    b_ada = a["b_ada"].reshape(L, NMIX, 3, DM)
    later = np.concatenate([b_ada[:, 1:, 0:2], np.roll(b_ada[:, 0:1, 0:2], -1, axis=0)], 1)
    par[:, :, PAR["b_mod"]] = tiles(later, 8)
    par[:, :, PAR["mu"]] = tiles(a["rw_mu"], 10)
    par[:, :, PAR["k_k"]] = tiles(a["rw_k_k"], 2)
    par[:, :, PAR["k_a"]] = tiles(a["rw_k_a"], 2)
    par[:, :, PAR["w0"]] = tiles(a["rw_w0"], 2)
    par[:, :, PAR["a0"]] = tiles(a["rw_a0"], 2)
    par[:, :, PAR["gla_b"]] = tiles(a["gla_a_b"], 1)
    rk = np.zeros((L, P, 2, 2, HEADS), np.float32)
    for h in range(HEADS):
        lo = 64 * (h % 2)
        rk[:, lo:lo + 64, :, h // 2, h] = a["rw_r_k"][:, :, h, :].transpose(0, 2, 1)
    par[:, :, PAR["r_k"]] = rk.reshape(L, P, 16)
    for l in range(L):
        par[l, :, PAR["lam_init"]] = (0.8 - 0.6 * math.exp(-0.3 * l), 1.0 - (0.8 - 0.6 * math.exp(-0.3 * l)))
    ln = np.concatenate([a["ln_g"], a["ln_b"]], 2)
    row = np.concatenate([a["rw_gn_g"].reshape(L, -1), a["rw_gn_b"].reshape(L, -1), a["gla_gn_g"], a["diff_gn_g"],
                          a["diff_lam"].reshape(L, -1)], 1)
    bg = np.stack([b_ada[:, :, 2]] * 2, 1)
    rw0 = np.zeros((L, P, 2, 2, P), np.float32)
    gl0 = np.zeros((L, P, 2, HEADS, 64), np.float32)
    for h in range(HEADS):
        lo = 64 * (h % 2)
        rw0[:, lo:lo + 64, :, h // 2, lo:lo + 64] = a["state_rwkv"][0, :, :, h].transpose(0, 3, 1, 2)
        gl0[:, GLA_DK * h:GLA_DK * h + GLA_DK, :, h, :] = a["state_gla"][0, :, :, h].transpose(0, 2, 1, 3)
    kc = a["cache_diff_k"][0].transpose(0, 3, 2, 1)
    vc = a["cache_diff_v"][0].reshape(L, PAST, DIFF_W)
    xx = np.concatenate([a["x_prompt"][0], a["x_sample"][0]], 0).reshape(GROUPS, P, DM).transpose(1, 0, 2)
    cc = np.stack([a["c_ctx"], a["c"][0]], 1).reshape(KT, P, 2).transpose(1, 0, 2)

    ins = {"x_in": xx, "c_in": cc, "consts": shape_constants(), "weights": weights, "w_ad": ad, "par_in": par,
           "ln_in": ln, "row_in": row, "bgate_in": bg, "rw_state": rw0.reshape(L, P, 2, 256),
           "gla_state": gl0.reshape(L, P, 2, 256), "kc_in": kc, "vc_in": vc,
           "first_ada": ada[0, 0], "b_first": tiles(b_ada[:, 0, 0:2], 8)[0]}
    outs = {"y_out": (P, GROUPS, DM), "rw_out": (L, P, 2, 256), "gla_out": (L, P, 2, 256),
            "k_out": (L, P, HEADS, P), "v_out": (L, P, DIFF_W)}
    nc = _bacc.Bacc("TRN2", target_bir_lowering=False, num_devices=1)
    arrays = {k: np.ascontiguousarray(v) for k, v in ins.items()}
    args = [nc.dram_tensor(k, v.shape, F32, kind="ExternalInput").ap() for k, v in arrays.items()]
    args += [nc.dram_tensor(k, v, F32, kind="ExternalOutput").ap() for k, v in outs.items()]
    trunk_kernel(nc, *args)
    r = _run(nc, [arrays], core_ids=[0])
    got = {k: r.results[0][k] for k in outs}

    y = got["y_out"].transpose(1, 0, 2)
    new_rw = np.stack([got["rw_out"].reshape(L, P, 2, 2, P)[:, 64 * (h % 2):64 * (h % 2) + 64, :, h // 2,
                                                             64 * (h % 2):64 * (h % 2) + 64].transpose(0, 2, 3, 1)
                       for h in range(HEADS)], 2)
    new_gla = np.stack([got["gla_out"].reshape(L, P, 2, HEADS, 64)[:, GLA_DK * h:GLA_DK * h + GLA_DK, :, h]
                        .transpose(0, 2, 1, 3) for h in range(HEADS)], 2)
    new_k = got["k_out"].transpose(0, 3, 2, 1)
    new_v = got["v_out"].reshape(L, P, HEADS, P)
    return (y[0][None], y[1:].reshape(1, LAT, DM), new_rw[None], new_gla[None], new_k[None], new_v[None])
```
